# Optimizing a Trainium2 kernel written in Bass

```python
import jax, jax.numpy as jnp
from jax import lax
import numpy as np
import math

D_MODEL = 1024
BATCH = 1
SEQ = 512
DEPTH = 1

CTX_LEN = 256
GRID_W = 64
N_MIXERS = 2
EPS = 1e-6
N_MOD = 6
HG_EXPAND = 128
HG_HEADS = D_MODEL // HG_EXPAND
HG_DV = D_MODEL // HG_HEADS
HG_CHUNK = 64
N_HG_PROJ = 5
POOL_WINDOWS = (2, 4, 8, 16)
POOL_GROUPS = len(POOL_WINDOWS)
POOL_GDIM = D_MODEL // POOL_GROUPS
N_EXPERTS = 16
N_EXPERT_GROUPS = 4
EXPERTS_PER_GROUP = N_EXPERTS // N_EXPERT_GROUPS
TOP_K = 2
D_EXPERT = 256


def rms_norm(x, g):
    xf = x.astype(jnp.float32)
    y = xf * lax.rsqrt(jnp.mean(xf * xf, axis=-1, keepdims=True) + EPS)
    return (y * g.astype(jnp.float32)).astype(x.dtype)

def modulate(x, g, shift, scale):
    return rms_norm(x, g) * (1.0 + scale) + shift

def _heads(t):
    b, l, _ = t.shape
    return t.reshape(b, l, HG_HEADS, -1).transpose(0, 2, 1, 3).astype(jnp.float32)

def _rev(t):
    return jnp.flip(t, axis=2)

def _lower_bound(logits, slot):
    p = jax.nn.softmax(logits.astype(jnp.float32), axis=0)
    return jnp.cumsum(p, axis=0)[slot].reshape(HG_HEADS, 1, HG_EXPAND)

def _gate(z, lb):
    log_f = jnp.logaddexp(jnp.log(lb), jnp.log1p(-lb) + jax.nn.log_sigmoid(z))
    k = (1.0 - lb) * jax.nn.sigmoid(-z)
    return log_f, k

def _gla_scan(q, k, v, log_f, s0):
    b, h, l, _ = q.shape
    dv = v.shape[-1]
    n = l // HG_CHUNK
    rs = lambda t: t.reshape(b, h, n, HG_CHUNK, t.shape[-1])
    q, k, v, log_f = rs(q), rs(k), rs(v), rs(log_f)
    cum = jnp.cumsum(log_f, axis=3)
    ref = cum[:, :, :, HG_CHUNK // 2 - 1:HG_CHUNK // 2, :]
    scores = jnp.einsum('bhnck,bhnsk->bhncs', q * jnp.exp(cum - ref), k * jnp.exp(ref - cum))
    tri = jnp.tril(jnp.ones((HG_CHUNK, HG_CHUNK), dtype=bool))
    scores = jnp.where(tri, scores, 0.0)
    intra = jnp.einsum('bhncs,bhnsv->bhncv', scores, v)
    last = cum[:, :, :, -1:, :]
    chunk_kv = jnp.einsum('bhnck,bhncv->nbhkv', k * jnp.exp(last - cum), v)
    chunk_decay = jnp.moveaxis(jnp.exp(last[:, :, :, 0, :]), 2, 0)

    def step(s, inp):
        dec, kv = inp
        return dec[..., None] * s + kv, s

    s_final, s_prev = lax.scan(step, s0, (chunk_decay, chunk_kv))
    inter = jnp.einsum('bhnck,nbhkv->bhncv', q * jnp.exp(cum), s_prev)
    return (intra + inter).reshape(b, h, l, dv), s_final

def _hgrn_inputs(h, w_in):
    q, v, zf, zb, g = jnp.split(h @ w_in, N_HG_PROJ, axis=-1)
    return jax.nn.silu(_heads(q)), _heads(v), _heads(zf), _heads(zb), g

def _hgrn_readout(o, g, gnorm, w_out):
    b, h, l, dv = o.shape
    o = o * lax.rsqrt(jnp.mean(o * o, axis=-1, keepdims=True) + EPS) * gnorm.astype(jnp.float32)
    o = o.transpose(0, 2, 1, 3).reshape(b, l, h * dv)
    y = (o * jax.nn.silu(g.astype(jnp.float32))).astype(g.dtype)
    return y @ w_out

def hgrn2_mixer(h_lat, h_ctx, w_in, lb_fwd, lb_bwd, gnorm, w_out, slot, need_ctx):
    lbf = _lower_bound(lb_fwd, slot)
    lbb = _lower_bound(lb_bwd, slot)
    qc, vc, zfc, zbc, gc = _hgrn_inputs(h_ctx, w_in)
    ql, vl, zfl, zbl, gl = _hgrn_inputs(h_lat, w_in)
    s0 = jnp.zeros((h_lat.shape[0], HG_HEADS, HG_EXPAND, HG_DV), jnp.float32)
    lf, kf = _gate(zfc, lbf)
    o_cf, s_f = _gla_scan(qc, kf, vc, lf, s0)
    lf, kf = _gate(zfl, lbf)
    o_lf, _ = _gla_scan(ql, kf, vl, lf, s_f)
    lbk, kb = _gate(zbc, lbb)
    o_cb, s_b = _gla_scan(_rev(qc), _rev(kb), _rev(vc), _rev(lbk), s0)
    lbk, kb = _gate(zbl, lbb)
    o_lb, _ = _gla_scan(_rev(ql), _rev(kb), _rev(vl), _rev(lbk), s_b)
    y_lat = _hgrn_readout(o_lf + _rev(o_lb), gl, gnorm, w_out)
    y_ctx = _hgrn_readout(o_cf + _rev(o_cb), gc, gnorm, w_out) if need_ctx else None
    return y_lat, y_ctx

def _box_sum(u, win, axis):
    n = u.shape[axis]
    cs = jnp.cumsum(u, axis=axis)
    pad = [(0, 0)] * u.ndim
    pad[axis] = (1, 0)
    cs = jnp.pad(cs, pad)
    t = jnp.arange(n)
    lo = jnp.clip(t - win // 2, 0, n)
    hi = jnp.clip(t - win // 2 + win, 0, n)
    return jnp.take(cs, hi, axis=axis) - jnp.take(cs, lo, axis=axis), hi - lo

def _grid_mean(u, win):
    b, l, d = u.shape
    rows = l // GRID_W
    g = u.reshape(b, rows, GRID_W, d)
    s, cnt_c = _box_sum(g, win, 2)
    s, cnt_r = _box_sum(s, win, 1)
    cnt = (cnt_r[:, None] * cnt_c[None, :]).astype(u.dtype)
    return (s / cnt[None, :, :, None]).reshape(b, l, d)

def _seq_mean(u, win):
    s, cnt = _box_sum(u, win, 1)
    return s / cnt.astype(u.dtype)[None, :, None]

def _pool_mix(h, mean_fn, w_in, w_grp, p_scale, w_out):
    u = (h @ w_in).astype(jnp.float32)
    parts = []
    for gi, win in enumerate(POOL_WINDOWS):
        ug = u[..., gi * POOL_GDIM:(gi + 1) * POOL_GDIM]
        parts.append((mean_fn(ug, win) - ug) @ w_grp[gi].astype(jnp.float32))
    y = jnp.concatenate(parts, axis=-1) * p_scale.astype(jnp.float32)
    return y.astype(h.dtype) @ w_out

def pool_mixer(h_lat, h_ctx, w_in, w_grp, p_scale, w_out, need_ctx):
    y_lat = _pool_mix(h_lat, _grid_mean, w_in, w_grp, p_scale, w_out)
    y_ctx = _pool_mix(h_ctx, _seq_mean, w_in, w_grp, p_scale, w_out) if need_ctx else None
    return y_lat, y_ctx

def moe_ffn(h, router_w, router_b, w_gate, w_up, w_down):
    n = h.shape[0]
    s = jax.nn.sigmoid((h @ router_w).astype(jnp.float32))
    sel = (s + router_b.astype(jnp.float32)).reshape(n, N_EXPERT_GROUPS, EXPERTS_PER_GROUP)
    top_v, top_i = lax.top_k(sel, TOP_K)
    best = jnp.argmax(jnp.sum(top_v, axis=-1), axis=-1)
    loc = jnp.take_along_axis(top_i, best[:, None, None], axis=1)[:, 0]
    ids = best[:, None] * EXPERTS_PER_GROUP + loc
    w = jnp.take_along_axis(s, ids, axis=1)
    w = w / jnp.sum(w, axis=-1, keepdims=True)
    combine = jnp.sum(jax.nn.one_hot(ids, N_EXPERTS, dtype=jnp.float32) * w[..., None], axis=1)
    y = jnp.zeros(h.shape, jnp.float32)
    for e in range(N_EXPERTS):
        a = jax.nn.silu(h @ w_gate[e]) * (h @ w_up[e])
        y = y + combine[:, e:e + 1] * (a @ w_down[e]).astype(jnp.float32)
    return y.astype(h.dtype)

def first_inputs(seed: int = 0) -> dict:
    key = jax.random.key(seed)
    ks = jax.random.split(key, 24)
    n_a = (DEPTH + N_MIXERS - 1) // N_MIXERS
    n_b = DEPTH // N_MIXERS
    nrm = lambda k, shape, sc: jax.random.normal(k, shape, jnp.float32) * sc
    d = D_MODEL
    return {
        "x": nrm(ks[0], (BATCH, SEQ, d), 1.0),
        "c": nrm(ks[1], (BATCH, d), 1.0),
        "ctx": nrm(ks[2], (BATCH, CTX_LEN, d), 1.0),
        "c_ctx": nrm(ks[3], (d,), 1.0),
        "w_mod": nrm(ks[4], (DEPTH, d, N_MOD * d), 0.5 * d ** -0.5),
        "b_mod": nrm(ks[5], (DEPTH, N_MOD * d), 0.01),
        "norm1_g": 1.0 + nrm(ks[6], (DEPTH, d), 0.05),
        "norm2_g": 1.0 + nrm(ks[7], (DEPTH, d), 0.05),
        "hg_w_in": nrm(ks[8], (n_a, d, N_HG_PROJ * d), d ** -0.5),
        "hg_lb_fwd": nrm(ks[9], (n_a + 1, d), 0.5),
        "hg_lb_bwd": nrm(ks[10], (n_a + 1, d), 0.5),
        "hg_gnorm": 1.0 + nrm(ks[11], (n_a, HG_DV), 0.05),
        "hg_w_out": nrm(ks[12], (n_a, d, d), d ** -0.5),
        "pool_w_in": nrm(ks[13], (n_b, d, d), d ** -0.5),
        "pool_w_grp": nrm(ks[14], (n_b, POOL_GROUPS, POOL_GDIM, POOL_GDIM), POOL_GDIM ** -0.5),
        "pool_scale": 1.0 + nrm(ks[15], (n_b, d), 0.1),
        "pool_w_out": nrm(ks[16], (n_b, d, d), d ** -0.5),
        "router_w": nrm(ks[17], (d, N_EXPERTS), d ** -0.5),
        "router_b": nrm(ks[18], (N_EXPERTS,), 0.01),
        "moe_w_gate": nrm(ks[19], (DEPTH, N_EXPERTS, d, D_EXPERT), d ** -0.5),
        "moe_w_up": nrm(ks[20], (DEPTH, N_EXPERTS, d, D_EXPERT), d ** -0.5),
        "moe_w_down": nrm(ks[21], (DEPTH, N_EXPERTS, D_EXPERT, d), D_EXPERT ** -0.5),
        "final_g": 1.0 + nrm(ks[22], (d,), 0.05),
    }

def first_block(x, c, ctx, c_ctx, w_mod, b_mod, norm1_g, norm2_g, hg_w_in, hg_lb_fwd, hg_lb_bwd, hg_gnorm,
              hg_w_out, pool_w_in, pool_w_grp, pool_scale, pool_w_out, router_w, router_b, moe_w_gate,
              moe_w_up, moe_w_down, final_g):
    x_lat, x_ctx = x, ctx
    d = x.shape[-1]
    for i in range(DEPTH):
        need_ctx = i < DEPTH - 1
        slot = i // N_MIXERS
        mod = jax.nn.silu(c) @ w_mod[i] + b_mod[i]
        sh1, sc1, g1, sh2, sc2, g2 = jnp.split(mod[:, None, :], N_MOD, axis=-1)
        mod_c = jax.nn.silu(c_ctx) @ w_mod[i] + b_mod[i]
        csh1, csc1, cg1, csh2, csc2, cg2 = jnp.split(mod_c, N_MOD, axis=-1)
        h_lat = modulate(x_lat, norm1_g[i], sh1, sc1)
        h_ctx = modulate(x_ctx, norm1_g[i], csh1, csc1)
        if i % N_MIXERS == 0:
            y_lat, y_ctx = hgrn2_mixer(h_lat, h_ctx, hg_w_in[slot], hg_lb_fwd, hg_lb_bwd, hg_gnorm[slot],
                                       hg_w_out[slot], slot, need_ctx)
        else:
            y_lat, y_ctx = pool_mixer(h_lat, h_ctx, pool_w_in[slot], pool_w_grp[slot], pool_scale[slot],
                                      pool_w_out[slot], need_ctx)
        x_lat = x_lat + g1 * y_lat
        h2_lat = modulate(x_lat, norm2_g[i], sh2, sc2).reshape(-1, d)
        n_lat = h2_lat.shape[0]
        if need_ctx:
            x_ctx = x_ctx + cg1 * y_ctx
            h2_ctx = modulate(x_ctx, norm2_g[i], csh2, csc2).reshape(-1, d)
            ff = moe_ffn(jnp.concatenate([h2_lat, h2_ctx], axis=0), router_w, router_b,
                         moe_w_gate[i], moe_w_up[i], moe_w_down[i])
            x_ctx = x_ctx + cg2 * ff[n_lat:].reshape(x_ctx.shape)
            ff_lat = ff[:n_lat]
        else:
            ff_lat = moe_ffn(h2_lat, router_w, router_b, moe_w_gate[i], moe_w_up[i], moe_w_down[i])
        x_lat = x_lat + g2 * ff_lat.reshape(x_lat.shape)
    return rms_norm(x_lat, final_g)


DEPTH_2 = 2

CHUNK = 64
Q_BLOCK = 128
D_FF = 2816
NORM_EPS = 1e-6

A_HEADS = 4
A_QK_DIM = 64
A_V_DIM = 2 * A_QK_DIM
A_WIDTH = A_HEADS * A_V_DIM
A_COLS = 3 * A_WIDTH

B_HEAD_DIM = 64
B_WIDTH = D_MODEL - A_WIDTH
B_HEADS = B_WIDTH // B_HEAD_DIM
B_DECAY_RANK = 64
B_A_RANK = 64
B_GATE_RANK = 128
B_VRES_RANK = 32
B_LN_EPS = 64e-5
B_COLS = 3 * B_WIDTH + B_DECAY_RANK + B_A_RANK + B_GATE_RANK
B_SPLITS = [B_WIDTH, 2 * B_WIDTH, 3 * B_WIDTH, 3 * B_WIDTH + B_DECAY_RANK,
            3 * B_WIDTH + B_DECAY_RANK + B_A_RANK]
EVEN_IN = A_COLS + B_COLS

C_HEADS = 4
C_QK_DIM = D_MODEL // C_HEADS
C_V_DIM = 2 * C_QK_DIM
C_QK_WIDTH = C_HEADS * C_QK_DIM
C_V_WIDTH = C_HEADS * C_V_DIM
ODD_IN = 2 * C_QK_WIDTH + 2 * C_V_WIDTH

N_EVEN = (DEPTH_2 + 1) // 2
N_ODD = DEPTH_2 // 2


def rms_norm_2(x, g, eps=NORM_EPS):
    xf = x.astype(jnp.float32)
    y = xf * lax.rsqrt(jnp.mean(xf * xf, axis=-1, keepdims=True) + eps)
    return (y * g.astype(jnp.float32)).astype(x.dtype)

def swiglu(x, w_gu, w_d):
    gate, up = jnp.split(x @ w_gu, 2, axis=-1)
    return (jax.nn.silu(gate) * up) @ w_d

def token_shift(z, mu):
    z_prev = jnp.pad(z, ((0, 0), (1, 0), (0, 0)))[:, :-1]
    return z + (z_prev - z) * mu

def diff_attention(q, k, v, lam):
    S_ = q.shape[1]
    q = q * (A_QK_DIM ** -0.5)
    slopes = 2.0 ** (-8.0 / A_HEADS * jnp.arange(1, A_HEADS + 1, dtype=jnp.float32))
    pos = jnp.arange(S_)
    chunk_id = pos // CHUNK
    outs = []
    for s0 in range(0, S_, Q_BLOCK):
        kend = s0 + Q_BLOCK
        scores = jnp.einsum('bqhmd,bkhmd->bhmqk', q[:, s0:kend], k[:, :kend]).astype(jnp.float32)
        dist = jnp.abs(pos[s0:kend][:, None] - pos[:kend][None, :]).astype(jnp.float32)
        bias = -slopes[:, None, None, None] * dist
        allowed = chunk_id[:kend][None, :] <= chunk_id[s0:kend][:, None]
        scores = jnp.where(allowed, scores + bias, -jnp.inf)
        p = jax.nn.softmax(scores, axis=-1)
        p = p[:, :, 0] - lam * p[:, :, 1]
        outs.append(jnp.einsum('bhqk,bkhe->bqhe', p.astype(v.dtype), v[:, :kend]))
    return jnp.concatenate(outs, axis=1)

def rwkv7_recurrence(r, w, k, v, kk, a):
    Bn, _, H, N = r.shape

    def step(state, inp):
        r_t, w_t, k_t, v_t, kk_t, a_t = inp
        sa = jnp.einsum('bhvk,bhk->bhv', state, -kk_t)
        state = (state * w_t[:, :, None, :]
                 + sa[..., None] * (kk_t * a_t)[:, :, None, :]
                 + v_t[..., None] * k_t[:, :, None, :])
        return state, jnp.einsum('bhvk,bhk->bhv', state, r_t)

    xs = tuple(jnp.moveaxis(t, 1, 0) for t in (r, w, k, v, kk, a))
    state0 = jnp.zeros((Bn, H, N, N), jnp.float32)
    _, y = lax.scan(step, state0, xs)
    return jnp.moveaxis(y, 0, 1)

def head_group_norm(y, w, b):
    Bn, S_ = y.shape[:2]
    mean = jnp.mean(y, axis=-1, keepdims=True)
    var = jnp.mean(jnp.square(y - mean), axis=-1, keepdims=True)
    yn = (y - mean) * lax.rsqrt(var + B_LN_EPS)
    return yn.reshape(Bn, S_, -1) * w + b

def rwkv7_time_mix(zb, mu, vec, w_up, a_up, g_up, v_first, vres):
    Bn, S_, _ = zb.shape
    f32 = jnp.float32
    zs = token_shift(zb.astype(f32), mu.astype(f32))
    r, k, v, xw, xa, xg = jnp.split(zs, B_SPLITS, axis=-1)
    w0, a0, k_k, k_a, r_k, ln_w, ln_b = vec.astype(f32)
    w = -jax.nn.softplus(-(w0 + jnp.tanh(xw) @ w_up.astype(f32))) - 0.5
    decay = jnp.exp(-jnp.exp(w))
    if vres is not None:
        v0, v_down, v_up = vres
        v = v + (v_first - v) * jax.nn.sigmoid(v0.astype(f32) + (v @ v_down.astype(f32)) @ v_up.astype(f32))
    a = jax.nn.sigmoid(a0 + xa @ a_up.astype(f32))
    g = jax.nn.sigmoid(xg) @ g_up.astype(f32)
    heads = lambda t: t.reshape(Bn, S_, B_HEADS, B_HEAD_DIM)
    kk = heads(k * k_k)
    kk = kk / jnp.maximum(jnp.sqrt(jnp.sum(kk * kk, axis=-1, keepdims=True)), 1e-12)
    k = k * (1.0 + (a - 1.0) * k_a)
    rh, kh, vh = heads(r), heads(k), heads(v)
    y = rwkv7_recurrence(rh, heads(decay), kh, vh, kk, heads(a))
    y = head_group_norm(y, ln_w, ln_b)
    r_k_h = r_k.reshape(B_HEADS, B_HEAD_DIM)
    bonus = jnp.sum(rh * kh * r_k_h, axis=-1, keepdims=True) * vh
    y = y + bonus.reshape(Bn, S_, B_WIDTH)
    return y * g, v

def diff_rwkv_mixer(h, w_in, w_out, lam_vecs, subln, lam_init, mu, vec, w_up, a_up, g_up, v_first, vres):
    Bn, S_, _ = h.shape
    z = h @ w_in
    za, zb = z[..., :A_COLS], z[..., A_COLS:]
    qa, ka, va = jnp.split(za, 3, axis=-1)
    qa = qa.reshape(Bn, S_, A_HEADS, 2, A_QK_DIM)
    ka = ka.reshape(Bn, S_, A_HEADS, 2, A_QK_DIM)
    va = va.reshape(Bn, S_, A_HEADS, A_V_DIM)
    lv = lam_vecs.astype(jnp.float32)
    lam = jnp.exp(jnp.sum(lv[0] * lv[1])) - jnp.exp(jnp.sum(lv[2] * lv[3])) + lam_init
    oa = diff_attention(qa, ka, va, lam)
    oa = rms_norm_2(oa, subln) * (1.0 - lam_init)
    ob, v_b = rwkv7_time_mix(zb, mu, vec, w_up, a_up, g_up, v_first, vres)
    mix = jnp.concatenate([oa.reshape(Bn, S_, A_WIDTH), ob.astype(h.dtype)], axis=-1)
    return mix @ w_out, v_b

def retention(q, k, v):
    Bn, S_, H, _ = q.shape
    dk, dv = q.shape[-1], v.shape[-1]
    n_chunks = S_ // CHUNK
    log_g = jnp.log(1.0 - 2.0 ** (-5.0 - jnp.arange(H, dtype=jnp.float32)))
    idx = jnp.arange(CHUNK, dtype=jnp.float32)
    intra = jnp.exp(log_g[:, None, None] * jnp.abs(idx[:, None] - idx[None, :]))
    q_decay = jnp.exp(log_g[:, None] * (idx + 1.0))
    k_decay = jnp.exp(log_g[:, None] * (CHUNK - 1.0 - idx))
    chunk_decay = jnp.exp(log_g * CHUNK)

    def to_chunks(t):
        return t.reshape(Bn, n_chunks, CHUNK, H, t.shape[-1]).transpose(1, 0, 3, 2, 4)

    def step(state, inp):
        qc, kc, vc = inp
        scores = jnp.einsum('bhid,bhjd->bhij', qc, kc) * intra
        y = (jnp.einsum('bhij,bhjv->bhiv', scores, vc)
             + jnp.einsum('bhid,bhdv->bhiv', qc, state) * q_decay[:, :, None])
        state = (state * chunk_decay[:, None, None]
                 + jnp.einsum('bhjd,bhjv->bhdv', kc * k_decay[:, :, None], vc))
        return state, y

    state0 = jnp.zeros((Bn, H, dk, dv), jnp.float32)
    _, y = lax.scan(step, state0, (to_chunks(q), to_chunks(k), to_chunks(v)))
    return y.transpose(1, 0, 3, 2, 4).reshape(Bn, S_, H, dv)

def retention_mixer(h, w_in, w_out):
    Bn, S_, _ = h.shape
    z = (h @ w_in).astype(jnp.float32)
    q, k, v, g = jnp.split(z, [C_QK_WIDTH, 2 * C_QK_WIDTH, 2 * C_QK_WIDTH + C_V_WIDTH], axis=-1)
    q = q.reshape(Bn, S_, C_HEADS, C_QK_DIM)
    k = k.reshape(Bn, S_, C_HEADS, C_QK_DIM) * (C_QK_DIM ** -0.5)
    v = v.reshape(Bn, S_, C_HEADS, C_V_DIM)
    y = retention(q, k, v)
    y = y * lax.rsqrt(jnp.mean(y * y, axis=-1, keepdims=True) + NORM_EPS)
    y = jax.nn.silu(g) * y.reshape(Bn, S_, C_V_WIDTH)
    return y.astype(h.dtype) @ w_out

def second_inputs(seed: int = 0) -> dict:
    key = jax.random.key(seed)
    ks = jax.random.split(key, 24)
    nrm = lambda k, shape, s: s * jax.random.normal(k, shape, jnp.float32)
    x = nrm(ks[0], (BATCH, SEQ, D_MODEL), 1.0)
    norms = 1.0 + nrm(ks[1], (DEPTH_2, 6, D_MODEL), 0.05)
    ffn_wgu = nrm(ks[2], (DEPTH_2, 2, D_MODEL, 2 * D_FF), D_MODEL ** -0.5)
    ffn_wd = nrm(ks[3], (DEPTH_2, 2, D_FF, D_MODEL), D_FF ** -0.5)
    even_w_in = nrm(ks[4], (N_EVEN, D_MODEL, EVEN_IN), D_MODEL ** -0.5)
    even_w_out = nrm(ks[5], (N_EVEN, D_MODEL, D_MODEL), D_MODEL ** -0.5)
    diff_lam = nrm(ks[6], (N_EVEN, 4, A_QK_DIM), 0.1)
    diff_subln = 1.0 + nrm(ks[7], (N_EVEN, A_V_DIM), 0.05)
    rwkv_mu = jax.random.uniform(ks[8], (N_EVEN, B_COLS), jnp.float32)
    vshape = (N_EVEN, B_WIDTH)
    w0 = jnp.linspace(-6.0, -1.0, B_WIDTH, dtype=jnp.float32)[None, :] + nrm(ks[9], vshape, 0.1)
    a0 = nrm(ks[10], vshape, 0.1)
    k_k = 0.85 + nrm(ks[11], vshape, 0.05)
    k_a = 1.0 + nrm(ks[12], vshape, 0.05)
    r_k = nrm(ks[13], vshape, 0.1)
    ln_w = 1.0 + nrm(ks[14], vshape, 0.05)
    ln_b = nrm(ks[15], vshape, 0.02)
    rwkv_vec = jnp.stack([w0, a0, k_k, k_a, r_k, ln_w, ln_b], axis=1)
    rwkv_w_up = nrm(ks[16], (N_EVEN, B_DECAY_RANK, B_WIDTH), 0.1 * B_DECAY_RANK ** -0.5)
    rwkv_a_up = nrm(ks[17], (N_EVEN, B_A_RANK, B_WIDTH), 0.5 * B_A_RANK ** -0.5)
    rwkv_g_up = nrm(ks[18], (N_EVEN, B_GATE_RANK, B_WIDTH), B_GATE_RANK ** -0.5)
    rwkv_v0 = nrm(ks[19], (N_EVEN - 1, B_WIDTH), 0.1)
    rwkv_v_down = nrm(ks[20], (N_EVEN - 1, B_WIDTH, B_VRES_RANK), B_WIDTH ** -0.5)
    rwkv_v_up = nrm(ks[21], (N_EVEN - 1, B_VRES_RANK, B_WIDTH), 0.5 * B_VRES_RANK ** -0.5)
    odd_w_in = nrm(ks[22], (N_ODD, D_MODEL, ODD_IN), D_MODEL ** -0.5)
    odd_w_out = nrm(ks[23], (N_ODD, C_V_WIDTH, D_MODEL), C_V_WIDTH ** -0.5)
    return {'x': x, 'norms': norms, 'ffn_wgu': ffn_wgu, 'ffn_wd': ffn_wd,
            'even_w_in': even_w_in, 'even_w_out': even_w_out,
            'diff_lam': diff_lam, 'diff_subln': diff_subln,
            'rwkv_mu': rwkv_mu, 'rwkv_vec': rwkv_vec,
            'rwkv_w_up': rwkv_w_up, 'rwkv_a_up': rwkv_a_up, 'rwkv_g_up': rwkv_g_up,
            'rwkv_v0': rwkv_v0, 'rwkv_v_down': rwkv_v_down, 'rwkv_v_up': rwkv_v_up,
            'odd_w_in': odd_w_in, 'odd_w_out': odd_w_out}

def second_block(x, norms, ffn_wgu, ffn_wd, even_w_in, even_w_out, diff_lam, diff_subln,
              rwkv_mu, rwkv_vec, rwkv_w_up, rwkv_a_up, rwkv_g_up,
              rwkv_v0, rwkv_v_down, rwkv_v_up, odd_w_in, odd_w_out):
    v_first = None
    for i in range(DEPTH_2):
        g = norms[i]
        x = x + 0.5 * rms_norm_2(swiglu(rms_norm_2(x, g[0]), ffn_wgu[i, 0], ffn_wd[i, 0]), g[1])
        h = rms_norm_2(x, g[2])
        j = i // 2
        if i % 2 == 0:
            lam_init = 0.8 - 0.6 * math.exp(-0.3 * i)
            vres = None if j == 0 else (rwkv_v0[j - 1], rwkv_v_down[j - 1], rwkv_v_up[j - 1])
            mix, v_b = diff_rwkv_mixer(h, even_w_in[j], even_w_out[j], diff_lam[j], diff_subln[j],
                                       lam_init, rwkv_mu[j], rwkv_vec[j], rwkv_w_up[j],
                                       rwkv_a_up[j], rwkv_g_up[j], v_first, vres)
            if j == 0:
                v_first = v_b
        else:
            mix = retention_mixer(h, odd_w_in[j], odd_w_out[j])
        x = x + rms_norm_2(mix, g[3])
        x = x + 0.5 * rms_norm_2(swiglu(rms_norm_2(x, g[4]), ffn_wgu[i, 1], ffn_wd[i, 1]), g[5])
    return x


def setup_inputs(seed=0):
    out = dict(first_inputs(seed))
    for name, value in second_inputs(seed + 1).items():
        if name != "x":
            out[name + "_2"] = value
    return out


def reference(
    x, c, ctx, c_ctx, w_mod, b_mod, norm1_g, norm2_g, hg_w_in, hg_lb_fwd, hg_lb_bwd, hg_gnorm,
    hg_w_out, pool_w_in, pool_w_grp, pool_scale, pool_w_out, router_w, router_b, moe_w_gate,
    moe_w_up, moe_w_down, final_g, norms_2, ffn_wgu_2, ffn_wd_2, even_w_in_2, even_w_out_2,
    diff_lam_2, diff_subln_2, rwkv_mu_2, rwkv_vec_2, rwkv_w_up_2, rwkv_a_up_2, rwkv_g_up_2,
    rwkv_v0_2, rwkv_v_down_2, rwkv_v_up_2, odd_w_in_2, odd_w_out_2,
):
    x = first_block(
        x, c, ctx, c_ctx, w_mod, b_mod, norm1_g, norm2_g, hg_w_in, hg_lb_fwd, hg_lb_bwd,
        hg_gnorm, hg_w_out, pool_w_in, pool_w_grp, pool_scale, pool_w_out, router_w, router_b,
        moe_w_gate, moe_w_up, moe_w_down, final_g,
    )
    return second_block(
        x, norms_2, ffn_wgu_2, ffn_wd_2, even_w_in_2, even_w_out_2, diff_lam_2, diff_subln_2,
        rwkv_mu_2, rwkv_vec_2, rwkv_w_up_2, rwkv_a_up_2, rwkv_g_up_2, rwkv_v0_2, rwkv_v_down_2,
        rwkv_v_up_2, odd_w_in_2, odd_w_out_2,
    )


_drawn_inputs = setup_inputs


def setup_inputs(seed=0):
    import zlib

    import numpy as np

    out = dict(_drawn_inputs(seed))
    spreads = {}
    factors = {'c_ctx': 4.442, 'rwkv_w_up_2': 8.0}
    for name, (base, spread) in spreads.items():
        noise = np.random.default_rng([zlib.crc32(name.encode()), seed]).standard_normal(out[name].shape)
        drawn = base * np.exp(spread * noise) if base else spread * noise
        out[name] = __import__('jax').numpy.asarray(drawn.astype(out[name].dtype))
    for name, factor in factors.items():
        out[name] = (out[name] * factor).astype(out[name].dtype)
    return out
```

```python
from contextlib import ExitStack
import math
import numpy as np
import concourse.bass as bass
from concourse import mybir

F32 = mybir.dt.float32
F32R = mybir.dt.float32r
I8 = mybir.dt.int8
ACT = mybir.ActivationFunctionType
ALU = mybir.AluOpType
AX = mybir.AxisListType

P = 128
D = 1024
DC = D // P
T = 512
TC = 256
EPS = 1e-6
RING = 4
LEAD = 2
D_FF = 2816
FF_SEGMENTS = (8, 8, 6)
assert sum(FF_SEGMENTS) * P == D_FF


class At:

    def __init__(self, base, mult=0, reg=None):
        self.base, self.mult, self.reg = base, mult, reg

    def __add__(self, n):
        return At(self.base + n, self.mult, self.reg)

    def __sub__(self, n):
        return At(self.base - n, self.mult, self.reg)

    def times(self, k):
        return At(self.base * k, self.mult * k, self.reg)

    @property
    def value(self):
        return self.base if self.reg is None or self.mult == 0 else self.reg * self.mult + self.base

    @property
    def slot(self):
        assert self.mult % RING == 0
        return self.base % RING

    @property
    def turn(self):
        assert self.mult % RING == 0
        return At(self.base // RING, self.mult // RING, self.reg)


def wait(eng, sem, at):
    if isinstance(at, At):
        if at.base <= 0:
            assert at.reg is None or at.mult == 0, "peel this iteration"
            return
        eng.wait_ge(sem, at.value)
    elif at > 0:
        eng.wait_ge(sem, at)


class Order:

    def __init__(self, eng, sem):
        self.eng, self.sem, self.n = eng, sem, At(0)

    def __call__(self, ins):
        ins.then_inc(self.sem, 1)
        self.n = self.n + 1
        return self.n

    def wait(self, at=None):
        wait(self.eng, self.sem, self.n if at is None else at)

    def enter(self, reg, per):
        self.outer = self.n
        self.per = per
        self.n = At(self.outer.base, per, reg)

    def leave(self, trips):
        assert self.n.base - self.outer.base == self.per, (self.n.base - self.outer.base, self.per)
        self.n = At(self.outer.base + trips * self.per)


class Phase:
    blocks = 0

    def layout(self, k, ctx):
        pass

    def advance(self, q):
        pass

    def pool(self, k, q):
        pass


BLOCK_NORMS = [f"norm_{i}_{n}" for i in range(2) for n in range(6)]
RWKV_VECS = "w0 a0 k_k k_a r_k ln_w ln_b".split()
VEC_WIDTH = {"b_mod": 6 * DC, "norm1_g": DC, "norm2_g": DC, "gnorm": 1, "lb_f": 2 * DC, "lb_b": 2 * DC, "final_g": DC,
             "router_b": 16, **{n: DC for n in BLOCK_NORMS}, "mu": 14, "subln": 1, **{n: 4 for n in RWKV_VECS}}
VEC_AT, VEC_COLS = {}, 0
for _name, _width in VEC_WIDTH.items():
    VEC_AT[_name], VEC_COLS = VEC_COLS, VEC_COLS + _width
HALVED = ["norm_0_1", "norm_0_5", "norm_1_1", "norm_1_5"]


def sp_stream(k, n_blocks):
    sp = k.nc.sync
    for g in range(RING):
        sp.dma_start(k.raw[:, g, :], k.W[g]).then_inc(k.raw_landed[g], 16)
    rest = n_blocks - RING
    with sp.Fori(0, rest // RING) as it:
        for b in range(RING):
            g = At(RING + b, RING, it)
            wait(sp, k.split_lo, g - (RING - 1))
            sp.dma_start(k.raw[:, g.slot, :], k.W[bass.ds(g.value, 1)].rearrange("o p f -> p (o f)")
                         ).then_inc(k.raw_landed[g.slot], 16)
    for g in range(n_blocks - rest % RING, n_blocks):
        wait(sp, k.split_lo, g - (RING - 1))
        sp.dma_start(k.raw[:, g % RING, :], k.W[g]).then_inc(k.raw_landed[g % RING], 16)


def act_split(k, g):
    if g.reg is None and g.base >= k.n_blocks:
        return
    act = k.nc.scalar
    wait(act, k.raw_landed[g.slot], (g.turn + 1).times(16))
    wait(act, k.block_done, g - (RING - 1))
    act.activation(k.whi[:, g.slot, :], k.raw[:, g.slot, :], ACT.Copy).then_inc(k.split_hi, 1)


def dve_split(k, g):
    if g.reg is None and g.base >= k.n_blocks:
        return
    dve = k.nc.vector
    wait(dve, k.split_hi, g + 1)
    dve.tensor_tensor(k.wlo[:, g.slot, :], k.raw[:, g.slot, :], k.whi[:, g.slot, :].bitcast(F32),
                      ALU.subtract).then_inc(k.split_lo, 1)


def pe_block(k, g, tiles, moving, out=None, more=None, ready=None):
    pe = k.nc.tensor
    wait(pe, k.split_lo, g + 1)
    wait(pe, k.bank_free, g - (RING - 1))
    out = k.bank[g.slot][:, :] if out is None else out
    both = [(moving, out)] + ([more[:2]] if more else [])
    for which, (mv, o) in enumerate(both):
        if which:
            wait(pe, k.cbank_free, more[2])
        for t in range(tiles):
            if ready is not None and which == 0:
                ready(t)
            hi, lo = mv(t)
            w_hi = k.whi[:, g.slot, t * P:(t + 1) * P]
            w_lo = k.wlo[:, g.slot, t * P:(t + 1) * P]
            pe.matmul(o, w_hi, hi, start=(t == 0), stop=False)
            pe.matmul(o, w_hi, lo, start=False, stop=False)
            last = pe.matmul(o, w_lo, hi, start=False, stop=(t == tiles - 1))
    last.then_inc(k.block_done, 1)


def act_square(k, src, at, ready):
    act = k.nc.scalar
    ready(act)
    wait(act, k.ssq_added, at - 1)
    sq = k.sq[:, at.base % 2, :src.shape[-1]] if len(src.shape) == 2 else k.sq[:, at.base % 2:at.base % 2 + 1, :]
    act.activation(sq, src, ACT.Square).then_inc(k.sq_ready, 1)


def dve_add_square(k, at, first, width=T):
    dve = k.nc.vector
    wait(dve, k.sq_ready, at + 1)
    sq = k.sq[:, at.base % 2, :width]
    if first:
        dve.tensor_copy(k.ssq[:, :width], sq).then_inc(k.ssq_added, 1)
    else:
        wait(dve, k.ssq_added, at)
        dve.tensor_tensor(k.ssq[:, :width], k.ssq[:, :width], sq, ALU.add).then_inc(k.ssq_added, 1)


def pe_norm(k, n, squares, width=T):
    pe = k.nc.tensor
    wait(pe, k.ssq_added, squares)
    wait(pe, k.rstd_ready, n)
    pe.matmul(k.nbank[:, :width], k.ones[:, :], k.ssq[:, :width], start=True, stop=True).then_inc(k.norm_sum, 1)


def act_rstd(k, n, used, width=T, scale=1.0 / D):
    act = k.nc.scalar
    wait(act, k.norm_sum, n + 1)
    act.activation(k.lnv[:, :width], k.nbank[:, :width], ACT.Ln, bias=k.eps_col[:, :], scale=scale).then_inc(k.ln_ready, 1)
    wait(act, k.ln_ready, n + 1)
    used(act)
    act.activation(k.rstd[:, :width], k.lnv[:, :width], ACT.Exp, scale=-0.5).then_inc(k.rstd_ready, 1)


def act_h_high(k, i, shift, hi, width=T):
    act = k.nc.scalar
    wait(act, k.h_made, i + 1)
    if shift is None:
        act.activation(hi, k.h32[:, i % 2, :width], ACT.Copy).then_inc(k.h_hi, 1)
    else:
        act.activation(hi, k.h32[:, i % 2, :width], ACT.Identity, bias=shift).then_inc(k.h_hi, 1)


def dve_h_low(k, i, shift, hi, lo, width=T):
    dve = k.nc.vector
    wait(dve, k.h_hi, i + 1)
    h32 = k.h32[:, i % 2, :width]
    if shift is None:
        dve.tensor_tensor(lo, h32, hi.bitcast(F32), ALU.subtract).then_inc(k.h_ready, 1)
    else:
        dve.scalar_tensor_tensor(lo, h32, shift, hi.bitcast(F32), ALU.add, ALU.subtract).then_inc(k.h_ready, 1)


def act_prenorm(k, i0, shift, hi, width=T):
    for c in range(DC):
        act_h_high(k, i0 + c, None if shift is None else shift[:, c:c + 1], hi[:, c, :width], width)


def dve_prenorm(k, n, i0, src, gain, shift, hi, lo, width=T):
    dve = k.nc.vector
    wait(dve, k.rstd_ready, n + 1)
    for c in range(DC + 1):
        if c < DC:
            if i0 + c >= 2:
                wait(dve, k.h_ready, i0 + c - 1)
            dve.scalar_tensor_tensor(k.h32[:, (i0 + c) % 2, :width], src[:, c, :width], gain[:, c:c + 1],
                                     k.rstd[:, :width], ALU.mult, ALU.mult).then_inc(k.h_made, 1)
        if c >= 1:
            dve_h_low(k, i0 + c - 1, None if shift is None else shift[:, c - 1:c],
                      hi[:, c - 1, :width], lo[:, c - 1, :width], width)


def act_residual(k, c0, sq0):
    for c in range(DC):
        act_square(k, k.x[:, c, :], At(sq0 + c), lambda act: wait(act, k.x_ready, c0 + c + 1))


def dve_residual(k, n, c0, y0, sq0, gain):
    dve = k.nc.vector
    wait(dve, k.rstd_ready, n + 1)
    for c in range(DC + 1):
        if c < DC:
            dve.scalar_tensor_tensor(k.acc[:, c, :], k.acc[:, c, :], gain[:, c:c + 1], k.rstd[:, :],
                                     ALU.mult, ALU.mult).then_inc(k.y_scaled, 1)
            wait(dve, k.y_scaled, y0 + c + 1)
            dve.tensor_tensor(k.x[:, c, :], k.x[:, c, :], k.acc[:, c, :], ALU.add).then_inc(k.x_ready, 1)
        if c >= 1 and sq0 is not None:
            dve_add_square(k, At(sq0 + c - 1), first=(c == 1))


def pe_pass(k, g0, nk, a0, h_ready=None, e0=None):
    pe = k.nc.tensor
    h = lambda t: (k.h_hi_buf[:, t, :], k.h_lo_buf[:, t, :])
    if h_ready is not None:
        wait(pe, k.h_ready, h_ready)
    with pe.Fori(0, nk // 2) as it:
        for b in range(RING):
            pe_block(k, At(g0 + b, RING, it), DC, h)
            if e0 is not None and b == 0:
                wait(pe, k.share_used, At(2 * e0 + 1, 2, it))
                wait(pe, k.share_sel_ready, e0 // 4 + 1)
                pe.matmul(k.gbank[0][:, :], k.ones[0:N_EXPERTS, :],
                          k.share_sel[:, bass.ds(At(e0, 1, it).value, 1), :].rearrange("p o f -> p (o f)"),
                          start=True, stop=True).then_inc(k.share_ready, 1)
    a = lambda t: (k.a_hi_buf[:, t, :], k.a_lo_buf[:, t, :])
    g1 = g0 + 2 * nk
    wait(pe, k.a_ready, a0 + nk)
    with pe.Fori(0, DC // RING) as it:
        for b in range(RING):
            pe_block(k, At(g1 + b, RING, it), nk, a)


def act_pass(k, g0, nk, a0):
    act = k.nc.scalar
    with act.Fori(0, nk // 2) as it:
        for p in range(2):
            g, a = At(g0 + 2 * p, RING, it), At(a0 + p, 2, it)
            act_split(k, g + LEAD)
            act_split(k, g + LEAD + 1)
            wait(act, k.block_done, g + 1)
            act.activation(k.sil[:, p, :], k.bank[g.slot][:, :], ACT.Silu).then_inc(k.silu_ready, 1)
            wait(act, k.bank_free, g + 2)
            act.activation(k.a_hi_buf[:, bass.ds(At(p, 2, it).value, 1), :], k.a32[:, p:p + 1, :], ACT.Copy
                           ).then_inc(k.a_hi, 1)


def dve_pass(k, g0, nk, a0, e0=None):
    dve = k.nc.vector
    with dve.Fori(0, nk // 2) as it:
        for p in range(2):
            g, a = At(g0 + 2 * p, RING, it), At(a0 + p, 2, it)
            dve_split(k, g + LEAD)
            dve_split(k, g + LEAD + 1)
            wait(dve, k.block_done, g + 2)
            wait(dve, k.silu_ready, a + 1)
            if e0 is not None:
                wait(dve, k.share_ready, At(e0 + 1, 1, it))
                dve.tensor_tensor(k.sil[:, p, :], k.sil[:, p, :], k.gbank[0][:, :], ALU.mult).then_inc(k.share_used, 1)
                wait(dve, k.share_used, At(2 * e0 + p + 2, 2, it))
            if a0 + p >= 2:
                wait(dve, k.a_ready, a - 1)
            dve.tensor_tensor(k.a32[:, p, :], k.sil[:, p, :], k.bank[(g + 1).slot][:, :], ALU.mult
                              ).then_inc(k.bank_free, 2)
            wait(dve, k.a_hi, a + 1)
            f = At(p, 2, it).value
            dve.tensor_tensor(k.a_lo_buf[:, bass.ds(f, 1), :], k.a32[:, p:p + 1, :],
                              k.a_hi_buf[:, bass.ds(f, 1), :].bitcast(F32), ALU.subtract).then_inc(k.a_ready, 1)


def act_down(k, g1, sq0=None, x0=None):
    act = k.nc.scalar
    trips = DC // RING
    final = g1 + DC == k.n_blocks
    def body(it, t0):
        for b in range(RING):
            g = At(g1 + t0 * RING + b, RING if it is not None else 0, it)
            act_split(k, g + LEAD)
            if sq0 is not None:
                c = At(b + t0 * RING, RING, it) if it is not None else At(b + t0 * RING)
                src = k.acc if x0 is None else k.x
                act_square(k, src[:, bass.ds(c.value, 1), :] if it is not None else src[:, c.base, :], c + sq0,
                           lambda act: wait(act, k.bank_free, g + 1) if x0 is None else wait(act, k.x_ready, c + (x0 + 1)))
    loop_but_last(act, trips, final, body)


def loop_but_last(eng, trips, peel, body):
    with eng.Fori(0, trips - 1 if peel else trips) as it:
        body(it, 0)
    if peel:
        body(None, trips - 1)


def dve_down(k, g1, add, sq0=None, into_x=None):
    dve = k.nc.vector
    trips = DC // RING
    final = g1 + DC == k.n_blocks
    if sq0 is not None:
        dve.memset(k.ssq[:, :], 0.0).then_inc(k.ssq_clear, 1)
        k.n_clear += 1
        dve.wait_ge(k.ssq_clear, k.n_clear)
    def body(it, t0):
        for b in range(RING):
            g = At(g1 + t0 * RING + b, RING if it is not None else 0, it)
            c = At(b + t0 * RING, RING if it is not None else 0, it)
            acc = k.acc[:, bass.ds(c.value, 1), :] if it is not None else k.acc[:, c.base:c.base + 1, :]
            bank = k.bank[g.slot][:, :].rearrange("p (o f) -> p o f", o=1)
            dve_split(k, g + LEAD)
            wait(dve, k.block_done, g + 1)
            if add:
                dve.tensor_tensor(acc, acc, bank, ALU.add).then_inc(k.bank_free, 1)
            else:
                dve.tensor_copy(acc, bank).then_inc(k.bank_free, 1)
            if into_x is not None:
                x0, gate = into_x
                x = k.x[:, bass.ds(c.value, 1), :]
                wait(dve, k.bank_free, g + 1)
                dve.scalar_tensor_tensor(x, acc, gate[:, bass.ds(c.value, 1)], x, ALU.mult, ALU.add).then_inc(k.x_ready, 1)
            if sq0 is not None:
                dve_add_square(k, c + sq0, first=False)
    loop_but_last(dve, trips, final, body)


class Counts:

    def __init__(self):
        self.g = 0
        self.a = 0
        self.sq = 0
        self.norm = 0
        self.h = 0
        self.xc = 0
        self.y = 0


def pe_mod_block(k, g):
    c = lambda t: (k.c_hi[:, t, :], k.c_lo[:, t, :])
    pe_block(k, g, DC, c, out=k.bank[g.slot][:, 0:2])


def dve_mod_block(k, g, j):
    dve = k.nc.vector
    wait(dve, k.block_done, g + 1)
    dst = k.mod[:, bass.ds(j.value, 1), :] if isinstance(j, At) else k.mod[:, j:j + 1, :]
    dve.tensor_copy(dst, k.bank[g.slot][:, 0:2].rearrange("p (o f) -> p o f", o=1)).then_inc(k.bank_free, 1)


class Mod(Phase):
    blocks = 2 * DC
    LOADS = 2

    def advance(self, q):
        q.g += self.blocks

    def pe(self, k, q):
        k.nc.tensor.wait_ge(k.c_ready, 3)
        for b in range(RING):
            pe_mod_block(k, At(b))
        with k.nc.tensor.Fori(0, self.blocks // RING - 1) as it:
            for b in range(RING):
                pe_mod_block(k, At(RING + b, RING, it))

    def act(self, k, q):
        act = k.nc.scalar
        act.wait_ge(k.small_loaded, 16 * self.LOADS)
        act.activation(k.c32[:, :, :], k.c_in[:, :, :], ACT.Silu).then_inc(k.c_ready, 1)
        act.wait_ge(k.c_ready, 1)
        act.activation(k.c_hi[:, :, :], k.c32[:, :, :], ACT.Copy).then_inc(k.c_ready, 1)
        for g in range(RING + LEAD):
            act_split(k, At(g))
        with act.Fori(0, self.blocks // RING - 1) as it:
            for b in range(RING):
                act_split(k, At(RING + LEAD + b, RING, it))

    def dve(self, k, q):
        dve = k.nc.vector
        dve.wait_ge(k.c_ready, 2)
        dve.tensor_tensor(k.c_lo[:, :, :], k.c32[:, :, :], k.c_hi[:, :, :].bitcast(F32), ALU.subtract).then_inc(k.c_ready, 1)
        for g in range(LEAD):
            dve_split(k, At(g))
        for b in range(RING):
            dve_split(k, At(b + LEAD))
            dve_mod_block(k, At(b), b)
        with dve.Fori(0, self.blocks // RING - 1) as it:
            for b in range(RING):
                g = At(RING + b, RING, it)
                dve_split(k, g + LEAD)
                dve_mod_block(k, g, g)


HEADS = 8
CH = 64
NCH = (T + TC) // CH
CCH = TC // CH
TT = T + TC
HEAD_BLOCKS = 8
CHAIN = [list(range(NCH)), list(range(CCH - 1, -1, -1)) + list(range(NCH - 1, CCH - 1, -1))]
STEPS = NCH - 1
REF = [CH // 2 - 1, CH // 2]
END = [CH - 1, 0]
N_TOK, N_SC, N_KV = 6, 2, 6
G_HEAD = N_TOK + N_SC + N_KV + 1
STATE_COPIES = 2 * (STEPS - 3)


class Head:

    def __init__(self, n):
        self.n = n if isinstance(n, At) else At(n)

    def count(self, per, i=0):
        return self.n.times(per) + i


def head_view(buf, h):
    return buf[:, bass.ds(h.value, 1), :].rearrange("p o f -> p (o f)") if h.reg is not None else buf[:, h.base, :]


def column(buf, h):
    return buf[:, bass.ds(h.value, 1)] if h.reg is not None else buf[:, h.base:h.base + 1]


class Hgrn(Phase):
    blocks = HEADS * HEAD_BLOCKS
    prefix = 0

    def advance(self, q):
        q.g += self.blocks
        q.norm += HEADS

    def layout(self, k, ctx):
        at = k.low
        def put(name, shape, dt=F32):
            nonlocal at
            t = k.sb(name, shape, dt, at=at)
            at += -(-int(np.prod(shape[1:])) * (1 if dt == I8 else 4) // 64) * 64
            return t
        k.hc_hi = put("hc_hi", [P, DC, TC], F32R)
        k.hc_lo = put("hc_lo", [P, DC, TC], F32R)
        k.z_st = put("z_st", [P, 2, TT])
        k.v_st = put("v_st", [P, TT])
        k.q_st = put("q_st", [P, T])
        k.g_st = put("g_st", [P, T])
        k.keep = put("keep", [P, 2, TT])
        k.kk = put("kk", [P, 2, TT])
        k.cum = put("cum", [P, 2, TT])
        k.ktok = k.sb("ktok", [P, 2, TT // P, P], F32, at=k.arena["cum"][0])
        k.qq = put("qq", [P, 2, T])
        k.vtok = put("vtok", [P, T // P, P])
        k.v_half = put("v_half", [P, 2, TT // P, P])
        k.pt = put("pt", [P, 2, T // P, P])
        k.pt_mask = put("pt_mask", [P, 2, T // P, P], I8)
        k.state = put("state", [P, 2, T // CH, P])
        k.xs = put("xs", [P, 2, 2, P])
        k.restart = put("restart", [P, TT])
        k.silg = put("silg", [P, T])
        k.o32 = put("o32", [P, T])
        k.osq = put("osq", [P, T])
        k.refs = put("refs", [P, 2, NCH])
        k.lastref = put("lastref", [P, 2, NCH])
        k.rho = put("rho", [P, 2, NCH])
        k.lb = put("lb", [P, 2, HEADS])
        k.one_lb = put("one_lb", [P, 2, HEADS])
        k.lbt = put("lbt", [P, 4, HEADS])
        assert at <= k.limit
        (k.y_hi, k.y_parts, k.pool_order, k.lb_max, k.lb_sub, k.lb_exp, k.lb_sum
         ) = k.sems("y_hi y_parts pool_order lb_max lb_sub lb_exp lb_sum")
        (k.mod1, k.mod2, k.cbank_free, k.silq_done, k.silg_done, k.tok_part, k.y32_ready
         ) = k.sems("mod1 mod2 cbank_free silq_done silg_done tok_part y32_ready")
        (k.sig_done, k.ln_done, k.scan_done, k.exp_done, k.kk_done, k.qq_done, k.gla_full
         ) = k.sems("sig_done ln_done scan_done exp_done kk_done qq_done gla_full")
        (k.tok_copied, k.pt_ready, k.state_copied, k.o_taken, k.osq_ready, k.y_ready, k.lb_ready
         ) = k.sems("tok_copied pt_ready state_copied o_taken osq_ready y_ready lb_ready")
        k.hd_order, k.chain_step, k.rho_done = k.sems("hd_order chain_step rho_done")

    def pe_iteration(self, k, q, h, e):
        pe = k.nc.tensor
        lat = lambda t: (k.h_hi_buf[:, t, :], k.h_lo_buf[:, t, :])
        con = lambda t: (k.hc_hi[:, t, :], k.hc_lo[:, t, :])
        if h is not None:
            g = h.n.times(HEAD_BLOCKS) + q.g
            for b in range(2):
                pe_block(k, g + b, DC, lat, more=(con, k.cbank[:, 0:TC], h.count(3, b)))
            pe_block(k, g + 2, DC, lat)
        if e is not None:
            self.pe_tokens(k, e)
        if h is not None:
            pe_block(k, g + 3, DC, lat, more=(con, k.cbank[:, 0:TC], h.count(3, 2)))
        if e is not None:
            self.pe_states(k, e)
        if h is not None:
            pe_block(k, g + 4, DC, lat)
            for b in range(5, 8):
                pe_mod_block(k, g + b)
        if e is not None:
            self.pe_output(k, q, e)

    def pe_tokens(self, k, e):
        pe = k.nc.tensor
        wait(pe, k.kk_done, e.count(2, 2))
        n = 0
        for src in (lambda j: k.v_st[:, j * P:(j + 1) * P], lambda j: k.kk[:, 0, j * P:(j + 1) * P],
                    lambda j: k.kk[:, 1, j * P:(j + 1) * P]):
            for tiles in (range(4), range(4, 6)):
                if n < 2:
                    wait(pe, k.o_taken, e.n)
                else:
                    wait(pe, k.tok_copied, e.count(N_TOK, n - 1))
                for i, j in enumerate(tiles):
                    last = pe.transpose(k.gbank[n % 2][:, i * P:(i + 1) * P], src(j), k.ident[:, :])
                last.then_inc(k.gla_full, 1)
                n += 1
        wait(pe, k.qq_done, e.count(2, 2))
        for d in range(2):
            wait(pe, k.tok_copied, e.count(N_TOK, 5 + d))
            for j in range(T // P):
                last = pe.matmul(k.gbank[d][:, j * P:(j + 1) * P], k.kk[:, d, TC + j * P:TC + (j + 1) * P],
                                 k.qq[:, d, j * P:(j + 1) * P], start=True, stop=True)
            last.then_inc(k.gla_full, 1)
            n += 1

    def pe_states(self, k, e):
        pe = k.nc.tensor
        for n in range(N_KV):
            d, lot = n % 2, n // 2
            if n < 2:
                wait(pe, k.tok_copied, e.count(N_TOK, N_TOK))
                wait(pe, k.tok_part, e.count(4, 4))
                wait(pe, k.pt_ready, e.count(N_SC, n + 1))
            else:
                wait(pe, k.chain_step, e.count(2 * STEPS, 2 * (4 * lot - 1) + d + 1))
            for i, j in enumerate(range(4 * lot, min(4 * lot + 4, STEPS))):
                c = CHAIN[d][j]
                last = pe.matmul(k.gbank[d][:, i * P:(i + 1) * P], k.ktok[:, d, c // 2, :],
                                 k.v_half[:, c % 2, c // 2, :], start=True, stop=True)
            last.then_inc(k.gla_full, 1)

    def pe_output(self, k, q, e):
        pe = k.nc.tensor
        wait(pe, k.chain_step, e.count(2 * STEPS, 2 * STEPS))
        wait(pe, k.state_copied, e.count(STATE_COPIES, STATE_COPIES))
        o = k.gbank[0]
        for j in range(T // P):
            for d in range(2):
                pe.matmul(o[:, j * P:(j + 1) * P], k.vtok[:, j, :], k.pt[:, d, j, :], start=(d == 0), stop=False)
            for half in range(2):
                c = 2 * j + half
                for d in range(2):
                    at = c if d == 0 else T // CH - 1 - c
                    last = pe.matmul(o[:, c * CH:(c + 1) * CH], k.state[:, d, at, :], k.qq[:, d, c * CH:(c + 1) * CH],
                                     start=False, stop=(half == 1 and d == 1))
        last.then_inc(k.gla_full, 1)
        wait(pe, k.osq_ready, e.count(1, 1))
        wait(pe, k.rstd_ready, e.n + q.norm)
        pe.matmul(k.nbank[:, :], k.ones[:, :], k.osq[:, :], start=True, stop=True).then_inc(k.norm_sum, 1)

    def run(self, eng, k, q, iteration):
        iteration(k, q, Head(0), None)
        iteration(k, q, Head(1), Head(0))
        with eng.Fori(0, HEADS - 2) as it:
            iteration(k, q, Head(At(2, 1, it)), Head(At(1, 1, it)))
        iteration(k, q, None, Head(HEADS - 1))

    def pe(self, k, q):
        pe = k.nc.tensor
        pe.wait_ge(k.h_ready, q.h)
        self.run(pe, k, q, self.pe_iteration)

    def act_iteration(self, k, q, h, e):
        act = k.nc.scalar
        g = h.n.times(HEAD_BLOCKS) + q.g if h is not None else None
        last = h is None
        def split(b):
            if h is not None:
                act_split(k, g + b + LEAD)
        if e is not None:
            wait(act, k.bank_free, e.n.times(HEAD_BLOCKS) + (q.g + 5))
            wait(act, k.cbank_free, e.count(3, 3))
            for d in range(2):
                act.activation(k.keep[:, d, :], k.z_st[:, d, :], ACT.Sigmoid).then_inc(k.sig_done, 1)
                act.activation(k.kk[:, d, :], k.z_st[:, d, :], ACT.Sigmoid, scale=-1.0).then_inc(k.sig_done, 1)
            act.activation(k.qq[:, 0, :], k.q_st[:, :], ACT.Sigmoid).then_inc(k.sig_done, 1)
            act.activation(k.silg[:, :], k.g_st[:, :], ACT.Sigmoid).then_inc(k.sig_done, 1)
        split(0)
        if e is not None:
            for d in range(2):
                wait(act, k.sig_done, e.count(6, 2 * d + 1))
                act.activation(k.keep[:, d, :], k.keep[:, d, :], ACT.Ln, bias=column(k.lb[:, d, :], e.n),
                               scale=column(k.one_lb[:, d, :], e.n)).then_inc(k.ln_done, 1)
        split(1)
        if e is not None:
            for d in range(2):
                wait(act, k.scan_done, e.count(2, d + 1))
                act.activation(k.rho[:, d, :], k.rho[:, d, :], ACT.Exp).then_inc(k.rho_done, 1)
                act.activation(k.keep[:, d, :], k.cum[:, d, :], ACT.Exp, scale=-1.0).then_inc(k.exp_done, 1)
                if d == 0:
                    wait(act, k.silq_done, e.count(1, 1))
                act.activation(k.qq[:, d, :], k.cum[:, d, TC:], ACT.Exp).then_inc(k.exp_done, 1)
        split(2)
        if e is not None:
            n = 0
            wait(act, k.exp_done, e.count(4, 4))
            for dst in ("v", 0, 1):
                for tiles in (range(4), range(4, 6)):
                    wait(act, k.gla_full, e.count(G_HEAD, n + 1))
                    src = k.gbank[n % 2][:, :len(tiles) * P].rearrange("p (j v) -> p j v", v=P)
                    j0, j1 = tiles[0], tiles[-1] + 1
                    if dst == "v":
                        a, b = max(j0, TC // P), j1
                        act.activation(k.vtok[:, a - TC // P:b - TC // P, :], src[:, a - j0:b - j0, :], ACT.Copy).then_inc(k.tok_part, 1)
                        act.activation(k.v_half[0:CH, 0, j0:j1, :], src[0:CH], ACT.Copy).then_inc(k.tok_part, 1)
                        act.activation(k.v_half[CH:P, 1, j0:j1, :], src[CH:P], ACT.Copy).then_inc(k.tok_copied, 1)
                    else:
                        act.activation(k.ktok[:, dst, j0:j1, :], src, ACT.Copy).then_inc(k.tok_copied, 1)
                    n += 1
        split(3)
        split(4)
        if e is not None:
            for j in range(3, STEPS):
                for d in range(2):
                    c = CHAIN[d][j]
                    wait(act, k.chain_step, e.count(2 * STEPS, 2 * j + d + 1))
                    act.activation(k.state[:, d, j - 3, :], k.xs[:, d, j % 2, :], ACT.Copy,
                                   scale=k.rho[:, d, c:c + 1]).then_inc(k.state_copied, 1)
        for b in (5, 6, 7):
            split(b)
        if e is not None:
            wait(act, k.o_taken, e.count(1, 1))
            act.activation(k.osq[:, :], k.o32[:, :], ACT.Square).then_inc(k.osq_ready, 1)
            act_rstd(k, e.n + q.norm, lambda act: wait(act, k.y_ready, e.n), scale=1.0 / P)
            wait(act, k.y32_ready, e.count(1, 1))
            act.activation(head_view(k.a_hi_buf, e.n), k.o32[:, :], ACT.Copy).then_inc(k.y_hi, 1)

    def act(self, k, q):
        self.run(k.nc.scalar, k, q, self.act_iteration)

    def dve_iteration(self, k, q, h, e):
        dve = k.nc.vector
        g = h.n.times(HEAD_BLOCKS) + q.g if h is not None else None
        def block(b, dst=None, con=None):
            if h is None:
                return
            if b != 3:
                dve_split(k, g + b + LEAD)
            if dst is None:
                j = h.n.times(3) + (2 * DC + b - 5)
                dve_mod_block(k, g + b, j if j.reg is not None else j.base)
                return
            wait(dve, k.block_done, g + b + 1)
            if con is not None:
                dve.tensor_copy(dst[:, 0:TC], k.cbank[:, 0:TC]).then_inc(k.cbank_free, 1)
                dve.tensor_copy(dst[:, TC:], k.bank[(g + b).slot][:, :]).then_inc(k.bank_free, 1)
            else:
                dve.tensor_copy(dst, k.bank[(g + b).slot][:, :]).then_inc(k.bank_free, 1)
        if e is not None:
            wait(dve, k.sig_done, e.count(6, 6))
            wait(dve, k.y32_ready, e.n)
            dve.tensor_tensor(k.q_st[:, :], k.q_st[:, :], k.qq[:, 0, :], ALU.mult).then_inc(k.silq_done, 1)
            dve.tensor_tensor(k.silg[:, :], k.silg[:, :], k.g_st[:, :], ALU.mult).then_inc(k.silg_done, 1)
        block(0, k.z_st[:, 0, :], 0)
        if e is not None:
            for d in range(2):
                wait(dve, k.ln_done, e.count(2, d + 1))
                way = slice(None) if d == 0 else slice(None, None, -1)
                dve.tensor_tensor_scan(k.cum[:, d, way], k.restart[:, :], k.keep[:, d, way], 0.0, ALU.mult, ALU.add
                                       ).then_inc(k.hd_order, 1)
                wait(dve, k.hd_order, e.count(10, 5 * d + 1))
                cum = k.cum[:, d, :].rearrange("p (n c) -> p n c", c=CH)
                dve.tensor_copy(k.refs[:, d, :], cum[:, :, REF[d]]).then_inc(k.hd_order, 1)
                wait(dve, k.hd_order, e.count(10, 5 * d + 2))
                dve.tensor_tensor(k.lastref[:, d, :], cum[:, :, END[d]], k.refs[:, d, :], ALU.subtract).then_inc(k.hd_order, 1)
                wait(dve, k.hd_order, e.count(10, 5 * d + 3))
                if d == 0:
                    dve.tensor_tensor(k.rho[:, 0, 0:NCH - 1], k.lastref[:, 0, 0:NCH - 1], k.refs[:, 0, 1:NCH], ALU.add
                                      ).then_inc(k.hd_order, 1)
                    dve.tensor_copy(k.rho[:, 0, NCH - 1:NCH], k.lastref[:, 0, NCH - 1:NCH]).then_inc(k.hd_order, 1)
                else:
                    dve.tensor_tensor(k.rho[:, 1, 1:NCH], k.lastref[:, 1, 1:NCH], k.refs[:, 1, 0:NCH - 1], ALU.add
                                      ).then_inc(k.hd_order, 1)
                    dve.tensor_tensor(k.rho[:, 1, 0:1], k.lastref[:, 1, 0:1], k.refs[:, 1, NCH - 1:NCH], ALU.add
                                      ).then_inc(k.hd_order, 1)
                wait(dve, k.hd_order, e.count(10, 5 * d + 5))
                dve.tensor_tensor(cum, cum, k.refs[:, d, :].rearrange("p (n o) -> p n o", o=1).to_broadcast([P, NCH, CH]),
                                  ALU.subtract).then_inc(k.scan_done, 1)
        block(1, k.z_st[:, 1, :], 1)
        if e is not None:
            for d in range(2):
                wait(dve, k.exp_done, e.count(4, 2 * d + 2))
                dve.scalar_tensor_tensor(k.kk[:, d, :], k.kk[:, d, :], column(k.one_lb[:, d, :], e.n), k.keep[:, d, :],
                                         ALU.mult, ALU.mult).then_inc(k.kk_done, 1)
                dve.tensor_tensor(k.qq[:, d, :], k.qq[:, d, :], k.q_st[:, :], ALU.mult).then_inc(k.qq_done, 1)
            wait(dve, k.qq_done, e.count(2, 2))
        block(2, k.q_st[:, :])
        if e is not None:
            wait(dve, k.gla_full, e.count(G_HEAD, N_TOK + N_SC))
        if h is not None:
            dve_split(k, g + 3 + LEAD)
        if e is not None:
            for d in range(2):
                dve.copy_predicated(k.pt[:, d, :, :], k.pt_mask[:, d, :, :],
                                    k.gbank[d][:, :].rearrange("p (j t) -> p j t", t=P)).then_inc(k.pt_ready, 1)
        block(3, k.v_st[:, :], 0)
        if e is not None:
            for j in range(STEPS):
                for d in range(2):
                    s = 2 * j + d
                    if j % 4 == 0:
                        wait(dve, k.gla_full, e.count(G_HEAD, N_TOK + N_SC + 2 * (j // 4) + d + 1))
                    if j > 0:
                        wait(dve, k.chain_step, e.count(2 * STEPS, s - 1))
                    if j >= 5:
                        wait(dve, k.state_copied, e.count(STATE_COPIES, 2 * (j - 5) + d + 1))
                    kv = k.gbank[d][:, (j % 4) * P:(j % 4 + 1) * P]
                    before = CHAIN[d][j - 1]
                    if j == 0:
                        ins = dve.tensor_copy(k.xs[:, d, 0, :], kv)
                    else:
                        ins = dve.scalar_tensor_tensor(k.xs[:, d, j % 2, :], k.xs[:, d, (j - 1) % 2, :],
                                                       k.rho[:, d, before:before + 1], kv, ALU.mult, ALU.add)
                    ins.then_inc(k.chain_step, 1)
        if e is not None:
            wait(dve, k.silg_done, e.count(1, 1))
        block(4, k.g_st[:, :])
        for b in (5, 6, 7):
            block(b)
        if e is not None:
            wait(dve, k.gla_full, e.count(G_HEAD, G_HEAD))
            wait(dve, k.y_parts, e.n)
            dve.tensor_copy(k.o32[:, :], k.gbank[0][:, :]).then_inc(k.o_taken, 1)
            wait(dve, k.rstd_ready, e.n + (q.norm + 1))
            wait(dve, k.osq_ready, e.count(1, 1))
            dve.scalar_tensor_tensor(k.o32[:, :], k.o32[:, :], k.vec("gnorm")[:, 0:1], k.rstd[:, :], ALU.mult, ALU.mult
                                     ).then_inc(k.y_ready, 1)
            wait(dve, k.y_ready, e.count(1, 1))
            dve.tensor_tensor(k.o32[:, :], k.o32[:, :], k.silg[:, :], ALU.mult).then_inc(k.y32_ready, 1)
            wait(dve, k.y_hi, e.n + 1)
            dve.tensor_tensor(head_view(k.a_lo_buf, e.n), k.o32[:, :], head_view(k.a_hi_buf, e.n).bitcast(F32), ALU.subtract
                              ).then_inc(k.y_parts, 1)


    def dve(self, k, q):
        self.run(k.nc.vector, k, q, self.dve_iteration)


class HgrnInput(Phase):
    blocks = 0

    def advance(self, q):
        q.sq += 2 * DC
        q.norm += 2
        q.h += 2 * DC

    def layout(self, k, ctx):
        at = k.low + 2 * DC * TC * 4
        k.x1 = k.sb("x1", [P, DC, T], F32, at=at)
        k.xc1 = k.sb("xc1", [P, DC, TC], F32, at=at + DC * T * 4)
        k.sq1 = k.sb("sq1", [P, 2, T], F32, at=at + DC * (T + TC) * 4)
        k.h321 = k.sb("h321", [P, 2, T], F32, at=at + DC * (T + TC) * 4 + 2 * T * 4)

    def pool(self, k, q):
        pool = k.nc.gpsimd
        done = Order(pool, k.pool_order)
        def then(ins):
            done(ins)
            done.wait()
        then(pool.memset(k.restart[:, :], 1.0))
        then(pool.memset(k.pt_mask[:, :, :, :], 1))
        then(pool.memset(k.restart[:, ::CH], 0.0))
        for d in range(2):
            then(pool.affine_select(out=k.pt_mask[:, d, :, :], in_=k.pt_mask[:, d, :, :], compare_op=ALU.is_ge,
                                    fill=0.0, base=0, pattern=[[0, T // P], [1 - 2 * d, P]],
                                    channel_multiplier=2 * d - 1))
        then(pool.memset(k.pt_mask[0:CH, 0, :, CH:P], 0))
        then(pool.memset(k.pt_mask[CH:P, 1, :, 0:CH], 0))
        then(pool.memset(k.pt[:, :, :, :], 0.0))
        then(pool.memset(k.v_half[:, :, :, :], 0.0))

    def pe(self, k, q):
        pe_norm(k, q.norm, q.sq + DC, TC)
        pe_norm(k, q.norm + 1, q.sq + 2 * DC)

    def act(self, k, q):
        act = k.nc.scalar
        k.sq, k.h32 = k.sq1, k.h321
        act.wait_ge(k.lb_sub, 4)
        act.activation(k.lbt[:, 0:2, :], k.lbt[:, 0:2, :], ACT.Exp).then_inc(k.lb_exp, 1)
        act.activation(k.lbt[:, 2:4, :], k.lbt[:, 2:4, :], ACT.Exp).then_inc(k.lb_exp, 1)
        for c in range(DC):
            act_square(k, k.xc1[:, c, :], At(q.sq + c), lambda act: wait(act, k.x_loaded, 32))
        act_rstd(k, q.norm, lambda act: None, TC)
        for c in range(DC):
            act_square(k, k.x1[:, c, :], At(q.sq + DC + c), lambda act: wait(act, k.x_loaded, 32))
        act_prenorm(k, q.h, k.shift1[:, 1, :], k.hc_hi, TC)
        act_rstd(k, q.norm + 1, lambda act: wait(act, k.h_ready, q.h + DC))
        act_prenorm(k, q.h + DC, k.shift1[:, 0, :], k.h_hi_buf)
        act.wait_ge(k.pool_order, 9)
        act.wait_ge(k.lb_ready, 4)

    def dve(self, k, q):
        dve = k.nc.vector
        k.sq, k.h32 = k.sq1, k.h321
        lbf, lbb = k.vec("lb_f"), k.vec("lb_b")
        for d, v in enumerate((lbf, lbb)):
            dve.tensor_tensor(k.lb[:, d, :], v[:, 0:8], v[:, 8:16], ALU.max).then_inc(k.lb_max, 1)
        dve.wait_ge(k.lb_max, 2)
        for d, v in enumerate((lbf, lbb)):
            dve.tensor_tensor(k.lbt[:, 2 * d, :], v[:, 0:8], k.lb[:, d, :], ALU.subtract).then_inc(k.lb_sub, 1)
            dve.tensor_tensor(k.lbt[:, 2 * d + 1, :], v[:, 8:16], k.lb[:, d, :], ALU.subtract).then_inc(k.lb_sub, 1)
        dve.wait_ge(k.lb_sub, 4)
        for c in range(DC):
            dve_add_square(k, At(q.sq + c), first=(c == 0), width=TC)
        dve.wait_ge(k.lb_exp, 2)
        for d in range(2):
            dve.tensor_tensor(k.lb[:, d, :], k.lbt[:, 2 * d, :], k.lbt[:, 2 * d + 1, :], ALU.add).then_inc(k.lb_sum, 1)
        dve.wait_ge(k.lb_sum, 2)
        dve.reciprocal(k.lb[:, :, :], k.lb[:, :, :]).then_inc(k.lb_sum, 1)
        dve.wait_ge(k.lb_sum, 3)
        for d in range(2):
            dve.tensor_tensor(k.one_lb[:, d, :], k.lbt[:, 2 * d + 1, :], k.lb[:, d, :], ALU.mult).then_inc(k.lb_ready, 1)
        dve.wait_ge(k.lb_ready, 2)
        for d in range(2):
            dve.tensor_tensor(k.lb[:, d, :], k.lbt[:, 2 * d, :], k.lb[:, d, :], ALU.mult).then_inc(k.lb_ready, 1)
        dve.wait_ge(k.bank_free, q.g)
        b = k.vec("b_mod")
        for w in range(2):
            dve.tensor_tensor(k.shift1[:, w, :], k.mod[:, 0:DC, w], b[:, 0:DC], ALU.add).then_inc(k.mod1, 1)
            dve.tensor_tensor(k.gain1[:, w, :], k.mod[:, DC:2 * DC, w], b[:, DC:2 * DC], ALU.add).then_inc(k.mod1, 1)
        dve.wait_ge(k.mod1, 4)
        for w in range(2):
            dve.scalar_tensor_tensor(k.gain1[:, w, :], k.gain1[:, w, :], 1.0, k.vec("norm1_g"), ALU.add, ALU.mult
                                     ).then_inc(k.mod1, 1)
        dve.wait_ge(k.rstd_ready, q.norm + 1)
        for c in range(DC):
            dve_add_square(k, At(q.sq + DC + c), first=(c == 0))
        dve.wait_ge(k.mod1, 6)
        dve_prenorm(k, q.norm, q.h, k.xc1, k.gain1[:, 1, :], k.shift1[:, 1, :], k.hc_hi, k.hc_lo, TC)
        dve_prenorm(k, q.norm + 1, q.h + DC, k.x1, k.gain1[:, 0, :], k.shift1[:, 0, :], k.h_hi_buf, k.h_lo_buf)
        dve.wait_ge(k.pool_order, 9)


class HgrnOutput(Phase):
    blocks = 2 * DC

    def advance(self, q):
        q.g += self.blocks
        q.sq += DC

    def pe(self, k, q):
        pe = k.nc.tensor
        pe.wait_ge(k.y_parts, HEADS)
        y = lambda t: (k.a_hi_buf[:, t, :], k.a_lo_buf[:, t, :])
        with pe.Fori(0, DC // 2) as it:
            for b in range(RING):
                g = At(q.g + b, RING, it)
                if b % 2 == 0:
                    pe_block(k, g, DC, y)
                else:
                    pe_mod_block(k, g)

    def act(self, k, q):
        act = k.nc.scalar
        k.sq, k.h32 = k.sq0, k.h320
        act.wait_ge(k.block_done, q.g)
        act.wait_ge(k.y32_ready, HEADS)
        act.wait_ge(k.y_parts, HEADS)
        act.dma_start(k.x[:, :, :], k.xT).then_inc(k.x_loaded, 16)
        with act.Fori(0, DC // 2) as it:
            for b in range(RING):
                g = At(q.g + b, RING, it)
                act_split(k, g + LEAD)
                if b % 2 == 0:
                    c = At(b // 2, 2, it)
                    act_square(k, k.x[:, bass.ds(c.value, 1), :], c + q.sq, lambda act: wait(act, k.bank_free, g + 1))

    def dve(self, k, q):
        dve = k.nc.vector
        k.sq, k.h32 = k.sq0, k.h320
        n = DC * 3 + 2 * DC
        b = k.vec("b_mod")
        dve.wait_ge(k.bank_free, q.g)
        dve.tensor_tensor(k.mod[:, 2 * DC:n, 0], k.mod[:, 2 * DC:n, 0], b[:, 2 * DC:n], ALU.add).then_inc(k.mod2, 1)
        dve.wait_ge(k.mod2, 1)
        dve.scalar_tensor_tensor(k.gain2[:, :], k.mod[:, 4 * DC:5 * DC, 0], 1.0, k.vec("norm2_g"), ALU.add, ALU.mult
                                 ).then_inc(k.mod2, 1)
        dve.tensor_copy(k.shift2[:, :], k.mod[:, 3 * DC:4 * DC, 0]).then_inc(k.mod2, 1)
        dve.memset(k.ssq[:, :], 0.0).then_inc(k.ssq_clear, 1)
        k.n_clear += 1
        dve.wait_ge(k.ssq_clear, k.n_clear)
        dve.wait_ge(k.x_loaded, 48)
        with dve.Fori(0, DC // 2) as it:
            for b in range(RING):
                g = At(q.g + b, RING, it)
                dve_split(k, g + LEAD)
                if b % 2 == 0:
                    c = At(b // 2, 2, it)
                    x = k.x[:, bass.ds(c.value, 1), :]
                    wait(dve, k.block_done, g + 1)
                    dve.scalar_tensor_tensor(x, k.bank[g.slot][:, :].rearrange("p (o f) -> p o f", o=1),
                                             k.mod[:, bass.ds((c + 2 * DC).value, 1), 0], x, ALU.mult, ALU.add
                                             ).then_inc(k.bank_free, 1)
                    dve_add_square(k, c + q.sq, first=False)
                else:
                    dve_mod_block(k, g, At(5 * DC + b // 2, 2, it))


N_EXPERTS = 16
GROUPS = 4
PER_GROUP = N_EXPERTS // GROUPS
D_EXPERT = 256
TT4 = T // P


class MoeInput(Phase):
    blocks = 0

    def advance(self, q):
        q.norm += 1
        q.h += DC

    def layout(self, k, ctx):
        at = k.top
        def put(name, shape, dt=F32):
            nonlocal at
            t = k.sb(name, shape, dt, at=at)
            at += -(-int(np.prod(shape[1:])) * 4 // 64) * 64
            return t
        k.share_sel = put("share_sel", [N_EXPERTS, N_EXPERTS, T])
        E = [P, TT4, GROUPS, PER_GROUP]
        k.score = put("score", E)
        k.choice = put("choice", E)
        k.rank = put("rank", E)
        k.above = put("above", E)
        k.keep4 = put("keep4", E)
        k.gsum = put("gsum", [P, TT4, GROUPS])
        k.grank = put("grank", [P, TT4, GROUPS])
        k.gabove = put("gabove", [P, TT4, GROUPS])
        k.den = put("den", [P, TT4])
        k.share_t = put("share_t", [N_EXPERTS, T])
        k.rw = put("rw", [P, DC, N_EXPERTS])
        k.rw_hi = put("rw_hi", [P, DC, N_EXPERTS], F32R)
        k.rw_lo = put("rw_lo", [P, DC, N_EXPERTS], F32R)
        assert at <= k.limit, at
        (k.share_ready, k.share_used, k.share_sel_ready, k.rw_loaded, k.rw_split, k.logits_done, k.score_done
         ) = k.sems("share_ready share_used share_sel_ready rw_loaded rw_split logits_done score_done")
        k.route, = k.sems("route")

    def pe(self, k, q):
        pe = k.nc.tensor
        pe_norm(k, q.norm, q.sq)
        pe.wait_ge(k.h_ready, q.h + DC)
        pe.wait_ge(k.rw_split, 2)
        for t in range(TT4):
            tok = slice(t * P, (t + 1) * P)
            out = k.gbank[1][:, t * N_EXPERTS:(t + 1) * N_EXPERTS]
            for c in range(DC):
                pe.matmul(out, k.h_hi_buf[:, c, tok], k.rw_hi[:, c, :], start=(c == 0), stop=False)
                pe.matmul(out, k.h_lo_buf[:, c, tok], k.rw_hi[:, c, :], start=False, stop=False)
                last = pe.matmul(out, k.h_hi_buf[:, c, tok], k.rw_lo[:, c, :], start=False, stop=(c == DC - 1))
        last.then_inc(k.logits_done, 1)
        pe.wait_ge(k.route, k.ROUTE_STEPS)
        for t in range(TT4):
            last = pe.transpose(k.gbank[1][0:N_EXPERTS, t * P:(t + 1) * P],
                                k.keep4[:, t, :, :].rearrange("p g e -> p (g e)"), k.ident[:, :])
        last.then_inc(k.logits_done, 1)

    def act(self, k, q):
        act = k.nc.scalar
        act_rstd(k, q.norm, lambda act: None)
        act.dma_start(k.rw[:, :, :], k.dram["rw"]).then_inc(k.rw_loaded, 16)
        act_prenorm(k, q.h, k.shift2[:, :], k.h_hi_buf)
        act.wait_ge(k.rw_loaded, 16)
        act.activation(k.rw_hi[:, :, :], k.rw[:, :, :], ACT.Copy).then_inc(k.rw_split, 1)
        act.wait_ge(k.logits_done, 1)
        act.activation(k.score[:, :, :, :].rearrange("p t g e -> p (t g e)"), k.gbank[1][:, 0:TT4 * N_EXPERTS], ACT.Sigmoid
                       ).then_inc(k.score_done, 1)

    def dve(self, k, q):
        dve = k.nc.vector
        dve_prenorm(k, q.norm, q.h, k.x, k.gain2, k.shift2, k.h_hi_buf, k.h_lo_buf)
        dve.wait_ge(k.rw_split, 1)
        dve.tensor_tensor(k.rw_lo[:, :, :], k.rw[:, :, :], k.rw_hi[:, :, :].bitcast(F32), ALU.subtract).then_inc(k.rw_split, 1)
        step = Order(dve, k.route)
        def then(ins):
            step(ins)
            step.wait()
        for i in range(PER_GROUP):
            then(dve.memset(k.rank[:, :, :, i:i + 1], float(PER_GROUP - 1 - i)))
            then(dve.memset(k.grank[:, :, i:i + 1], float(GROUPS - 1 - i)))
        dve.wait_ge(k.score_done, 1)
        bias = k.vec("router_b").rearrange("p (o g e) -> p o g e", o=1, g=GROUPS).to_broadcast([P, TT4, GROUPS, PER_GROUP])
        then(dve.tensor_tensor(k.choice[:, :, :, :], k.score[:, :, :, :], bias, ALU.add))
        for d in range(1, PER_GROUP):
            n = PER_GROUP - d
            ab = k.above[:, :, :, 0:n]
            then(dve.tensor_tensor(ab, k.choice[:, :, :, 0:n], k.choice[:, :, :, d:], ALU.is_ge))
            then(dve.tensor_tensor(k.rank[:, :, :, d:], k.rank[:, :, :, d:], ab, ALU.add))
            then(dve.tensor_tensor(k.rank[:, :, :, 0:n], k.rank[:, :, :, 0:n], ab, ALU.subtract))
        then(dve.tensor_scalar(k.keep4[:, :, :, :], k.rank[:, :, :, :], 1.5, None, ALU.is_lt))
        then(dve.tensor_tensor(k.above[:, :, :, :], k.keep4[:, :, :, :], k.choice[:, :, :, :], ALU.mult))
        then(dve.tensor_reduce(k.gsum[:, :, :], k.above[:, :, :, :], AX.X, ALU.add))
        for d in range(1, GROUPS):
            n = GROUPS - d
            ab = k.gabove[:, :, 0:n]
            then(dve.tensor_tensor(ab, k.gsum[:, :, 0:n], k.gsum[:, :, d:], ALU.is_ge))
            then(dve.tensor_tensor(k.grank[:, :, d:], k.grank[:, :, d:], ab, ALU.add))
            then(dve.tensor_tensor(k.grank[:, :, 0:n], k.grank[:, :, 0:n], ab, ALU.subtract))
        then(dve.tensor_scalar(k.grank[:, :, :], k.grank[:, :, :], 0.5, None, ALU.is_lt))
        then(dve.tensor_tensor(k.keep4[:, :, :, :], k.keep4[:, :, :, :],
                               k.grank[:, :, :].rearrange("p t (g o) -> p t g o", o=1).to_broadcast([P, TT4, GROUPS, PER_GROUP]), ALU.mult))
        then(dve.tensor_tensor(k.keep4[:, :, :, :], k.keep4[:, :, :, :], k.score[:, :, :, :], ALU.mult))
        then(dve.tensor_reduce(k.den[:, :], k.keep4[:, :, :, :], AX.XY, ALU.add))
        then(dve.reciprocal(k.den[:, :], k.den[:, :]))
        then(dve.tensor_tensor(k.keep4[:, :, :, :], k.keep4[:, :, :, :],
                               k.den[:, :].rearrange("p (t a b) -> p t a b", a=1, b=1).to_broadcast([P, TT4, GROUPS, PER_GROUP]), ALU.mult))
        assert step.n.base == k.ROUTE_STEPS, step.n.base
        dve.wait_ge(k.logits_done, 2)
        dve.tensor_copy(k.share_t[:, :], k.gbank[1][0:N_EXPERTS, :]).then_inc(k.share_used, 1)
        dve.wait_ge(k.share_used, 1)
        for n in range(4):
            dve.tensor_tensor(k.share_sel[:, 4 * n:4 * n + 4, :],
                              k.share_t[:, :].rearrange("p (o f) -> p o f", o=1).to_broadcast([N_EXPERTS, 4, T]),
                              k.ident[0:N_EXPERTS, 4 * n:4 * n + 4].rearrange("p (e o) -> p e o", o=1).to_broadcast([N_EXPERTS, 4, T]),
                              ALU.mult).then_inc(k.share_sel_ready, 1)


class Moe(Phase):
    PASSES = N_EXPERTS // 4
    blocks = PASSES * (16 + DC)

    def advance(self, q):
        q.g += self.blocks
        q.a += 2 * N_EXPERTS
        q.sq += DC
        q.xc += DC

    def pe(self, k, q):
        for n in range(self.PASSES):
            pe_pass(k, q.g + n * 24, 8, q.a + 8 * n, e0=4 * n)

    def act(self, k, q):
        for n in range(self.PASSES):
            act_pass(k, q.g + n * 24, 8, q.a + 8 * n)
            end = n == self.PASSES - 1
            act_down(k, q.g + n * 24 + 16, q.sq if end else None, q.xc if end else None)

    def dve(self, k, q):
        for n in range(self.PASSES):
            end = n == self.PASSES - 1
            if end:
                k.nc.vector.tensor_tensor(k.mod[:, 5 * DC:6 * DC, 0], k.mod[:, 5 * DC:6 * DC, 0],
                                          k.vec("b_mod")[:, 5 * DC:6 * DC], ALU.add).then_inc(k.mod2, 1)
                k.nc.vector.wait_ge(k.mod2, 4)
            dve_pass(k, q.g + n * 24, 8, q.a + 8 * n, e0=4 * n)
            dve_down(k, q.g + n * 24 + 16, add=n > 0, sq0=q.sq if end else None,
                     into_x=(q.xc, k.mod[:, 5 * DC:6 * DC, 0]) if end else None)


class Renorm(Phase):
    blocks = 0

    def advance(self, q):
        q.norm += 1
        q.sq += DC
        q.xc += DC

    def pe(self, k, q):
        pe_norm(k, q.norm, q.sq)

    def act(self, k, q):
        act_rstd(k, q.norm, lambda act: None)
        act_residual(k, q.xc, q.sq)

    def dve(self, k, q):
        dve = k.nc.vector
        wait(dve, k.rstd_ready, q.norm + 1)
        for c in range(DC + 1):
            if c < DC:
                dve.scalar_tensor_tensor(k.x[:, c, :], k.x[:, c, :], k.vec("final_g")[:, c:c + 1], k.rstd[:, :],
                                         ALU.mult, ALU.mult).then_inc(k.x_ready, 1)
            if c >= 1:
                dve_add_square(k, At(q.sq + c - 1), first=(c == 1))


class Ffn(Phase):
    blocks = sum(2 * nk + DC for nk in FF_SEGMENTS)

    def __init__(self, g_pre, g_post, last=False):
        self.g_pre, self.g_post, self.last = g_pre, g_post, last

    def advance(self, q):
        q.g += self.blocks
        q.a += D_FF // P
        q.sq += DC if self.last else 2 * DC
        q.norm += 2
        q.h += DC
        q.xc += DC
        q.y += DC

    def pe(self, k, q):
        pe_norm(k, q.norm, q.sq)
        g, a = q.g, q.a
        for s, nk in enumerate(FF_SEGMENTS):
            pe_pass(k, g, nk, a, h_ready=q.h + DC if s == 0 else None)
            g, a = g + 2 * nk + DC, a + nk
        pe_norm(k, q.norm + 1, q.sq + DC)

    def act(self, k, q):
        act_rstd(k, q.norm, lambda act: None)
        act_prenorm(k, q.h, None, k.h_hi_buf)
        g, a = q.g, q.a
        for s, nk in enumerate(FF_SEGMENTS):
            act_pass(k, g, nk, a)
            act_down(k, g + 2 * nk, q.sq if s == len(FF_SEGMENTS) - 1 else None)
            g, a = g + 2 * nk + DC, a + nk
        act_rstd(k, q.norm + 1, lambda act: wait(act, k.h_ready, q.h + DC))
        if not self.last:
            act_residual(k, q.xc, q.sq + DC)

    def dve(self, k, q):
        dve_prenorm(k, q.norm, q.h, k.x, k.vec(self.g_pre), None, k.h_hi_buf, k.h_lo_buf)
        g, a = q.g, q.a
        for s, nk in enumerate(FF_SEGMENTS):
            dve_pass(k, g, nk, a)
            dve_down(k, g + 2 * nk, add=s > 0, sq0=q.sq if s == len(FF_SEGMENTS) - 1 else None)
            g, a = g + 2 * nk + DC, a + nk
        dve_residual(k, q.norm + 1, q.xc, q.y, None if self.last else q.sq + DC, k.vec(self.g_post))


A_HEADS = 4
LAM_INIT = 0.8 - 0.6 * math.exp(-0.3 * 0)
B_HEADS = 8
BH = 64
BC = 4
RC = P
RN = T // RC
KAPPA = math.exp(-0.5)
LN_SCALE = 2.0 ** 17
LEVELS = [2, 4, 8, 16, 32, 64]
PREP_MM = 5


class EvenProj(Phase):
    blocks = 26

    def __init__(self, g_pre):
        self.g_pre = g_pre

    def advance(self, q):
        q.g += self.blocks
        q.norm += 1
        q.h += DC

    def layout(self, k, ctx):
        base = k.arena["acc"][0]
        def put(name, at, shape, dt=F32):
            size = int(np.prod(shape[1:])) * (1 if dt == I8 else 4)
            assert base + at + size <= k.limit, (name, base + at + size, k.limit)
            t = k.sb(name, shape, dt, at=base + at)
            return t, at + -(-size // 32) * 32
        KB = 1024
        k.rkv, _ = put("rkv", 0, [P, 3 * BC, T])
        k.qkv, _ = put("qkv", 24 * KB, [P, 12, T])
        k.ar, _ = put("ar", 24 * KB, [P, BC, 2, T])
        k.bt_y, _ = put("bt_y", 40 * KB, [P, BC, T])
        k.gin, _ = put("gin", 48 * KB, [P, T])
        k.lvl_mask, at = put("lvl_mask", 50 * KB, [P, len(LEVELS) + 1, 2, P], I8)
        k.tri, at = put("tri", at, [P, 3, P], I8)
        k.mcol, at = put("mcol", at, [P, BC, RN])
        k.rhos, at = put("rhos", at, [P, RN, BC])
        mats = at
        k.mat_a, at = put("mat_a", at, [P, B_HEADS, P])
        k.mat_at, at = put("mat_at", at, [P, B_HEADS, P])
        k.inv, at = put("inv", at, [P, B_HEADS, P])
        k.inv_t, at = put("inv_t", at, [P, B_HEADS, P])
        k.zst, at = put("zst", mats, [P, 2, T + 1])
        at = mats
        k.cumw, at = put("cumw", at, [P, T])
        k.ab, at = put("ab", at, [P, T])
        k.e_pos, at = put("e_pos", at, [P, RN * (RC + 1)])
        k.e_neg, at = put("e_neg", at, [P, T])
        k.kkr, at = put("kkr", at, [P, T])
        k.tmp1, at = put("tmp1", at, [P, T])
        k.tmp2, at = put("tmp2", at, [P, T])
        hb, ab = k.arena["h_hi_buf"][0], k.arena["a_hi_buf"][0]
        def putat(name, at, shape):
            return k.sb(name, shape, F32, at=at), at + int(np.prod(shape[1:])) * 4
        at = hb
        k.vtok_a, at = putat("vtok_a", at, [P, T // P, T])
        k.sc, at = putat("sc", at, [P, 2, 2, T])
        k.pn, at = putat("pn", at, [P, 2, T])
        k.ptr, at = putat("ptr", at, [P, 2, T])
        k.dist, at = putat("dist", at, [P, T])
        k.bias_h, at = putat("bias_h", at, [P, T])
        k.oa, at = putat("oa", at, [P, T])
        k.att_small, at = putat("att_small", at, [P, 64])
        assert at <= hb + 32 * KB
        k.vt, at = putat("vt", hb, [P, RN, T])
        k.btok, at = putat("btok", at, [P, RN, T])
        k.ktokr, at = putat("ktokr", at, [P, RN, T])
        k.mat_x, at = putat("mat_x", at, [P, B_HEADS, P])
        k.t_ak, at = putat("t_ak", at, [P, B_HEADS, P])
        assert at <= hb + 32 * KB
        k.t_rb, at = putat("t_rb", ab + 8 * KB, [P, B_HEADS, P])
        k.t_rk, at = putat("t_rk", at, [P, B_HEADS, P])
        at = k.arena["a_lo_buf"][0] + 8 * KB
        k.sqa, _ = putat("sqa", at, [P, 2, T])
        k.u_sb, at = putat("u_sb", at, [P, B_HEADS * BH])
        k.rhs_sb, at = putat("rhs_sb", at, [P, B_HEADS * BH])
        k.st, at = putat("st", at, [P, BC, BH])
        k.st2, at = putat("st2", at, [P, BC, BH])
        k.gup, at = putat("gup", at, [P, T])
        k.waup, _ = putat("waup", ab + 8 * KB, [P, T])
        k.wa, _ = putat("wa", ab + 10 * KB, [P, T])
        k.lam_in, _ = putat("lam_in", k.arena["a_lo_buf"][0] + 8 * KB, [P, 4 * BH])
        k.up_loaded, k.lam_loaded, k.shift_d, k.shifted = k.sems("up_loaded lam_loaded shift_d shifted")

    def pe(self, k, q):
        pe = k.nc.tensor
        pe_norm(k, q.norm, q.sq)
        pe.wait_ge(k.h_ready, q.h + DC)
        h = lambda t: (k.h_hi_buf[:, t, :], k.h_lo_buf[:, t, :])
        with pe.Fori(0, 6) as it:
            for b in range(RING):
                pe_block(k, At(q.g + b, RING, it), DC, h)
        for b in range(24, 26):
            pe_block(k, At(q.g + b), DC, h)

    def act(self, k, q):
        act = k.nc.scalar
        act_rstd(k, q.norm, lambda act: None)
        act.wait_ge(k.block_done, q.g)
        act.dma_start(k.waup[:, :], k.dram["waup"]).then_inc(k.up_loaded, 16)
        act.dma_start(k.gup[:, :], k.dram["gup"]).then_inc(k.up_loaded, 16)
        act.dma_start(k.lam_in[:, :], k.dram["lam"]).then_inc(k.lam_loaded, 16)
        act_prenorm(k, q.h, None, k.h_hi_buf)
        with act.Fori(0, 6) as it:
            for b in range(RING):
                act_split(k, At(q.g + b, RING, it) + LEAD)
        for b in range(24, 26):
            act_split(k, At(q.g + b) + LEAD)

    def dve(self, k, q):
        dve = k.nc.vector
        dve_prenorm(k, q.norm, q.h, k.x, k.vec(self.g_pre), None, k.h_hi_buf, k.h_lo_buf)
        with dve.Fori(0, 3) as it:
            for b in range(RING):
                g = At(q.g + b, RING, it)
                dve_split(k, g + LEAD)
                wait(dve, k.block_done, g + 1)
                dve.tensor_copy(k.qkv[:, bass.ds(At(b, RING, it).value, 1), :],
                                k.bank[g.slot][:, :].rearrange("p (o f) -> p o f", o=1)).then_inc(k.bank_free, 1)
        dve.memset(k.zst[:, :, 0:1], 0.0).then_inc(k.shifted, 1)
        dve.wait_ge(k.shifted, 1)
        mu = k.vec("mu")

        def shifted_block(g, i, dst, col):
            z = k.zst[:, i.base % 2, :].rearrange("p (o f) -> p o f", o=1)
            dve_split(k, g + LEAD)
            wait(dve, k.block_done, g + 1)
            if i.base >= 2:
                wait(dve, k.shifted, i)
            dve.tensor_copy(z[:, :, 1:], k.bank[g.slot][:, :].rearrange("p (o f) -> p o f", o=1)).then_inc(k.bank_free, 1)
            wait(dve, k.bank_free, g + 1)
            dve.tensor_tensor(dst, z[:, :, 0:T], z[:, :, 1:], ALU.subtract).then_inc(k.shift_d, 1)
            wait(dve, k.shift_d, i + 1)
            dve.scalar_tensor_tensor(dst, dst, col, z[:, :, 1:], ALU.mult, ALU.add).then_inc(k.shifted, 1)

        for b in range(RING):
            shifted_block(At(q.g + 12 + b), At(b), k.rkv[:, b:b + 1, :], mu[:, b:b + 1])
        with dve.Fori(0, 2) as it:
            for b in range(RING):
                j = At(RING + b, RING, it)
                shifted_block(At(q.g + 16 + b, RING, it), j, k.rkv[:, bass.ds(j.value, 1), :], mu[:, bass.ds(j.value, 1)])
        for n, buf in enumerate((k.wa, k.gin)):
            shifted_block(At(q.g + 24 + n), At(12 + n), buf[:, :].rearrange("p (o f) -> p o f", o=1), mu[:, 12 + n:13 + n])


class Attention(Phase):
    blocks = 0
    UNITS = [(h, b) for h in range(A_HEADS) for b in range(T // P)]

    def advance(self, q):
        q.norm += A_HEADS

    def layout(self, k, ctx):
        (k.dist_ready, k.bias_ready, k.lam_ready, k.sc_full, k.sc_biased, k.mx_ready, k.p_exp
         ) = k.sems("dist_ready bias_ready lam_ready sc_full sc_biased mx_ready p_exp")
        (k.rinv, k.p_neg, k.p_ready, k.ptr_full, k.ptr_copied, k.pv_done, k.oa_copied
         ) = k.sems("rinv p_neg p_ready ptr_full ptr_copied pv_done oa_copied")
        (k.oa_sq, k.oa_scaled, k.oa_hi, k.at_parts, k.vt_full, k.vt_copied, k.lam_exp
         ) = k.sems("oa_sq oa_scaled oa_hi at_parts vt_full vt_copied lam_exp")

    def pool(self, k, q):
        pool = k.nc.gpsimd
        pool.wait_ge(k.block_done, q.g)
        pool.iota(k.dist[:, :], pattern=[[1, T]], base=-(T - P), channel_multiplier=-1,
                  allow_small_or_imprecise_dtypes=True).then_inc(k.dist_ready, 1)

    def pe(self, k, q):
        pe = k.nc.tensor
        for n in range(T // P):
            if n >= 2:
                pe.wait_ge(k.vt_copied, n - 1)
            else:
                pe.wait_ge(k.bank_free, q.g)
            for c in range(4):
                last = pe.transpose(k.gbank[n % 2][:, c * P:(c + 1) * P], k.qkv[:, 8 + c, n * P:(n + 1) * P], k.ident[:, :])
            last.then_inc(k.vt_full, 1)
        units = self.UNITS

        def scores(u):
            h, b = units[u]
            if u >= 2:
                pe.wait_ge(k.sc_biased, 2 * (u - 1))
            for m in range(2):
                half = slice(m * BH, (m + 1) * BH)
                last = pe.matmul(k.bank[2 * (u % 2) + m][:, 0:(b + 1) * P], k.qkv[half, h, b * P:(b + 1) * P],
                                 k.qkv[half, 4 + h, 0:(b + 1) * P], start=True, stop=True)
                last.then_inc(k.sc_full, 1)

        def values(u):
            h, b = units[u]
            pe.wait_ge(k.p_ready, u + 1)
            if u >= 2:
                pe.wait_ge(k.ptr_copied, u - 1)
            else:
                pe.wait_ge(k.vt_copied, T // P)
            for j in range(b + 1):
                last = pe.transpose(k.gbank[u % 2][:, j * P:(j + 1) * P], k.pn[:, u % 2, j * P:(j + 1) * P], k.ident[:, :])
            last.then_inc(k.ptr_full, 1)

        def weigh(u):
            h, b = units[u]
            pe.wait_ge(k.ptr_copied, u + 1)
            if b == 0 and h > 0:
                pe.wait_ge(k.oa_copied, h)
            for j in range(b + 1):
                last = pe.matmul(k.cbank[:, b * P:(b + 1) * P], k.vtok_a[:, j, h * P:(h + 1) * P], k.ptr[:, u % 2, j * P:(j + 1) * P],
                                 start=(j == 0), stop=(j == b))
            last.then_inc(k.pv_done, 1)
            if b == T // P - 1:
                pe.wait_ge(k.oa_sq, h + 1)
                pe.wait_ge(k.rstd_ready, q.norm + h)
                pe.matmul(k.nbank[:, :], k.ones[:, :], k.sqa[:, h % 2, :], start=True, stop=True).then_inc(k.norm_sum, 1)

        N = len(units)
        for u in range(N + 2):
            if u < N:
                scores(u)
            if 1 <= u <= N:
                values(u - 1)
            if u >= 2:
                weigh(u - 2)

    def act(self, k, q):
        act = k.nc.scalar
        units = self.UNITS
        act.wait_ge(k.lam_ready, 2)
        act.activation(k.att_small[:, 0:2], k.att_small[:, 0:2], ACT.Exp).then_inc(k.lam_exp, 1)
        for n in range(T // P):
            act.wait_ge(k.vt_full, n + 1)
            act.activation(k.vtok_a[:, n, :], k.gbank[n % 2][:, :], ACT.Copy).then_inc(k.vt_copied, 1)

        def exps(u):
            h, b = units[u]
            for m in range(2):
                act.wait_ge(k.mx_ready, 2 * u + m + 1)
                act.activation(k.sc[:, u % 2, m, 0:(b + 1) * P], k.sc[:, u % 2, m, 0:(b + 1) * P], ACT.Exp,
                               bias=k.att_small[:, 8 + 4 * (u % 2) + m:9 + 4 * (u % 2) + m],
                               accum_out=k.att_small[:, 16 + 4 * (u % 2) + m:17 + 4 * (u % 2) + m]).then_inc(k.p_exp, 1)

        def copies(u):
            h, b = units[u]
            act.wait_ge(k.ptr_full, u + 1)
            if u >= 2:
                act.wait_ge(k.pv_done, u - 1)
            act.activation(k.ptr[:, u % 2, 0:(b + 1) * P], k.gbank[u % 2][:, 0:(b + 1) * P], ACT.Copy).then_inc(k.ptr_copied, 1)

        def head(h):
            act.wait_ge(k.oa_copied, h + 1)
            if h >= 2:
                act.wait_ge(k.norm_sum, q.norm + h - 1)
            act.activation(k.sqa[:, h % 2, :], k.oa[:, :], ACT.Square).then_inc(k.oa_sq, 1)
            act_rstd(k, q.norm + h, lambda act: wait(act, k.oa_scaled, h), scale=1.0 / P)
            act.wait_ge(k.oa_scaled, h + 1)
            act.activation(k.a_hi_buf[:, h, :], k.oa[:, :], ACT.Copy).then_inc(k.oa_hi, 1)

        N = len(units)
        for u in range(N + 2):
            if u < N:
                exps(u)
            if 1 <= u <= N:
                copies(u - 1)
            if u >= 5 and u % 4 == 1:
                head((u - 2) // 4)

    def dve(self, k, q):
        dve = k.nc.vector
        units = self.UNITS
        dve.wait_ge(k.lam_loaded, 16)
        lam = k.lam_in[:, :].rearrange("p (a b d) -> p a b d", a=2, b=2)
        prod = k.oa[:, 0:2 * BH].rearrange("p (a d) -> p a d", a=2)
        dve.wait_ge(k.block_done, q.g)
        dve.tensor_tensor(prod, lam[:, :, 0, :], lam[:, :, 1, :], ALU.mult).then_inc(k.lam_ready, 1)
        dve.wait_ge(k.lam_ready, 1)
        dve.tensor_reduce(k.att_small[:, 0:2], prod, AX.X, ALU.add).then_inc(k.lam_ready, 1)
        dve.wait_ge(k.lam_exp, 1)
        dve.tensor_tensor(k.att_small[:, 2:3], k.att_small[:, 0:1], k.att_small[:, 1:2], ALU.subtract).then_inc(k.lam_ready, 1)
        dve.wait_ge(k.lam_ready, 3)
        dve.tensor_scalar(k.att_small[:, 2:3], k.att_small[:, 2:3], LAM_INIT, None, ALU.add).then_inc(k.lam_ready, 1)
        dve.tensor_scalar(k.att_small[:, 4:5], k.vec("subln"), 1.0 - LAM_INIT, None, ALU.mult).then_inc(k.lam_ready, 1)
        dve.wait_ge(k.lam_ready, 5)
        dve.wait_ge(k.dist_ready, 1)
        dve.scalar_tensor_tensor(k.dist[:, :], k.dist[:, :], -1.0, k.dist[:, :], ALU.mult, ALU.min).then_inc(k.dist_ready, 1)
        dve.wait_ge(k.dist_ready, 2)
        dve.memset(k.dist[0:CH, T - CH:T], -1e30).then_inc(k.dist_ready, 1)
        dve.wait_ge(k.dist_ready, 3)

        def bias(u):
            h, b = units[u]
            w = (b + 1) * P
            if b == 0:
                if h > 0:
                    dve.wait_ge(k.sc_biased, 2 * u)
                dve.tensor_scalar(k.bias_h[:, :], k.dist[:, :], 2.0 ** (-8.0 / A_HEADS * (h + 1)), None, ALU.mult).then_inc(k.bias_ready, 1)
                dve.wait_ge(k.bias_ready, h + 1)
            for m in range(2):
                dve.wait_ge(k.sc_full, 2 * u + m + 1)
                if u >= 2:
                    dve.wait_ge(k.p_ready, u - 1)
                dve.scalar_tensor_tensor(k.sc[:, u % 2, m, 0:w], k.bank[2 * (u % 2) + m][:, 0:w], BH ** -0.5,
                                         k.bias_h[:, T - w:T], ALU.mult, ALU.add).then_inc(k.sc_biased, 1)
            for m in range(2):
                dve.wait_ge(k.sc_biased, 2 * u + m + 1)
                dve.tensor_reduce(k.att_small[:, 8 + 4 * (u % 2) + m:9 + 4 * (u % 2) + m], k.sc[:, u % 2, m, 0:w], AX.X, ALU.max,
                                  negate=True).then_inc(k.mx_ready, 1)

        def mix(u):
            h, b = units[u]
            w = (b + 1) * P
            s = 16 + 4 * (u % 2)
            dve.wait_ge(k.p_exp, 2 * u + 2)
            dve.reciprocal(k.att_small[:, s:s + 2], k.att_small[:, s:s + 2]).then_inc(k.rinv, 1)
            dve.wait_ge(k.rinv, 2 * u + 1)
            dve.tensor_tensor(k.att_small[:, s + 1:s + 2], k.att_small[:, s + 1:s + 2], k.att_small[:, 2:3], ALU.mult).then_inc(k.rinv, 1)
            dve.wait_ge(k.rinv, 2 * u + 2)
            dve.tensor_scalar(k.sc[:, u % 2, 1, 0:w], k.sc[:, u % 2, 1, 0:w], k.att_small[:, s + 1:s + 2], None, ALU.mult).then_inc(k.p_neg, 1)
            dve.wait_ge(k.p_neg, u + 1)
            if u >= 2:
                dve.wait_ge(k.ptr_full, u - 1)
            dve.scalar_tensor_tensor(k.pn[:, u % 2, 0:w], k.sc[:, u % 2, 0, 0:w], k.att_small[:, s:s + 1], k.sc[:, u % 2, 1, 0:w],
                                     ALU.mult, ALU.subtract).then_inc(k.p_ready, 1)

        def head(h):
            dve.wait_ge(k.pv_done, 4 * (h + 1))
            if h > 0:
                dve.wait_ge(k.at_parts, h)
            dve.tensor_copy(k.oa[:, :], k.cbank[:, :]).then_inc(k.oa_copied, 1)
            dve.wait_ge(k.rstd_ready, q.norm + h + 1)
            dve.scalar_tensor_tensor(k.oa[:, :], k.oa[:, :], k.att_small[:, 4:5], k.rstd[:, :], ALU.mult, ALU.mult).then_inc(k.oa_scaled, 1)
            dve.wait_ge(k.oa_hi, h + 1)
            dve.tensor_tensor(k.a_lo_buf[:, h, :], k.oa[:, :], k.a_hi_buf[:, h, :].bitcast(F32), ALU.subtract).then_inc(k.at_parts, 1)

        N = len(units)
        for u in range(N + 2):
            if u < N:
                bias(u)
            if 1 <= u <= N:
                mix(u - 1)
            if u >= 5 and u % 4 == 1:
                head((u - 2) // 4)


class Steps:

    def __init__(self, sem, *names):
        self.sem, self.names = sem, " ".join(names).split()

    def done(self, rep, name):
        return rep * len(self.names) + self.names.index(name) + 1


def stage(eng, steps, rep):
    at = [0]

    def do(name, ins):
        assert steps.names[at[0]] == name, (name, steps.names[at[0]])
        at[0] += 1
        ins.then_inc(steps.sem, 1)

    def after(other, name, r=None):
        r = rep if r is None else r
        if r >= 0:
            eng.wait_ge(other.sem, other.done(r, name))
    return do, after


class Rwkv(Phase):
    blocks = 0

    def advance(self, q):
        pass

    def layout(self, k, ctx):
        S = lambda name, *n: Steps(k.sem("s_" + name), *n)
        k.pp = S("pp", "w a ss bs")
        k.pa = S("pa", "sigw siga kksq ln rn epos ecol eneg")
        k.pd = S("pd", "kkr", *[f"scan{n}" for n in range(RN)], "mcol sub rho ssm am kp kkn rt at beta bt rk kt bon")
        (k.tk_full, k.tk_copied, k.rw_start, k.rho_exp, k.rw_masks, k.rw_zero
         ) = k.sems("tk_full tk_copied rw_start rho_exp rw_masks rw_zero")
        lv = range(1, len(LEVELS) + 1)
        k.cp = S("cp", "a0 a1 at0 at1 ak0 ak1 rk0 rk1 rb0 rb1", *[f"x{l}0 x{l}1 y{l}0 z{l}0 y{l}1 z{l}1" if l < len(LEVELS) else
                                                           f"x{l}0 x{l}1 z{l}0 z{l}1" for l in lv], "rhs0 rhs1 u y0 y1 p")
        k.ca = S("ca", "i0 i1 it0 it1", *[f"x{l}0 x{l}1" for l in lv], "rhs0 rhs1 y0 y1")
        k.cd = S("cd", "a0 a1 at0 it0 at1 it1 ak0 ak1 rk0 rk1 rb0 rb1", *[f"y{l}0 z{l}0 y{l}1 z{l}1" if l < len(LEVELS) else
                                                                     f"z{l}0 z{l}1" for l in lv], "u sp s")
        k.fp = S("fp", "mean var g")
        k.fa = S("fa", "sq ln rs hi")
        k.fd = S("fd", "yc yw yb yg lo")

    def pool(self, k, q):
        pool = k.nc.gpsimd
        done = Order(pool, k.rw_masks)
        def then(ins):
            done(ins)
            done.wait()
        pool.wait_ge(k.block_done, q.g)
        then(pool.memset(k.tri[:, :, :], 1))
        for i, (sign, base) in enumerate(((1, -1), (-1, -1), (-1, 0))):
            then(pool.affine_select(out=k.tri[:, i, :], in_=k.tri[:, i, :], compare_op=ALU.is_ge, fill=0.0, base=base,
                                    pattern=[[-sign, P]], channel_multiplier=sign))
        then(pool.memset(k.lvl_mask[:, :, :, :], 1))
        for l, b in enumerate([1] + LEVELS):
            m = k.lvl_mask[:, l, 0, :].rearrange("p (i two s) -> p i two s", two=2, s=b)
            mt = k.lvl_mask[:, l, 1, :].rearrange("p (i two s) -> p i two s", two=2, s=b)
            n = P // (2 * b)
            then(pool.affine_select(out=m, in_=m, compare_op=ALU.is_ge, fill=0.0, base=-b,
                                    pattern=[[-2 * b, n], [-b * 0 - 10000, 2], [0, b]], channel_multiplier=1))
            then(pool.affine_select(out=m, in_=m, compare_op=ALU.is_ge, fill=0.0, base=2 * b - 1,
                                    pattern=[[2 * b, n], [0, 2], [0, b]], channel_multiplier=-1))
            then(pool.affine_select(out=mt, in_=mt, compare_op=ALU.is_ge, fill=0.0, base=-10000,
                                    pattern=[[-2 * b, n], [10000, 2], [0, b]], channel_multiplier=1))
            then(pool.affine_select(out=mt, in_=mt, compare_op=ALU.is_ge, fill=0.0, base=b - 1,
                                    pattern=[[2 * b, n], [0, 2], [0, b]], channel_multiplier=-1))
        self.n_masks = done.n.base
        pool.wait_ge(k.pd.sem, BC * len(k.pd.names))
        pool.wait_ge(k.pa.sem, BC * len(k.pa.names))
        pool.wait_ge(k.pp.sem, BC * len(k.pp.names))
        zero = Order(pool, k.rw_zero)
        for buf in (k.mat_at, k.t_ak, k.t_rb, k.t_rk):
            zero(pool.memset(buf[:, :, :], 0.0))
            zero.wait()

    def pe(self, k, q):
        pe = k.nc.tensor
        pe.wait_ge(k.up_loaded, 32)
        pe.wait_ge(k.rw_start, 2)
        for c in range(BC):
            do, after = stage(pe, k.pp, c)
            col = slice(c * P, (c + 1) * P)
            after(k.pa, "sigw", c - 1)
            do("w", pe.matmul(k.bank[0][:, :], k.waup[0:BH, col], k.wa[0:BH, :], start=True, stop=True))
            after(k.pa, "siga", c - 1)
            do("a", pe.matmul(k.bank[1][:, :], k.waup[BH:P, col], k.wa[BH:P, :], start=True, stop=True))
            after(k.pa, "kksq")
            after(k.pd, "ssm", c - 1)
            do("ss", pe.matmul(k.bank[2][:, :], k.pair_ones[:, :], k.tmp1[:, :], start=True, stop=True))
            after(k.pd, "rk")
            after(k.pd, "bon", c - 1)
            do("bs", pe.matmul(k.bank[3][:, :], k.pair_ones[:, :], k.tmp1[:, :], start=True, stop=True))
        n = 0
        after(k.pd, "kt")
        for src in (lambda c: k.rkv[:, 2 * BC + c], lambda c: k.bt_y[:, c], lambda c: k.rkv[:, BC + c]):
            for t in range(RN):
                if n >= 2:
                    pe.wait_ge(k.tk_copied, n - 1)
                for c in range(BC):
                    last = pe.transpose(k.gbank[n % 2][:, c * P:(c + 1) * P], src(c)[:, t * RC:(t + 1) * RC], k.ident[:, :])
                last.then_inc(k.tk_full, 1)
                n += 1
        pe.wait_ge(k.tk_copied, n)
        after(k.pd, "bon")
        pe.wait_ge(k.rho_exp, 1)
        banks = k.bank + k.gbank + [k.cbank, k.nbank]
        for t in range(RN):
            self.pe_chunk(k, t, banks)
        for c in range(BC):
            do, after = stage(pe, k.fp, c)
            col = slice(c * P, (c + 1) * P)
            if c == 0:
                after(k.ca, "y1", RN - 1)
            after(k.fd, "yc", c - 1)
            do("mean", pe.matmul(k.cbank[:, :], k.pair_ones[:, :], k.bt_y[:, c, :], start=True, stop=True))
            after(k.fa, "sq")
            after(k.fa, "ln", c - 1)
            do("var", pe.matmul(k.nbank[:, :], k.pair_ones[:, :], k.tmp1[:, :], start=True, stop=True))
            after(k.fd, "yg", c - 1)
            do("g", pe.matmul(k.gbank[0][:, :], k.gup[:, col], k.gin[:, :], start=True, stop=True))

    def pe_chunk(self, k, t, banks):
        pe = k.nc.tensor
        do, after = stage(pe, k.cp, t)
        tok = slice(t * RC, (t + 1) * RC)
        ar = lambda i: (lambda c, half: k.ar[half, c, i, tok])
        b, kt = (lambda c, half: k.bt_y[half, c, tok]), (lambda c, half: k.rkv[half, BC + c, tok])
        kinds = [("a", ar(0), b), ("at", b, ar(0)), ("ak", kt, ar(0)), ("rk", kt, ar(1)), ("rb", b, ar(1))]
        for i, (name, lhs, rhs) in enumerate(kinds):
            for p in range(2):
                half = slice(p * BH, (p + 1) * BH)
                n = (2 * i + p) % 8
                if i == 0 and p == 0 and t > 0:
                    after(k.ca, "y1", t - 1)
                    after(k.cd, "u", t - 1)
                    if t - 1 < RN - 1:
                        after(k.cd, "s", t - 1)
                if i == 4:
                    after(k.cd, f"a{p}")
                for c in range(BC):
                    last = pe.matmul(banks[n][:, c * P:(c + 1) * P], lhs(c, half), rhs(c, half), start=True, stop=True)
                do(f"{name}{p}", last)
        grp = lambda buf, p, c: buf[:, p * BC + c, :]
        X, Y, Z = k.bank[0:2], k.bank[2:4], k.gbank
        for l in range(1, len(LEVELS) + 1):
            full = l < len(LEVELS)
            for p in range(2):
                if l == 1:
                    after(k.cd, f"rb{p}")
                    after(k.cd, f"a{p}")
                    after(k.cd, f"it{p}")
                else:
                    after(k.cd, f"y{l - 1}{p}")
                for c in range(BC):
                    last = pe.matmul(X[p][:, c * P:(c + 1) * P], grp(k.mat_at, p, c), grp(k.inv, p, c), start=True, stop=True)
                do(f"x{l}{p}", last)
            for p in range(2):
                after(k.ca, f"x{l}{p}")
                if l == 1:
                    after(k.cd, f"ak{p}")
                    after(k.cd, f"at{p}")
                else:
                    after(k.cd, f"z{l - 1}{p}")
                if full:
                    for c in range(BC):
                        last = pe.matmul(Y[p][:, c * P:(c + 1) * P], grp(k.inv_t, p, c), grp(k.mat_x, p, c), start=True, stop=True)
                    do(f"y{l}{p}", last)
                for c in range(BC):
                    last = pe.matmul(Z[p][:, c * P:(c + 1) * P], grp(k.mat_x, p, c), grp(k.inv_t, p, c), start=True, stop=True)
                do(f"z{l}{p}", last)
        L = len(LEVELS)
        for p in range(2):
            half = slice(p * BH, (p + 1) * BH)
            after(k.cd, f"rk{p}")
            after(k.cd, f"ak{p}")
            out = (k.cbank, k.nbank)[p]
            for c in range(BC):
                h = 2 * c + p
                o = out[:, c * BH:(c + 1) * BH]
                if t > 0:
                    pe.matmul(o, k.ar[half, c, 0, tok], k.st[half, c, :], start=True, stop=False)
                last = pe.matmul(o, grp(k.t_ak, p, c), k.vt[:, t, h * BH:(h + 1) * BH], start=(t == 0), stop=True)
            do(f"rhs{p}", last)
        after(k.cd, f"z{L}1")
        after(k.cd, f"z{L}0")
        for p in range(2):
            after(k.ca, f"rhs{p}")
            for c in range(BC):
                i = p * BC + c
                last = pe.matmul(k.gbank[0][:, i * BH:(i + 1) * BH], grp(k.inv_t, p, c), k.rhs_sb[:, i * BH:(i + 1) * BH],
                                 start=True, stop=True)
        do("u", last)
        after(k.cd, "u")
        for p in range(2):
            half = slice(p * BH, (p + 1) * BH)
            after(k.cd, f"rb{p}")
            after(k.cd, f"y{L - 1}{p}")
            for c in range(BC):
                h, i = 2 * c + p, p * BC + c
                o = Y[p][half, c * P:(c + 1) * P]
                if t > 0:
                    pe.matmul(o, k.st[half, c, :], k.ar[half, c, 1, tok], start=True, stop=False)
                pe.matmul(o, k.u_sb[:, i * BH:(i + 1) * BH], grp(k.t_rb, p, c), start=(t == 0), stop=False)
                last = pe.matmul(o, k.vt[:, t, h * BH:(h + 1) * BH], grp(k.t_rk, p, c), start=False, stop=True)
            do(f"y{p}", last)
        for p in range(2):
            half = slice(p * BH, (p + 1) * BH)
            for c in range(BC):
                h, i = 2 * c + p, p * BC + c
                o = k.gbank[1][half, c * BH:(c + 1) * BH]
                pe.matmul(o, k.btok[:, t, h * BH:(h + 1) * BH], k.u_sb[:, i * BH:(i + 1) * BH], start=True, stop=False)
                last = pe.matmul(o, k.ktokr[:, t, h * BH:(h + 1) * BH], k.vt[:, t, h * BH:(h + 1) * BH], start=False, stop=True)
        do("p", last)

    def act(self, k, q):
        act = k.nc.scalar
        act.wait_ge(k.shifted, 15)
        act.activation(k.wa[0:BH, :], k.wa[0:BH, :], ACT.Tanh).then_inc(k.rw_start, 1)
        act.activation(k.gin[:, :], k.gin[:, :], ACT.Sigmoid).then_inc(k.rw_start, 1)
        chunks = lambda b: b.rearrange("p (n c) -> p n c", n=RN)
        ep = chunks(k.e_pos[:, :])
        for c in range(BC):
            do, after = stage(act, k.pa, c)
            after(k.pp, "w")
            after(k.pd, "kkn", c - 1)
            do("sigw", act.activation(k.tmp2[:, :], k.bank[0][:, :], ACT.Sigmoid, bias=k.vec("w0")[:, c:c + 1]))
            after(k.pp, "a")
            after(k.pd, "bt", c - 1)
            do("siga", act.activation(k.ab[:, :], k.bank[1][:, :], ACT.Sigmoid, bias=k.vec("a0")[:, c:c + 1]))
            after(k.pd, "kkr")
            after(k.pp, "bs", c - 1)
            do("kksq", act.activation(k.tmp1[:, :], k.kkr[:, :], ACT.Square))
            after(k.pd, "ssm")
            do("ln", act.activation(k.tmp2[:, :], k.tmp2[:, :], ACT.Ln, scale=LN_SCALE))
            after(k.pa, "ln")
            do("rn", act.activation(k.tmp2[:, :], k.tmp2[:, :], ACT.Exp, scale=-0.5))
            after(k.pd, "rho")
            after(k.pd, "at", c - 1)
            do("epos", act.activation(ep[:, :, 1:], chunks(k.cumw[:, :]), ACT.Exp, scale=-KAPPA))
            do("ecol", act.activation(ep[:, :, 0], k.mcol[:, c, :], ACT.Exp, scale=KAPPA))
            after(k.pd, "kt", c - 1)
            do("eneg", act.activation(k.e_neg[:, :], k.cumw[:, :], ACT.Exp, scale=KAPPA))
        act.activation(k.rhos[:, 0:RN - 1, :], k.rhos[:, 0:RN - 1, :], ACT.Exp, scale=-KAPPA).then_inc(k.rho_exp, 1)
        n = 0
        for dst in (k.vt, k.btok, k.ktokr):
            for t in range(RN):
                act.wait_ge(k.tk_full, n + 1)
                act.activation(dst[:, t, :], k.gbank[n % 2][:, :], ACT.Copy).then_inc(k.tk_copied, 1)
                n += 1
        halves = lambda b, p: b[:, p * BC:(p + 1) * BC, :]
        idb = k.ident[:, :].rearrange("p (o f) -> p o f", o=1).to_broadcast([P, BC, P])
        as4 = lambda bank: bank[:, :].rearrange("p (h f) -> p h f", f=P)
        for t in range(RN):
            do, after = stage(act, k.ca, t)
            if t == 0:
                after(k.pd, "bon", BC - 1)
                after(k.pp, "bs", BC - 1)
            for p in range(2):
                after(k.cp, "x60", t - 1)
                after(k.cp, "x61", t - 1)
                do(f"i{p}", act.activation(halves(k.inv, p), idb, ACT.Copy))
            for p in range(2):
                after(k.cp, "u", t - 1)
                do(f"it{p}", act.activation(halves(k.inv_t, p), idb, ACT.Copy))
            for l in range(1, len(LEVELS) + 1):
                for p in range(2):
                    after(k.cp, f"x{l}{p}")
                    do(f"x{l}{p}", act.activation(halves(k.mat_x, p), as4(k.bank[p]), ACT.Copy))
            for p in range(2):
                after(k.cp, f"rhs{p}")
                do(f"rhs{p}", act.activation(k.rhs_sb[:, p * 256:(p + 1) * 256], (k.cbank, k.nbank)[p][:, 0:256], ACT.Copy))
            for p in range(2):
                half = slice(p * BH, (p + 1) * BH)
                after(k.cp, f"y{p}")
                do(f"y{p}", act.activation(k.bt_y[half, :, t * RC:(t + 1) * RC],
                                           k.bank[2 + p][half, :].rearrange("p (c f) -> p c f", f=RC), ACT.Copy))
        for c in range(BC):
            do, after = stage(act, k.fa, c)
            after(k.fd, "yc")
            after(k.fp, "var", c - 1)
            do("sq", act.activation(k.tmp1[:, :], k.bt_y[:, c, :], ACT.Square))
            after(k.fp, "var")
            do("ln", act.activation(k.tmp2[:, :], k.nbank[:, :], ACT.Ln, bias=k.eps2_col[:, :], scale=1.0 / BH))
            after(k.fa, "ln")
            after(k.fd, "yw", c - 1)
            do("rs", act.activation(k.kkr[:, :], k.tmp2[:, :], ACT.Exp, scale=-0.5))
            after(k.fd, "yg")
            do("hi", act.activation(k.a_hi_buf[:, BC + c, :], k.bt_y[:, c, :], ACT.Copy))

    def dve(self, k, q):
        dve = k.nc.vector
        chunks = lambda b: b.rearrange("p (n c) -> p n c", n=RN)
        ep = chunks(k.e_pos[:, :])
        vec = lambda name, c: k.vec(name)[:, c:c + 1]
        for c in range(BC):
            do, after = stage(dve, k.pd, c)
            r, kk, v = k.rkv[:, c, :], k.rkv[:, BC + c, :], k.rkv[:, 2 * BC + c, :]
            if c == 0:
                dve.wait_ge(k.shifted, 15)
            after(k.pd, "beta", c - 1)
            do("kkr", dve.tensor_scalar(k.kkr[:, :], kk, vec("k_k", c), None, ALU.mult))
            after(k.pa, "sigw")
            after(k.pa, "eneg", c - 1)
            cum, sigw = chunks(k.cumw[:, :]), chunks(k.tmp2[:, :])
            for n in range(RN):
                do(f"scan{n}", dve.tensor_tensor_scan(cum[:, n, :], k.ones[:, :], sigw[:, n, :], 0.0, ALU.mult, ALU.add))
            after(k.pd, f"scan{RN - 1}")
            do("mcol", dve.tensor_copy(k.mcol[:, c, :], cum[:, :, RC // 2 - 1]))
            after(k.pd, "mcol")
            do("sub", dve.tensor_tensor(cum, cum, k.mcol[:, c, :].rearrange("p (n o) -> p n o", o=1).to_broadcast([P, RN, RC]), ALU.subtract))
            after(k.pd, "sub")
            do("rho", dve.tensor_tensor(k.rhos[:, 0:RN - 1, c], cum[:, 0:RN - 1, RC - 1], k.mcol[:, c, 1:RN], ALU.add))
            after(k.pp, "ss")
            do("ssm", dve.tensor_scalar(k.tmp2[:, :], k.bank[2][:, :], 1e-24, None, ALU.max))
            after(k.pa, "siga")
            do("am", dve.tensor_scalar(k.tmp1[:, :], k.ab[:, :], 1.0, vec("k_a", c), ALU.subtract, ALU.mult))
            after(k.pd, "am")
            do("kp", dve.scalar_tensor_tensor(kk, k.tmp1[:, :], 1.0, kk, ALU.add, ALU.mult))
            after(k.pa, "rn")
            do("kkn", dve.scalar_tensor_tensor(k.kkr[:, :], k.kkr[:, :], LN_SCALE ** 0.5, k.tmp2[:, :], ALU.mult, ALU.mult))
            after(k.pa, "eneg")
            do("rt", dve.tensor_tensor(chunks(k.ar[:, c, 1, :]), chunks(r), ep[:, :, 1:], ALU.mult))
            after(k.pd, "kkn")
            do("at", dve.scalar_tensor_tensor(chunks(k.ar[:, c, 0, :]), chunks(k.kkr[:, :]), -1.0, ep[:, :, 0:RC], ALU.mult, ALU.mult))
            do("beta", dve.tensor_tensor(k.ab[:, :], k.ab[:, :], k.kkr[:, :], ALU.mult))
            after(k.pd, "beta")
            do("bt", dve.tensor_tensor(k.bt_y[:, c, :], k.ab[:, :], k.e_neg[:, :], ALU.mult))
            after(k.pd, "kp")
            do("rk", dve.scalar_tensor_tensor(k.tmp1[:, :], r, vec("r_k", c), kk, ALU.mult, ALU.mult))
            after(k.pd, "rk")
            do("kt", dve.tensor_tensor(kk, kk, k.e_neg[:, :], ALU.mult))
            after(k.pp, "bs")
            do("bon", dve.tensor_tensor(r, k.bank[3][:, :], v, ALU.mult))
        dve.wait_ge(k.rw_masks, self.n_masks)
        dve.wait_ge(k.rw_zero, 4)
        as4 = lambda bank: bank[:, :].rearrange("p (h f) -> p h f", f=P)
        over = lambda m: m.rearrange("p (o f) -> p o f", o=1).to_broadcast([P, BC, P])
        halves = lambda b, p: b[:, p * BC:(p + 1) * BC, :]
        banks = k.bank + k.gbank + [k.cbank, k.nbank]
        for t in range(RN):
            do, after = stage(dve, k.cd, t)
            for p in range(2):
                after(k.cp, f"a{p}")
                after(k.ca, f"i{p}")
                do(f"a{p}", dve.copy_predicated(halves(k.inv, p), over(k.lvl_mask[:, 0, 0, :]), as4(banks[p])))
            for p in range(2):
                after(k.cp, f"at{p}")
                after(k.ca, f"it{p}")
                do(f"at{p}", dve.copy_predicated(halves(k.mat_at, p), over(k.tri[:, 1, :]), as4(banks[2 + p])))
                do(f"it{p}", dve.copy_predicated(halves(k.inv_t, p), over(k.lvl_mask[:, 0, 1, :]), as4(banks[2 + p])))
            for name, buf, b, m in (("ak", k.t_ak, 4, 1), ("rk", k.t_rk, 6, 2), ("rb", k.t_rb, 0, 2)):
                for p in range(2):
                    after(k.cp, f"{name}{p}")
                    do(f"{name}{p}", dve.copy_predicated(halves(buf, p), over(k.tri[:, m, :]), as4(banks[b + p])))
            for l in range(1, len(LEVELS) + 1):
                for p in range(2):
                    if l < len(LEVELS):
                        after(k.cp, f"y{l}{p}")
                        do(f"y{l}{p}", dve.copy_predicated(halves(k.inv, p), over(k.lvl_mask[:, l, 0, :]), as4(k.bank[2 + p])))
                    after(k.cp, f"z{l}{p}")
                    do(f"z{l}{p}", dve.copy_predicated(halves(k.inv_t, p), over(k.lvl_mask[:, l, 1, :]), as4(k.gbank[p])))
            after(k.cp, "u")
            do("u", dve.tensor_copy(k.u_sb[:, :], k.gbank[0][:, :]))
            after(k.cp, "p")
            P4 = k.gbank[1][:, 0:BC * BH].rearrange("p (c f) -> p c f", f=BH)
            if t == 0:
                do("sp", dve.tensor_copy(k.st2[:, :, :], P4))
            else:
                do("sp", dve.tensor_tensor(k.st2[:, :, :], P4, k.st[:, :, :], ALU.add))
            after(k.cd, "sp")
            n = min(t, RN - 2)
            do("s", dve.tensor_tensor(k.st[:, :, :], k.st2[:, :, :],
                                      k.rhos[:, n, :].rearrange("p (c o) -> p c o", o=1).to_broadcast([P, BC, BH]), ALU.mult))
        for c in range(BC):
            do, after = stage(dve, k.fd, c)
            y = k.bt_y[:, c, :]
            after(k.fp, "mean")
            do("yc", dve.scalar_tensor_tensor(y, k.cbank[:, :], -1.0 / BH, y, ALU.mult, ALU.add))
            after(k.fa, "rs")
            do("yw", dve.scalar_tensor_tensor(y, y, vec("ln_w", c), k.kkr[:, :], ALU.mult, ALU.mult))
            after(k.fd, "yw")
            do("yb", dve.scalar_tensor_tensor(y, y, vec("ln_b", c), k.rkv[:, c, :], ALU.add, ALU.add))
            after(k.fp, "g")
            after(k.fd, "yb")
            do("yg", dve.tensor_tensor(y, y, k.gbank[0][:, :], ALU.mult))
            after(k.fa, "hi")
            do("lo", dve.tensor_tensor(k.a_lo_buf[:, BC + c, :], y, k.a_hi_buf[:, BC + c, :].bitcast(F32), ALU.subtract))


class MixerOutput(Phase):

    def __init__(self, g_post, passes=1):
        self.g_post, self.blocks = g_post, DC * passes

    def advance(self, q):
        q.g += self.blocks
        q.sq += 2 * DC
        q.norm += 1
        q.xc += DC
        q.y += DC

    def pe(self, k, q):
        pe = k.nc.tensor
        self.ready(pe, k, q)
        y = lambda t: (k.a_hi_buf[:, t, :], k.a_lo_buf[:, t, :])
        with pe.Fori(0, 2) as it:
            for b in range(RING):
                pe_block(k, At(q.g + b, RING, it), DC, y)
        pe_norm(k, q.norm, q.sq + DC)

    def ready(self, eng, k, q):
        eng.wait_ge(k.at_parts, A_HEADS)
        eng.wait_ge(k.fd.sem, BC * len(k.fd.names))

    def act(self, k, q):
        self.ready(k.nc.scalar, k, q)
        act_down(k, q.g, q.sq)
        act_rstd(k, q.norm, lambda act: None)
        act_residual(k, q.xc, q.sq + DC)

    def dve(self, k, q):
        self.ready(k.nc.vector, k, q)
        dve_down(k, q.g, add=False, sq0=q.sq)
        dve_residual(k, q.norm, q.xc, q.y, q.sq + DC, k.vec(self.g_post))


C_HEADS = 4
C_QK = D // C_HEADS
C_V = 2 * C_QK
QT, VT = C_QK // P, C_V // P
ODD_BLOCKS = 2 * QT + 2 * VT
KEY_BLOCKS = T // P


class Odd(Phase):
    FIRST_OUT = 3 * ODD_BLOCKS
    LAST_HEAD = FIRST_OUT + DC
    SECOND_OUT = LAST_HEAD + ODD_BLOCKS
    blocks = SECOND_OUT + DC

    def __init__(self, g_pre, g_post):
        self.g_pre, self.g_post = g_pre, g_post

    def advance(self, q):
        q.g += self.blocks
        q.norm += 2 + C_HEADS
        q.h += DC
        q.sq += 2 * DC
        q.xc += DC
        q.y += DC

    def layout(self, k, ctx):
        at = k.arena["sq"][0]
        def put(name, shape):
            nonlocal at
            t = k.sb(name, shape, F32, at=at)
            at += int(np.prod(shape[1:])) * 4
            assert at <= k.limit, (name, at, k.limit)
            return t
        k.r_scores = put("r_scores", [P, sum(T - P * s for s in range(KEY_BLOCKS))])
        k.r_dist = put("r_dist", [P, T])
        k.r_decay = put("r_decay", [P, T])
        k.r_sq = put("r_sq", [P, 2, T])
        k.r_v = put("r_v", [P, VT, T])
        k.r_qk = put("r_qk", [P, 2 * QT, T])
        k.r_gate = put("r_gate", [P, VT, T])
        k.r_vtok = put("r_vtok", [P, KEY_BLOCKS, C_V])
        k.r_y = put("r_y", [P, VT, T])
        (k.r_dist_ready, k.r_decay_ready, k.r_vt_full, k.r_vt_copied, k.r_sc_full, k.r_weighed, k.r_y_full
         ) = k.sems("r_dist_ready r_decay_ready r_vt_full r_vt_copied r_sc_full r_weighed r_y_full")
        (k.r_squared, k.r_added, k.r_gated, k.r_scaled, k.r_high, k.r_parts, k.r_silu
         ) = k.sems("r_squared r_added r_gated r_scaled r_high r_parts r_silu")

    def g0(self, q, h):
        return q.g + (h * ODD_BLOCKS if h < 3 else self.LAST_HEAD)

    STEPS = [(0, None), (1, 0), (2, 1), "out", (3, 2), (None, 3), "out"]

    @staticmethod
    def score_cols(s):
        at = sum(T - P * i for i in range(s))
        return slice(at, at + T - P * s)

    def pool(self, k, q):
        pool = k.nc.gpsimd
        pool.wait_ge(k.a_ready, q.a)
        pool.iota(k.r_dist[:, :], pattern=[[1, T]], base=0, channel_multiplier=-1,
                  allow_small_or_imprecise_dtypes=True).then_inc(k.r_dist_ready, 1)

    def pe(self, k, q):
        pe = k.nc.tensor
        pe_norm(k, q.norm, q.sq)
        pe.wait_ge(k.h_ready, q.h + DC)
        n_out = 0
        for step in self.STEPS:
            if step == "out":
                pe.wait_ge(k.r_parts, 2 * VT * (n_out + 1))
                y = lambda t: (k.a_hi_buf[:, t, :], k.a_lo_buf[:, t, :])
                with pe.Fori(0, DC // RING) as it:
                    for b in range(RING):
                        pe_block(k, At(q.g + (self.FIRST_OUT, self.SECOND_OUT)[n_out] + b, RING, it), DC, y)
                n_out += 1
            else:
                self.pe_step(k, q, *step)
        pe_norm(k, q.norm + 1 + C_HEADS, q.sq + DC)

    def pe_step(self, k, q, h, e):
        pe = k.nc.tensor
        hh = lambda t: (k.h_hi_buf[:, t, :], k.h_lo_buf[:, t, :])
        def blocks(lo, hi):
            if h is not None:
                for b in range(lo, hi):
                    pe_block(k, At(self.g0(q, h) + b), DC, hh)
        if e is not None:
            pe.wait_ge(k.bank_free, self.g0(q, e) + 2 * QT + VT)
            for n in range(KEY_BLOCKS):
                if n >= 2:
                    pe.wait_ge(k.r_vt_copied, KEY_BLOCKS * e + n - 1)
                elif e > 0:
                    pe.wait_ge(k.r_gated, VT * e)
                else:
                    pe.wait_ge(k.rstd_ready, q.norm + 1)
                for c in range(VT):
                    last = pe.transpose(k.gbank[n % 2][:, c * P:(c + 1) * P], k.r_v[:, c, n * P:(n + 1) * P], k.ident[:, :])
                last.then_inc(k.r_vt_full, 1)
            for s in range(KEY_BLOCKS):
                out = self.banks(k)[s][:, 0:T - P * s]
                if s == 1:
                    pe.wait_ge(k.rstd_ready, q.norm + 1 + e)
                if s >= 2:
                    pe.wait_ge(k.r_vt_copied, KEY_BLOCKS * e + s + 1)
                for c in range(QT):
                    last = pe.matmul(out, k.r_qk[:, QT + c, s * P:(s + 1) * P], k.r_qk[:, c, s * P:T],
                                     start=(c == 0), stop=(c == QT - 1))
                last.then_inc(k.r_sc_full, 1)
        blocks(0, VT)
        if e is not None:
            pe.wait_ge(k.r_weighed, KEY_BLOCKS * (e + 1))
            pe.wait_ge(k.r_vt_copied, KEY_BLOCKS * (e + 1))
            for j in range(VT):
                bank = self.banks(k)[j]
                for s in range(KEY_BLOCKS):
                    last = pe.matmul(bank[:, s * P:T], k.r_vtok[:, s, j * P:(j + 1) * P], k.r_scores[:, self.score_cols(s)],
                                     start=(s == 0), stop=(s == KEY_BLOCKS - 1))
                last.then_inc(k.r_y_full, 1)
        blocks(VT, VT + 2 * QT - 1)
        if e is not None:
            pe.wait_ge(k.r_added, VT * (e + 1))
            pe.wait_ge(k.r_gated, VT * (e + 1))
            pe.matmul(k.nbank[:, :], k.ones[:, :], k.ssq[:, :], start=True, stop=True).then_inc(k.norm_sum, 1)
        blocks(VT + 2 * QT - 1, ODD_BLOCKS)

    @staticmethod
    def banks(k):
        return [k.cbank, k.nbank, k.gbank[0], k.gbank[1]]

    def act(self, k, q):
        act = k.nc.scalar
        act_rstd(k, q.norm, lambda act: None)
        act_prenorm(k, q.h, None, k.h_hi_buf)
        n_out = 0
        for step in self.STEPS:
            if step == "out":
                last = n_out == 1
                act_down(k, q.g + (self.FIRST_OUT, self.SECOND_OUT)[n_out], q.sq if last else None)
                n_out += 1
            else:
                self.act_step(k, q, *step)
        act_rstd(k, q.norm + 1 + C_HEADS, lambda act: None)
        act_residual(k, q.xc, q.sq + DC)

    def act_step(self, k, q, h, e):
        act = k.nc.scalar
        def splits(lo, hi):
            if h is not None:
                for b in range(lo, hi):
                    act_split(k, At(self.g0(q, h) + b + LEAD))
        if e is not None:
            if e == 0:
                act.wait_ge(k.r_dist_ready, 3)
                act.wait_ge(k.h_ready, q.h + DC)
            else:
                act.wait_ge(k.r_weighed, KEY_BLOCKS * e)
            act.activation(k.r_decay[:, :], k.r_dist[:, :], ACT.Exp, scale=-math.log(1.0 - 2.0 ** (-5.0 - e))
                           ).then_inc(k.r_decay_ready, 1)
            for n in range(KEY_BLOCKS):
                act.wait_ge(k.r_vt_full, KEY_BLOCKS * e + n + 1)
                if n == 0 and e > 0:
                    act.wait_ge(k.r_y_full, VT * e)
                act.activation(k.r_vtok[:, n, :], k.gbank[n % 2][:, :], ACT.Copy).then_inc(k.r_vt_copied, 1)
        splits(0, VT)
        if e is not None:
            for j in range(VT):
                act.wait_ge(k.r_y_full, VT * e + j + 1)
                if VT * e + j >= 2:
                    act.wait_ge(k.r_added, VT * e + j - 1)
                act.activation(k.r_sq[:, j % 2, :], self.banks(k)[j][:, :], ACT.Square).then_inc(k.r_squared, 1)
        splits(VT, VT + 2 * QT)
        if e is not None:
            act_rstd(k, q.norm + 1 + e, lambda act: wait(act, k.r_scaled, VT * e), scale=1.0 / C_V)
            if e == 2:
                act.wait_ge(k.block_done, q.g + self.LAST_HEAD)
            for j in range(VT):
                act.wait_ge(k.r_scaled, VT * e + j + 1)
                act.activation(k.a_hi_buf[:, VT * (e % 2) + j, :], k.r_y[:, j, :], ACT.Copy).then_inc(k.r_high, 1)
        if h is not None:
            if e is not None:
                act.wait_ge(k.r_gated, VT * (e + 1))
            for j in range(VT):
                g = self.g0(q, h) + VT + 2 * QT + j
                act_split(k, At(g + LEAD))
                act.wait_ge(k.block_done, g + 1)
                act.wait_ge(k.bank_free, g)
                act.activation(k.r_gate[:, j, :], k.bank[g % RING][:, :], ACT.Silu).then_inc(k.bank_free, 1)

    def dve(self, k, q):
        dve = k.nc.vector
        dve_prenorm(k, q.norm, q.h, k.x, k.vec(self.g_pre), None, k.h_hi_buf, k.h_lo_buf)
        dve.wait_ge(k.r_dist_ready, 1)
        dve.scalar_tensor_tensor(k.r_dist[:, :], k.r_dist[:, :], -1.0, k.r_dist[:, :], ALU.mult, ALU.min).then_inc(k.r_dist_ready, 1)
        dve.wait_ge(k.r_dist_ready, 2)
        dve.memset(k.r_dist[CH:P, 0:CH], -1e30).then_inc(k.r_dist_ready, 1)
        n_out = 0
        for step in self.STEPS:
            if step == "out":
                last = n_out == 1
                dve.wait_ge(k.bank_free, q.g + (self.FIRST_OUT, self.SECOND_OUT)[n_out])
                dve_down(k, q.g + (self.FIRST_OUT, self.SECOND_OUT)[n_out], add=last, sq0=q.sq if last else None)
                n_out += 1
            else:
                self.dve_step(k, q, *step)
        dve_residual(k, q.norm + 1 + C_HEADS, q.xc, q.y, q.sq + DC, k.vec(self.g_post))

    def dve_step(self, k, q, h, e):
        dve = k.nc.vector
        def staged(b):
            if h is None:
                return
            g = self.g0(q, h) + b
            dve.wait_ge(k.block_done, g + 1)
            dve.wait_ge(k.bank_free, g)
            dst = k.r_v[:, b, :] if b < VT else k.r_qk[:, b - VT, :]
            dve.tensor_copy(dst, k.bank[g % RING][:, :]).then_inc(k.bank_free, 1)
        def split(b):
            if h is not None:
                dve_split(k, At(self.g0(q, h) + b + LEAD))
        if e is not None:
            dve.wait_ge(k.r_decay_ready, e + 1)
            for s in range(KEY_BLOCKS):
                dve.wait_ge(k.r_sc_full, KEY_BLOCKS * e + s + 1)
                if s == 0 and e > 0:
                    dve.wait_ge(k.r_y_full, VT * e)
                n = T - P * s
                dve.scalar_tensor_tensor(k.r_scores[:, self.score_cols(s)], self.banks(k)[s][:, 0:n], C_QK ** -0.5,
                                         k.r_decay[:, 0:n], ALU.mult, ALU.mult).then_inc(k.r_weighed, 1)
            if h is not None:
                dve.wait_ge(k.r_vt_full, KEY_BLOCKS * (e + 1))
        for b in range(VT):
            split(b)
            staged(b)
        if e is not None:
            for j in range(VT):
                n = VT * e + j
                dve.wait_ge(k.r_squared, n + 1)
                if j == 0:
                    dve.wait_ge(k.rstd_ready, q.norm + 1 + e)
                    dve.tensor_copy(k.ssq[:, :], k.r_sq[:, 0, :]).then_inc(k.r_added, 1)
                else:
                    dve.wait_ge(k.r_added, n)
                    dve.tensor_tensor(k.ssq[:, :], k.ssq[:, :], k.r_sq[:, j % 2, :], ALU.add).then_inc(k.r_added, 1)
                if j == 0 and e > 0:
                    dve.wait_ge(k.r_parts, VT * e)
                dve.tensor_tensor(k.r_y[:, j, :], self.banks(k)[j][:, :], k.r_gate[:, j, :], ALU.mult).then_inc(k.r_gated, 1)
        for b in range(VT, VT + 2 * QT):
            split(b)
            if b < VT + 2 * QT - 1:
                staged(b)
        if e is not None:
            dve.wait_ge(k.rstd_ready, q.norm + 2 + e)
            for j in range(VT + 1):
                if j < VT:
                    dve.wait_ge(k.r_gated, VT * e + j + 1)
                    dve.tensor_tensor(k.r_y[:, j, :], k.r_y[:, j, :], k.rstd[:, :], ALU.mult).then_inc(k.r_scaled, 1)
                if j >= 1:
                    i = j - 1
                    slot = VT * (e % 2) + i
                    dve.wait_ge(k.r_high, VT * e + i + 1)
                    dve.tensor_tensor(k.a_lo_buf[:, slot, :], k.r_y[:, i, :], k.a_hi_buf[:, slot, :].bitcast(F32), ALU.subtract
                                      ).then_inc(k.r_parts, 1)
        staged(VT + 2 * QT - 1)
        for b in range(VT + 2 * QT, ODD_BLOCKS):
            split(b)


class Kernel:
    ROUTE_STEPS = 36


def build(nc, W, vecs, small, xT, out, phases):
    k = Kernel()
    k.nc, k.W = nc, W
    k.n_blocks = W.shape[0]
    with ExitStack() as ctx:
        base = -(-nc.sbuf_base // 64) * 64
        arena = {}

        def sb(name, shape, dt=F32, at=None):
            size = int(np.prod(shape[1:])) * (1 if dt == I8 else 4)
            t = nc.alloc_sbuf_tensor_at(name, shape, dt, offset=base + at)
            arena[name] = (at, at + size)
            return t
        k.sb = sb
        KB = 1024
        at = 0
        def bump(name, shape, dt=F32):
            nonlocal at
            size = int(np.prod(shape[1:])) * (1 if dt == I8 else 4)
            t = sb(name, shape, dt, at=at)
            at += -(-size // 64) * 64
            return t
        k.raw = bump("raw", [P, RING, D])
        k.whi = bump("whi", [P, RING, D], F32R)
        k.wlo = bump("wlo", [P, RING, D], F32R)
        k.h_hi_buf = bump("h_hi_buf", [P, DC, T], F32R)
        k.h_lo_buf = bump("h_lo_buf", [P, DC, T], F32R)
        k.a_hi_buf = bump("a_hi_buf", [P, DC, T], F32R)
        k.a_lo_buf = bump("a_lo_buf", [P, DC, T], F32R)
        k.ssq = bump("ssq", [P, T])
        k.lnv = bump("lnv", [P, T])
        k.rstd = bump("rstd", [P, T])
        k.ones = bump("ones", [P, P])
        k.ident = bump("ident", [P, P])
        k.eps_col = bump("eps_col", [P, 1])
        k.vecs = bump("vecs_sb", [P, VEC_COLS])
        k.pair_ones = bump("pair_ones", [P, P])
        k.eps2_col = bump("eps2_col", [P, 1])
        k.c_in = bump("c_in", [P, DC, 2])
        k.c32 = bump("c32", [P, DC, 2])
        k.c_hi = bump("c_hi", [P, DC, 2], F32R)
        k.c_lo = bump("c_lo", [P, DC, 2], F32R)
        k.mod = bump("mod", [P, 6 * DC, 2])
        k.gain1 = bump("gain1", [P, 2, DC])
        k.shift1 = bump("shift1", [P, 2, DC])
        k.gain2 = bump("gain2", [P, DC])
        k.shift2 = bump("shift2", [P, DC])
        k.low = at
        k.x = bump("x", [P, DC, T])
        k.acc = bump("acc", [P, DC, T])
        k.sq = bump("sq", [P, 2, T])
        k.sil = bump("sil", [P, 2, T])
        k.a32 = bump("a32", [P, 2, T])
        k.h32 = sb("h32", [P, 2, T], at=arena["a32"][0])
        k.top = at
        k.sq0, k.h320 = k.sq, k.h32
        k.limit = nc.sbuf_usable_end - base
        k.arena = arena

        def ps(name, shape):
            return ctx.enter_context(nc.psum_tensor(name, shape, F32))
        k.bank = [ps(f"bank{i}", [P, T]) for i in range(RING)]
        k.nbank = ps("nbank", [P, T])

        def sem(name):
            return ctx.enter_context(nc.semaphore(name))
        k.sem = sem
        k.sems = lambda names: [sem(n) for n in names.split()]
        k.raw_landed = [sem(f"raw_landed{i}") for i in range(RING)]
        (k.split_hi, k.split_lo, k.block_done, k.bank_free, k.sq_ready, k.ssq_added, k.norm_sum
         ) = k.sems("split_hi split_lo block_done bank_free sq_ready ssq_added norm_sum")
        (k.ln_ready, k.rstd_ready, k.h_hi, k.h_made, k.h_ready, k.x_ready, k.y_scaled
         ) = k.sems("ln_ready rstd_ready h_hi h_made h_ready x_ready y_scaled")
        (k.a_ready, k.a_hi, k.silu_ready, k.ssq_clear, k.x_loaded, k.small_loaded, k.c_ready
         ) = k.sems("a_ready a_hi silu_ready ssq_clear x_loaded small_loaded c_ready")
        k.const_ready, k.gains_halved, k.stored = k.sems("const_ready gains_halved stored")
        k.vec = lambda name: k.vecs[:, VEC_AT[name]:VEC_AT[name] + VEC_WIDTH[name]]
        k.n_clear = 0
        k.dram = small
        k.xT = xT
        k.gbank = [ps(f"gbank{i}", [P, T]) for i in range(2)]
        k.cbank = ps("cbank", [P, T])
        for ph in phases:
            ph.layout(k, ctx)
        block = ctx.enter_context(nc.Block())

        @block.sync
        def _(sp):
            sp_stream(k, k.n_blocks)
            q = Counts()
            for ph in phases:
                ph.advance(q)
            for c in range(DC):
                sp.wait_ge(k.x_ready, q.xc - DC + c + 1)
                sp.dma_start(out[:, c, :], k.x[:, c, :]).then_inc(k.stored, 16)
            sp.wait_ge(k.stored, 16 * DC)

        @block.scalar
        def _(act):
            act.dma_start(k.c_in[:, :, :], small["c"]).then_inc(k.small_loaded, 16)
            act.dma_start(k.vecs[:, :], vecs).then_inc(k.small_loaded, 16)
            act.dma_start(k.xc1[:, :, :], small["xc"]).then_inc(k.x_loaded, 16)
            act.dma_start(k.x1[:, :, :], xT).then_inc(k.x_loaded, 16)
            act.wait_ge(k.const_ready, 8)
            q = Counts()
            for ph in phases:
                ph.act(k, q)
                ph.advance(q)

        @block.gpsimd
        def _(pool):
            pool.memset(k.ones[:, :], 1.0).then_inc(k.const_ready, 1)
            pool.memset(k.eps_col[:, :], EPS).then_inc(k.const_ready, 1)
            pool.memset(k.ident[:, :], 0.0).then_inc(k.const_ready, 1)
            pool.wait_ge(k.const_ready, 3)
            pool.affine_select(out=k.ident[:, :], in_=k.ident[:, :], compare_op=ALU.not_equal, fill=1.0,
                               base=0, pattern=[[-1, P]], channel_multiplier=1).then_inc(k.const_ready, 1)
            pool.memset(k.pair_ones[:, :], 0.0).then_inc(k.const_ready, 1)
            pool.wait_ge(k.const_ready, 5)
            for half in (slice(0, P // 2), slice(P // 2, P)):
                pool.memset(k.pair_ones[half, half], 1.0).then_inc(k.const_ready, 1)
            pool.wait_ge(k.const_ready, 7)
            pool.memset(k.eps2_col[:, :], 64e-5).then_inc(k.const_ready, 1)
            q = Counts()
            for ph in phases:
                ph.pool(k, q)
                ph.advance(q)

        @block.vector
        def _(dve):
            dve.wait_ge(k.const_ready, 8)
            dve.wait_ge(k.small_loaded, 32)
            for n, name in enumerate(HALVED):
                dve.tensor_scalar(k.vec(name), k.vec(name), 0.5, None, ALU.mult).then_inc(k.gains_halved, 1)
                dve.wait_ge(k.gains_halved, n + 1)
            q = Counts()
            for ph in phases:
                ph.dve(k, q)
                ph.advance(q)

        @block.tensor
        def _(pe):
            pe.wait_ge(k.const_ready, 8)
            q = Counts()
            for ph in phases:
                ph.pe(k, q)
                ph.advance(q)

def stages():
    return [Mod(), HgrnInput(), Hgrn(), HgrnOutput(), MoeInput(), Moe(), Renorm(),
            Ffn("norm_0_0", "norm_0_1"), EvenProj("norm_0_2"), Attention(), Rwkv(), MixerOutput("norm_0_3"), Ffn("norm_0_4", "norm_0_5"),
            Ffn("norm_1_0", "norm_1_1"), Odd("norm_1_2", "norm_1_3"), Ffn("norm_1_4", "norm_1_5", last=True)]


def pack(w):
    K, N = w.shape
    b = np.zeros((N // P, P, DC, P), w.dtype)
    b[:, :, :K // P] = w.reshape(K // P, P, N // P, P).transpose(2, 1, 0, 3)
    return b.reshape(N // P, P, D)


def ffn_blocks(wgu, wd):
    gate, up = pack(wgu[:, :D_FF]), pack(wgu[:, D_FF:])
    out, f = [], 0
    for nk in FF_SEGMENTS:
        gu = np.stack([gate[f:f + nk], up[f:f + nk]], 1).reshape(2 * nk, P, D)
        out += [gu, pack(wd[f * P:(f + nk) * P])]
        f += nk
    return out


def cols(v):
    return v.reshape(-1, P).T


def moe_blocks(wg, wu, wd):
    out = []
    for n in range(N_EXPERTS // 4):
        for e in range(4 * n, 4 * n + 4):
            g, u = pack(wg[e]), pack(wu[e])
            out.append(np.stack([g, u], 1).reshape(4, P, D))
        out.append(pack(wd[4 * n:4 * n + 4].reshape(4 * D_EXPERT, D)))
    return out


def odd_blocks(w_in, w_out):
    p = pack(w_in)
    nq, nv = C_HEADS * QT, C_HEADS * VT
    head = lambda h: np.concatenate([p[2 * nq + h * VT:2 * nq + (h + 1) * VT], p[h * QT:(h + 1) * QT],
                                     p[nq + h * QT:nq + (h + 1) * QT], p[2 * nq + nv + h * VT:2 * nq + nv + (h + 1) * VT]])
    return [head(0), head(1), head(2), pack(w_out[:D]), head(3), pack(w_out[D:])]


def token_cols(x):
    return x.T.reshape(DC, P, -1).transpose(1, 0, 2)


def weight_blocks(i):
    mod, hg, hg_out = pack(i["w_mod"][0]), pack(i["hg_w_in"][0]), pack(i["hg_w_out"][0])
    out = [mod[:2 * DC]]
    for h in range(HEADS):
        q, v, zf, zb, g = (hg[n * HEADS + h:n * HEADS + h + 1] for n in range(5))
        out += [zf, zb, q, v, g, mod[2 * DC + 3 * h:2 * DC + 3 * h + 3]]
    for c in range(DC):
        out += [hg_out[c:c + 1], mod[5 * DC + c:5 * DC + c + 1]]
    out += moe_blocks(i["moe_w_gate"][0], i["moe_w_up"][0], i["moe_w_down"][0])
    wgu, wd = i["ffn_wgu_2"], i["ffn_wd_2"]
    out += ffn_blocks(wgu[0, 0], wd[0, 0])
    out += [pack(i["even_w_in_2"][0]), pack(i["even_w_out_2"][0])]
    out += ffn_blocks(wgu[0, 1], wd[0, 1]) + ffn_blocks(wgu[1, 0], wd[1, 0])
    out += odd_blocks(i["odd_w_in_2"][0], i["odd_w_out_2"][0])
    out += ffn_blocks(wgu[1, 1], wd[1, 1])
    return np.concatenate(out)


def kernel(**inputs):
    import concourse.bacc as _bacc
    from concourse.bass_utils import run_bass_kernel_spmd as _run

    i = {name: np.asarray(a) for name, a in inputs.items()}
    wide = lambda v: np.broadcast_to(v.reshape(1, -1), (P, v.size))
    two = lambda v: np.concatenate([cols(v[0]), cols(v[1])], 1)
    vec = {"b_mod": cols(i["b_mod"][0]), "norm1_g": cols(i["norm1_g"][0]), "norm2_g": cols(i["norm2_g"][0]),
           "gnorm": cols(i["hg_gnorm"][0]), "lb_f": two(i["hg_lb_fwd"]), "lb_b": two(i["hg_lb_bwd"]),
           "final_g": cols(i["final_g"]), "router_b": wide(i["router_b"]),
           "mu": cols(i["rwkv_mu_2"][0]), "subln": cols(i["diff_subln_2"][0])}
    for b in range(2):
        for n in range(6):
            vec[f"norm_{b}_{n}"] = cols(i["norms_2"][b, n])
    for n, name in enumerate(RWKV_VECS):
        vec[name] = cols(i["rwkv_vec_2"][0, n])
    arrays = {"w": weight_blocks(i), "vecs": np.concatenate([vec[name] for name in VEC_WIDTH], 1),
              "x": token_cols(i["x"][0]), "xc": token_cols(i["ctx"][0]),
              "c": np.stack([cols(i["c"][0]), cols(i["c_ctx"])], -1),
              "rw": i["router_w"].reshape(DC, P, N_EXPERTS).transpose(1, 0, 2),
              "waup": np.concatenate([i["rwkv_w_up_2"][0], i["rwkv_a_up_2"][0]]), "gup": i["rwkv_g_up_2"][0],
              "lam": wide(i["diff_lam_2"][0])}
    nc = _bacc.Bacc("TRN2", target_bir_lowering=False, num_devices=1)
    arrays = {f"in_{name}": np.ascontiguousarray(a) for name, a in arrays.items()}
    dram = {name[3:]: nc.dram_tensor(name, a.shape, mybir.dt.from_np(a.dtype), kind="ExternalInput").ap()
            for name, a in arrays.items()}
    out = nc.dram_tensor("out", (P, DC, T), F32, kind="ExternalOutput").ap()
    build(nc, dram["w"], dram["vecs"], dram, dram["x"], out, stages())
    y = _run(nc, [arrays], core_ids=[0]).results[0]["out"]
    return y.transpose(1, 0, 2).reshape(D, T).T.reshape(1, T, D)
```

```python
from contextlib import ExitStack
import math
import numpy as np
import concourse.bass as bass
from concourse import mybir

F32 = mybir.dt.float32
F32R = mybir.dt.float32r
I8 = mybir.dt.int8
ACT = mybir.ActivationFunctionType
ALU = mybir.AluOpType
AX = mybir.AxisListType

P = 128
D = 1024
DC = D // P
T = 512
TC = 256
EPS = 1e-6
RING = 4
LEAD = 2
D_FF = 2816
FF_SEGMENTS = (8, 8, 6)
assert sum(FF_SEGMENTS) * P == D_FF


class At:

    def __init__(self, base, mult=0, reg=None):
        self.base, self.mult, self.reg = base, mult, reg

    def __add__(self, n):
        return At(self.base + n, self.mult, self.reg)

    def __sub__(self, n):
        return At(self.base - n, self.mult, self.reg)

    def times(self, k):
        return At(self.base * k, self.mult * k, self.reg)

    @property
    def value(self):
        return self.base if self.reg is None or self.mult == 0 else self.reg * self.mult + self.base

    @property
    def slot(self):
        assert self.mult % RING == 0
        return self.base % RING

    @property
    def turn(self):
        assert self.mult % RING == 0
        return At(self.base // RING, self.mult // RING, self.reg)


def wait(eng, sem, at):
    if isinstance(at, At):
        if at.base <= 0:
            assert at.reg is None or at.mult == 0, "peel this iteration"
            return
        eng.wait_ge(sem, at.value)
    elif at > 0:
        eng.wait_ge(sem, at)


class Order:

    def __init__(self, eng, sem):
        self.eng, self.sem, self.n = eng, sem, At(0)

    def __call__(self, ins):
        ins.then_inc(self.sem, 1)
        self.n = self.n + 1
        return self.n

    def wait(self, at=None):
        wait(self.eng, self.sem, self.n if at is None else at)

    def enter(self, reg, per):
        self.outer = self.n
        self.per = per
        self.n = At(self.outer.base, per, reg)

    def leave(self, trips):
        assert self.n.base - self.outer.base == self.per, (self.n.base - self.outer.base, self.per)
        self.n = At(self.outer.base + trips * self.per)


class Phase:
    blocks = 0

    def layout(self, k, ctx):
        pass

    def advance(self, q):
        pass

    def pool(self, k, q):
        pass


BLOCK_NORMS = [f"norm_{i}_{n}" for i in range(2) for n in range(6)]
RWKV_VECS = "w0 a0 k_k k_a r_k ln_w ln_b".split()
VEC_WIDTH = {"b_mod": 6 * DC, "norm1_g": DC, "norm2_g": DC, "gnorm": 1, "lb_f": 2 * DC, "lb_b": 2 * DC, "final_g": DC,
             "router_b": 16, **{n: DC for n in BLOCK_NORMS}, "mu": 14, "subln": 1, **{n: 4 for n in RWKV_VECS}}
VEC_AT, VEC_COLS = {}, 0
for _name, _width in VEC_WIDTH.items():
    VEC_AT[_name], VEC_COLS = VEC_COLS, VEC_COLS + _width
HALVED = ["norm_0_1", "norm_0_5", "norm_1_1", "norm_1_5"]


def sp_stream(k, n_blocks):
    sp = k.nc.sync
    for g in range(RING):
        sp.dma_start(k.raw[:, g, :], k.W[g]).then_inc(k.raw_landed[g], 16)
    rest = n_blocks - RING
    with sp.Fori(0, rest // RING) as it:
        for b in range(RING):
            g = At(RING + b, RING, it)
            wait(sp, k.split_lo, g - (RING - 1))
            sp.dma_start(k.raw[:, g.slot, :], k.W[bass.ds(g.value, 1)].rearrange("o p f -> p (o f)")
                         ).then_inc(k.raw_landed[g.slot], 16)
    for g in range(n_blocks - rest % RING, n_blocks):
        wait(sp, k.split_lo, g - (RING - 1))
        sp.dma_start(k.raw[:, g % RING, :], k.W[g]).then_inc(k.raw_landed[g % RING], 16)


def act_split(k, g):
    if g.reg is None and g.base >= k.n_blocks:
        return
    act = k.nc.scalar
    wait(act, k.raw_landed[g.slot], (g.turn + 1).times(16))
    wait(act, k.block_done, g - (RING - 1))
    act.activation(k.whi[:, g.slot, :], k.raw[:, g.slot, :], ACT.Copy).then_inc(k.split_hi, 1)


def dve_split(k, g):
    if g.reg is None and g.base >= k.n_blocks:
        return
    dve = k.nc.vector
    wait(dve, k.split_hi, g + 1)
    dve.tensor_tensor(k.wlo[:, g.slot, :], k.raw[:, g.slot, :], k.whi[:, g.slot, :].bitcast(F32),
                      ALU.subtract).then_inc(k.split_lo, 1)


def pe_products(k, out, slot, t, tiles, moving):
    pe = k.nc.tensor
    hi, lo = moving
    w_hi, w_lo = k.whi[:, slot, t * P:(t + 1) * P], k.wlo[:, slot, t * P:(t + 1) * P]
    pe.matmul(out, w_hi, hi, start=(t == 0), stop=False)
    pe.matmul(out, w_hi, lo, start=False, stop=False)
    return pe.matmul(out, w_lo, hi, start=False, stop=(t == tiles - 1))


def pe_block(k, g, tiles, moving, more=None, ready=None):
    pe = k.nc.tensor
    wait(pe, k.split_lo, g + 1)
    wait(pe, k.bank_free, g - (RING - 1))
    for t in range(tiles):
        if ready is not None:
            ready(t)
        last = pe_products(k, k.bank[g.slot][:, :], g.slot, t, tiles, moving(t))
    if more is not None:
        both, taken = more
        wait(pe, k.cbank_free, taken)
        for t in range(tiles):
            w_hi, w_lo = k.whi[:, g.slot, t * P:(t + 1) * P], k.wlo[:, g.slot, t * P:(t + 1) * P]
            if t == tiles - 1:
                pe.matmul(k.cbank[:, 0:TC], w_lo, both(t)[:, 0:TC], start=False, stop=False)
                last = pe.matmul(k.cbank[:, :], w_hi, both(t), start=False, stop=True)
            else:
                pe.matmul(k.cbank[:, :], w_hi, both(t), start=(t == 0), stop=False)
                pe.matmul(k.cbank[:, 0:TC], w_lo, both(t)[:, 0:TC], start=False, stop=False)
    last.then_inc(k.block_done, 1)


def act_square(k, src, at, ready):
    act = k.nc.scalar
    ready(act)
    wait(act, k.ssq_added, at - 1)
    sq = k.sq[:, at.base % 2, :src.shape[-1]] if len(src.shape) == 2 else k.sq[:, at.base % 2:at.base % 2 + 1, :]
    act.activation(sq, src, ACT.Square).then_inc(k.sq_ready, 1)


def dve_add_square(k, at, first, width=T):
    dve = k.nc.vector
    wait(dve, k.sq_ready, at + 1)
    sq = k.sq[:, at.base % 2, :width]
    if first:
        dve.tensor_copy(k.ssq[:, :width], sq).then_inc(k.ssq_added, 1)
    else:
        wait(dve, k.ssq_added, at)
        dve.tensor_tensor(k.ssq[:, :width], k.ssq[:, :width], sq, ALU.add).then_inc(k.ssq_added, 1)


def pe_norm(k, n, squares, width=T):
    pe = k.nc.tensor
    wait(pe, k.ssq_added, squares)
    wait(pe, k.rstd_ready, n)
    pe.matmul(k.nbank[:, :width], k.ones[:, :], k.ssq[:, :width], start=True, stop=True).then_inc(k.norm_sum, 1)


def act_rstd(k, n, used, width=T, scale=1.0 / D, out=None):
    act = k.nc.scalar
    out = k.rstd if out is None else out
    used(act)
    wait(act, k.norm_sum, n + 1)
    act.activation(k.lnv[:, :width], k.nbank[:, :width], ACT.Ln, bias=k.eps_col[:, :], scale=scale).then_inc(k.ln_ready, 1)
    wait(act, k.ln_ready, n + 1)
    act.activation(out[:, :width], k.lnv[:, :width], ACT.Exp, scale=-0.5).then_inc(k.rstd_ready, 1)


def act_h_high(k, i, shift, hi, width=T):
    act = k.nc.scalar
    wait(act, k.h_made, i + 1)
    if shift is None:
        act.activation(hi, k.h32[:, i % 2, :width], ACT.Copy).then_inc(k.h_hi, 1)
    else:
        act.activation(hi, k.h32[:, i % 2, :width], ACT.Identity, bias=shift).then_inc(k.h_hi, 1)


def dve_h_low(k, i, shift, hi, lo, width=T):
    dve = k.nc.vector
    wait(dve, k.h_hi, i + 1)
    h32 = k.h32[:, i % 2, :width]
    if shift is None:
        dve.tensor_tensor(lo, h32, hi.bitcast(F32), ALU.subtract).then_inc(k.h_ready, 1)
    else:
        dve.scalar_tensor_tensor(lo, h32, shift, hi.bitcast(F32), ALU.add, ALU.subtract).then_inc(k.h_ready, 1)


def act_prenorm(k, i0, shift, hi, width=T):
    for c in range(DC):
        act_h_high(k, i0 + c, None if shift is None else shift[:, c:c + 1], hi[:, c, :width], width)


def dve_prenorm(k, n, i0, src, gain, shift, hi, lo, width=T):
    dve = k.nc.vector
    wait(dve, k.rstd_ready, n + 1)
    for c in range(DC + 1):
        if c < DC:
            if i0 + c >= 2:
                wait(dve, k.h_ready, i0 + c - 1)
            dve.scalar_tensor_tensor(k.h32[:, (i0 + c) % 2, :width], src[:, c, :width], gain[:, c:c + 1],
                                     k.rstd[:, :width], ALU.mult, ALU.mult).then_inc(k.h_made, 1)
        if c >= 1:
            dve_h_low(k, i0 + c - 1, None if shift is None else shift[:, c - 1:c],
                      hi[:, c - 1, :width], lo[:, c - 1, :width], width)


class Between(Phase):

    def __init__(self, post, gain, first, renorm=False):
        self.post, self.gain, self.first, self.renorm = post, gain, first, renorm

    def advance(self, q):
        q.norm += 2
        q.sq += DC
        q.h += DC
        q.xc += DC
        q.first += RING
        if not self.renorm:
            q.y += DC

    def pe(self, k, q):
        pe = k.nc.tensor
        pe_norm(k, q.norm, q.sq)
        for t in range(DC):
            wait(pe, k.h_ready, q.h + t + 1)
            for b in range(RING):
                g = q.g + b
                if t == 0:
                    wait(pe, k.split_lo, g + 1)
                    wait(pe, k.bank_free, g - (RING - 1))
                if t == DC - 1 and b == RING - 1:
                    pe_norm(k, q.norm + 1, q.sq + DC)
                last = pe_products(k, k.bank[g % RING][:, :], g % RING, t, DC, (k.h_hi_buf[:, t, :], k.h_lo_buf[:, t, :]))
                if t == DC - 1:
                    last.then_inc(k.block_done, 1)

    def act(self, k, q):
        act = k.nc.scalar
        act_rstd(k, q.norm, lambda act: None)
        gain = k.vec(self.gain)
        for c in range(DC):
            wait(act, k.x_ready, q.xc + c + 1)
            act.activation(k.h_hi_buf[:, c, :], k.x[:, c, :], ACT.Copy, scale=gain[:, c:c + 1]).then_inc(k.h_hi, 1)
            act_square(k, k.x[:, c, :], At(q.sq + c), lambda act: None)
        for b in range(RING, RING + LEAD):
            act_split(k, At(q.g + b))
        act_rstd(k, q.norm + 1, lambda act: None)

    def dve(self, k, q):
        dve = k.nc.vector
        gain = k.vec(self.gain)
        def low(c):
            wait(dve, k.h_hi, q.h + c + 1)
            dve.scalar_tensor_tensor(k.h_lo_buf[:, c, :], k.x[:, c, :], gain[:, c:c + 1],
                                     k.h_hi_buf[:, c, :].bitcast(F32), ALU.mult, ALU.subtract).then_inc(k.h_ready, 1)
        wait(dve, k.rstd_ready, q.norm + 1)
        for c in range(DC):
            dve_renew(k, c, q.xc, q.y, k.vec(self.post), self.renorm, (lambda: low(c - 1)) if c > 0 else None)
        low(DC - 1)
        first = self.first(k)
        for b in range(RING):
            g = q.g + b
            wait(dve, k.block_done, g + 1)
            dve.tensor_copy(first[b], k.bank[g % RING][:, :]).then_inc(k.bank_free, 1)
            if b < LEAD:
                dve_split(k, At(q.g + RING + b))
        wait(dve, k.rstd_ready, q.norm + 2)
        for b in range(RING):
            wait(dve, k.bank_free, q.g + b + 1)
            dve.tensor_tensor(first[b], first[b], k.rstd[:, :], ALU.mult).then_inc(k.first_scaled, 1)

    def pool(self, k, q):
        pool = k.nc.gpsimd
        pool.wait_ge(k.rstd_ready, q.norm + 1)
        for c in range(DC):
            at = q.sq + c
            pool.wait_ge(k.sq_ready, at + 1)
            if c == 0:
                pool.tensor_copy(k.ssq[:, :], k.sq[:, at % 2, :]).then_inc(k.ssq_added, 1)
            else:
                pool.wait_ge(k.ssq_added, at)
                pool.tensor_tensor(k.ssq[:, :], k.ssq[:, :], k.sq[:, at % 2, :], ALU.add).then_inc(k.ssq_added, 1)


def dve_renew(k, c, x0, y0, post, renorm, between=None):
    dve = k.nc.vector
    if renorm:
        dve.scalar_tensor_tensor(k.x[:, c, :], k.x[:, c, :], post[:, c:c + 1], k.rstd[:, :], ALU.mult, ALU.mult
                                 ).then_inc(k.x_ready, 1)
        if between:
            between()
        return
    dve.scalar_tensor_tensor(k.acc[:, c, :], k.acc[:, c, :], post[:, c:c + 1], k.rstd[:, :], ALU.mult, ALU.mult
                             ).then_inc(k.y_scaled, 1)
    if between:
        between()
    wait(dve, k.y_scaled, y0 + c + 1)
    dve.tensor_tensor(k.x[:, c, :], k.x[:, c, :], k.acc[:, c, :], ALU.add).then_inc(k.x_ready, 1)


class Last(Phase):

    def __init__(self, post):
        self.post = post

    def advance(self, q):
        q.norm += 1
        q.xc += DC
        q.y += DC

    def pe(self, k, q):
        pe_norm(k, q.norm, q.sq)

    def act(self, k, q):
        act_rstd(k, q.norm, lambda act: None)

    def dve(self, k, q):
        wait(k.nc.vector, k.rstd_ready, q.norm + 1)
        for c in range(DC):
            dve_renew(k, c, q.xc, q.y, k.vec(self.post), False)


def pe_pass(k, g0, nk, a0, begun=False, e0=None):
    pe = k.nc.tensor
    h = lambda t: (k.h_hi_buf[:, t, :], k.h_lo_buf[:, t, :])
    with pe.Fori(0, nk // 2 - begun) as it:
        for b in range(RING):
            pe_block(k, At(g0 + RING * begun + b, RING, it), DC, h)
            if e0 is not None and b == 0:
                wait(pe, k.share_used, At(2 * e0 + 1, 2, it))
                wait(pe, k.share_sel_ready, e0 // 4 + 1)
                pe.matmul(k.gbank[0][:, :], k.ones[0:N_EXPERTS, :],
                          k.share_sel[:, bass.ds(At(e0, 1, it).value, 1), :].rearrange("p o f -> p (o f)"),
                          start=True, stop=True).then_inc(k.share_ready, 1)
    a = lambda t: (k.a_hi_buf[:, t, :], k.a_lo_buf[:, t, :])
    g1 = g0 + 2 * nk
    a_ready = lambda t: wait(pe, k.a_ready, a0 + t + 1)
    with pe.Fori(0, DC // RING) as it:
        for b in range(RING):
            pe_block(k, At(g1 + b, RING, it), nk, a, ready=a_ready if b == 0 else None)


def act_pass(k, g0, nk, a0):
    act = k.nc.scalar
    with act.Fori(0, nk // 2) as it:
        for p in range(2):
            g, a = At(g0 + 2 * p, RING, it), At(a0 + p, 2, it)
            act_split(k, g + LEAD)
            act_split(k, g + LEAD + 1)
            wait(act, k.block_done, g + 1)
            act.activation(k.sil[:, p, :], k.bank[g.slot][:, :], ACT.Silu).then_inc(k.silu_ready, 1)
            wait(act, k.bank_free, g + 2)
            act.activation(k.a_hi_buf[:, bass.ds(At(p, 2, it).value, 1), :], k.a32[:, p:p + 1, :], ACT.Copy
                           ).then_inc(k.a_hi, 1)


def dve_pass(k, g0, nk, a0, e0):
    dve = k.nc.vector
    with dve.Fori(0, nk // 2) as it:
        for p in range(2):
            g, a = At(g0 + 2 * p, RING, it), At(a0 + p, 2, it)
            dve_split(k, g + LEAD)
            dve_split(k, g + LEAD + 1)
            wait(dve, k.block_done, g + 2)
            wait(dve, k.silu_ready, a + 1)
            wait(dve, k.share_ready, At(e0 + 1, 1, it))
            dve.tensor_tensor(k.sil[:, p, :], k.sil[:, p, :], k.gbank[0][:, :], ALU.mult).then_inc(k.share_used, 1)
            wait(dve, k.share_used, At(2 * e0 + p + 2, 2, it))
            if a0 + p >= 2:
                wait(dve, k.a_ready, a - 1)
            dve.tensor_tensor(k.a32[:, p, :], k.sil[:, p, :], k.bank[(g + 1).slot][:, :], ALU.mult
                              ).then_inc(k.bank_free, 2)
            dve_a_low(k, a, p, it)


def dve_a_low(k, a, p, it):
    dve = k.nc.vector
    f = slice(p, p + 1) if it is None else bass.ds(At(p, 2, it).value, 1)
    wait(dve, k.a_hi, a + 1)
    dve.tensor_tensor(k.a_lo_buf[:, f, :], k.a32[:, p:p + 1, :], k.a_hi_buf[:, f, :].bitcast(F32), ALU.subtract
                      ).then_inc(k.a_ready, 1)


def trips(eng, nk, begun, body):
    if begun:
        body(None, 0)
    with eng.Fori(0, nk // 2 - begun) as it:
        body(it, int(begun))


def act_ffn_pass(k, g0, nk, a0, s0, begun):
    act = k.nc.scalar
    def body(it, first):
        for p in range(2):
            m = (2 if it is not None else 0)
            g, a, s = At(g0 + RING * first + 2 * p, 2 * m, it), At(a0 + 2 * first + p, m, it), At(s0 + 2 * first + p, m, it)
            if it is None:
                wait(act, k.first_scaled, k.n_first + 2 * p + 1)
            else:
                act_split(k, g + LEAD)
                act_split(k, g + LEAD + 1)
                wait(act, k.gate_scaled, s - k.n_unscaled + 1)
            act.activation(k.sil[:, p, :], k.sil[:, p, :], ACT.Silu).then_inc(k.silu_ready, 1)
            wait(act, k.a_made, s + 1)
            hi = k.a_hi_buf[:, p:p + 1, :] if it is None else k.a_hi_buf[:, bass.ds(At(2 * first + p, 2, it).value, 1), :]
            act.activation(hi, k.a32[:, p:p + 1, :], ACT.Copy).then_inc(k.a_hi, 1)
    trips(act, nk, begun, body)


def dve_ffn_pass(k, g0, nk, a0, s0, begun):
    dve = k.nc.vector
    def body(it, first):
        for p in range(2):
            m = (2 if it is not None else 0)
            g, a, s = At(g0 + RING * first + 2 * p, 2 * m, it), At(a0 + 2 * first + p, m, it), At(s0 + 2 * first + p, m, it)
            if it is None:
                wait(dve, k.first_scaled, k.n_first + 2 * p + 2)
            else:
                dve_split(k, g + LEAD)
                dve_split(k, g + LEAD + 1)
                wait(dve, k.a_ready, a - 1)
                wait(dve, k.block_done, g + 1)
                dve.tensor_tensor(k.sil[:, p, :], k.bank[g.slot][:, :], k.rstd[:, :], ALU.mult).then_inc(k.gate_scaled, 1)
                wait(dve, k.block_done, g + 2)
                dve.tensor_tensor(k.a32[:, p, :], k.bank[(g + 1).slot][:, :], k.rstd[:, :], ALU.mult
                                  ).then_inc(k.bank_free, 2)
                wait(dve, k.bank_free, g + 2)
            wait(dve, k.silu_ready, a + 1)
            dve.tensor_tensor(k.a32[:, p, :], k.a32[:, p, :], k.sil[:, p, :], ALU.mult).then_inc(k.a_made, 1)
            if it is None:
                dve_a_low(k, a, p, None)
            else:
                f = bass.ds(At(2 * first + p, 2, it).value, 1)
                wait(dve, k.a_hi, a + 1)
                dve.tensor_tensor(k.a_lo_buf[:, f, :], k.a32[:, p:p + 1, :], k.a_hi_buf[:, f, :].bitcast(F32), ALU.subtract
                                  ).then_inc(k.a_ready, 1)
    trips(dve, nk, begun, body)


def act_down(k, g1, sq0=None, x0=None):
    act = k.nc.scalar
    trips = DC // RING
    final = sq0 is not None
    def body(it, t0):
        for b in range(RING):
            g = At(g1 + t0 * RING + b, RING if it is not None else 0, it)
            act_split(k, g + LEAD)
            if it is None and b == RING - 1:
                act_split(k, g + LEAD + 1)
                act_split(k, g + LEAD + 2)
            if sq0 is not None:
                c = At(b + t0 * RING, RING, it) if it is not None else At(b + t0 * RING)
                src = k.acc if x0 is None else k.x
                act_square(k, src[:, bass.ds(c.value, 1), :] if it is not None else src[:, c.base, :], c + sq0,
                           lambda act: wait(act, k.bank_free, g + 1) if x0 is None else wait(act, k.x_ready, c + (x0 + 1)))
    loop_but_last(act, trips, final, body)


def loop_but_last(eng, trips, peel, body):
    with eng.Fori(0, trips - 1 if peel else trips) as it:
        body(it, 0)
    if peel:
        body(None, trips - 1)


def dve_down(k, g1, add, sq0=None, into_x=None):
    dve = k.nc.vector
    trips = DC // RING
    final = sq0 is not None
    if sq0 is not None:
        dve.memset(k.ssq[:, :], 0.0).then_inc(k.ssq_clear, 1)
        k.n_clear += 1
        dve.wait_ge(k.ssq_clear, k.n_clear)
    def body(it, t0):
        for b in range(RING):
            g = At(g1 + t0 * RING + b, RING if it is not None else 0, it)
            c = At(b + t0 * RING, RING if it is not None else 0, it)
            acc = k.acc[:, bass.ds(c.value, 1), :] if it is not None else k.acc[:, c.base:c.base + 1, :]
            bank = k.bank[g.slot][:, :].rearrange("p (o f) -> p o f", o=1)
            dve_split(k, g + LEAD)
            tail = it is None and b == RING - 1
            if tail:
                dve_split(k, g + LEAD + 1)
            wait(dve, k.block_done, g + 1)
            if add:
                dve.tensor_tensor(acc, acc, bank, ALU.add).then_inc(k.bank_free, 1)
            else:
                dve.tensor_copy(acc, bank).then_inc(k.bank_free, 1)
            if into_x is not None:
                x0, gate = into_x
                x = k.x[:, bass.ds(c.value, 1), :] if it is not None else k.x[:, c.base:c.base + 1, :]
                wait(dve, k.bank_free, g + 1)
                dve.scalar_tensor_tensor(x, acc, gate[:, bass.ds(c.value, 1)] if it is not None else gate[:, c.base:c.base + 1], x, ALU.mult, ALU.add).then_inc(k.x_ready, 1)
            if tail:
                dve_split(k, g + LEAD + 2)
            if sq0 is not None:
                dve_add_square(k, c + sq0, first=False)
    loop_but_last(dve, trips, final, body)


class Counts:

    def __init__(self):
        self.g = 0
        self.a = 0
        self.sq = 0
        self.norm = 0
        self.h = 0
        self.xc = 0
        self.y = 0
        self.first = 0
        self.f = 0


def pe_mod(k, slot, blocks, tiles, out, which):
    pe = k.nc.tensor
    width = blocks * P
    hi = k.whi[:, slot:slot + blocks, :].rearrange("p s f -> p (s f)")
    lo = k.wlo[:, slot:slot + blocks, :].rearrange("p s f -> p (s f)")
    for t in tiles:
        c_hi = k.c_hi[:, t, which:which + 1].to_broadcast([P, P])
        c_lo = k.c_lo[:, t, which:which + 1].to_broadcast([P, P])
        w_hi, w_lo = hi[:, t * width:(t + 1) * width], lo[:, t * width:(t + 1) * width]
        pe.matmul(out, c_hi, w_hi, start=(t == 0), stop=False)
        pe.matmul(out, c_lo, w_hi, start=False, stop=False)
        last = pe.matmul(out, c_hi, w_lo, start=False, stop=(t == DC - 1))
    return last


def dve_mod(k, bank, blocks, j, which, at, given, free):
    dve = k.nc.vector
    own = k.own[:, 0:blocks * P].rearrange("p (j f) -> p j f", f=P)
    ident = k.ident[:, :].rearrange("p (o f) -> p o f", o=1).to_broadcast([P, blocks, P])
    dst = k.mod[:, bass.ds(j.value, blocks), which] if isinstance(j, At) else k.mod[:, j:j + blocks, which]
    wait(dve, k.mod_kept, at)
    dve.tensor_tensor(own, bank.rearrange("p (j f) -> p j f", f=P), ident, ALU.mult).then_inc(k.bank_free, free)
    wait(dve, k.bank_free, given)
    dve.tensor_reduce(dst, own, AX.X, ALU.add).then_inc(k.mod_kept, 1)


class Mod(Phase):
    blocks = 2 * DC
    LOADS = 2

    def advance(self, q):
        q.g += self.blocks

    def layout(self, k, ctx):
        k.mod_kept, = k.sems("mod_kept")

    def banks(self, k, n):
        return k.bank[2 * (n % 2):2 * (n % 2) + 2]

    def pe(self, k, q):
        pe = k.nc.tensor
        pe.wait_ge(k.c_ready, 3)
        for n in range(self.blocks // RING):
            if n >= 2:
                pe.wait_ge(k.bank_free, RING * (n - 1))
            for b in range(RING):
                pe.wait_ge(k.split_lo, RING * n + b + 1)
                for which in range(2):
                    last = pe_mod(k, 0, RING, (2 * b, 2 * b + 1), self.banks(k, n)[which][:, :], which)
                last.then_inc(k.block_done, 1)

    def act(self, k, q):
        act = k.nc.scalar
        act.wait_ge(k.small_loaded, 16 * self.LOADS)
        act.activation(k.c32[:, :, :], k.c_in[:, :, :], ACT.Silu).then_inc(k.c_ready, 1)
        act.wait_ge(k.c_ready, 1)
        act.activation(k.c_hi[:, :, :], k.c32[:, :, :], ACT.Copy).then_inc(k.c_ready, 1)
        for g in range(self.blocks + LEAD):
            act_split(k, At(g))

    def dve(self, k, q):
        dve = k.nc.vector
        dve.wait_ge(k.c_ready, 2)
        dve.tensor_tensor(k.c_lo[:, :, :], k.c32[:, :, :], k.c_hi[:, :, :].bitcast(F32), ALU.subtract).then_inc(k.c_ready, 1)
        for g in range(LEAD):
            dve_split(k, At(g))
        for n in range(self.blocks // RING):
            for b in range(RING):
                dve_split(k, At(RING * n + b + LEAD))
            dve.wait_ge(k.block_done, RING * (n + 1))
            for which in range(2):
                dve_mod(k, self.banks(k, n)[which][:, :], RING, RING * n, which, 2 * n + which,
                        RING * n + RING // 2 * (which + 1), RING // 2)


HEADS = 8
CH = 64
NCH = (T + TC) // CH
CCH = TC // CH
TT = T + TC
MOD_BLOCKS = 3
ZB, QB, VB, GB = range(1 + MOD_BLOCKS, 5 + MOD_BLOCKS)
HEAD_BLOCKS = GB + 1
CHAIN = [list(range(NCH)), list(range(CCH - 1, -1, -1)) + list(range(NCH - 1, CCH - 1, -1))]
STEPS = NCH - 1
REF = [CH // 2 - 1, CH // 2]
END = [CH - 1, 0]
N_TOK, N_SC, N_KV = 6, 2, 6
G_HEAD = N_TOK + N_SC + N_KV + 1
STATE_COPIES = 2 * (STEPS - 3)


class Head:

    def __init__(self, n):
        self.n = n if isinstance(n, At) else At(n)

    def count(self, per, i=0):
        return self.n.times(per) + i


def head_view(buf, h):
    return buf[:, bass.ds(h.value, 1), :].rearrange("p o f -> p (o f)") if h.reg is not None else buf[:, h.base, :]


def column(buf, h):
    return buf[:, bass.ds(h.value, 1)] if h.reg is not None else buf[:, h.base:h.base + 1]


class Hgrn(Phase):
    blocks = HEADS * HEAD_BLOCKS

    def advance(self, q):
        q.g += self.blocks
        q.norm += HEADS

    def layout(self, k, ctx):
        at = k.low
        def put(name, shape, dt=F32):
            nonlocal at
            t = k.sb(name, shape, dt, at=at)
            at += -(-int(np.prod(shape[1:])) * (1 if dt == I8 else 4) // 64) * 64
            return t
        k.hc = put("hc", [P, DC, 2 * TC], F32R)
        k.hc_hi, k.hc_lo = k.hc[:, :, 0:TC], k.hc[:, :, TC:2 * TC]
        k.z_st = put("z_st", [P, 2, TT])
        k.v_st = put("v_st", [P, TT])
        k.q_st = put("q_st", [P, T])
        k.g_st = put("g_st", [P, T])
        k.keep = put("keep", [P, 2, TT])
        k.kk = put("kk", [P, 2, TT])
        k.cum = put("cum", [P, 2, TT])
        k.ktok = k.sb("ktok", [P, 2, TT // P, P], F32, at=k.arena["cum"][0])
        k.qq = put("qq", [P, 2, T])
        k.vtok = put("vtok", [P, T // P, P])
        k.v_half = put("v_half", [P, 2, TT // P, P])
        k.pt = put("pt", [P, 2, T // P, P])
        k.pt_mask = put("pt_mask", [P, 2, T // P, P], I8)
        k.state = put("state", [P, 2, T // CH, P])
        k.xs = put("xs", [P, 2, 2, P])
        k.restart = put("restart", [P, TT])
        k.silg = put("silg", [P, T])
        k.o32 = put("o32", [P, T])
        k.osq = put("osq", [P, T])
        k.refs = put("refs", [P, 2, NCH])
        k.lastref = put("lastref", [P, 2, NCH])
        k.rho = put("rho", [P, 2, NCH])
        k.lb = put("lb", [P, 2, HEADS])
        k.one_lb = put("one_lb", [P, 2, HEADS])
        k.lbt = put("lbt", [P, 4, HEADS])
        k.own = put("own", [P, RING * P])
        assert at <= k.limit
        (k.y_hi, k.y_parts, k.pool_order, k.lb_max, k.lb_sub, k.lb_exp, k.lb_sum
         ) = k.sems("y_hi y_parts pool_order lb_max lb_sub lb_exp lb_sum")
        (k.mod1, k.mod2, k.cbank_free, k.silq_done, k.silg_done, k.tok_part, k.y32_ready
         ) = k.sems("mod1 mod2 cbank_free silq_done silg_done tok_part y32_ready")
        (k.sig_done, k.ln_done, k.scan_done, k.exp_done, k.kk_done, k.qq_done, k.gla_full
         ) = k.sems("sig_done ln_done scan_done exp_done kk_done qq_done gla_full")
        (k.tok_copied, k.pt_ready, k.state_copied, k.o_taken, k.osq_ready, k.y_ready, k.lb_ready
         ) = k.sems("tok_copied pt_ready state_copied o_taken osq_ready y_ready lb_ready")
        k.hd_order, k.chain_step, k.rho_done, k.ctx_half = k.sems("hd_order chain_step rho_done ctx_half")

    def pe_iteration(self, k, q, h, e):
        pe = k.nc.tensor
        lat = lambda t: (k.h_hi_buf[:, t, :], k.h_lo_buf[:, t, :])
        con = lambda t: k.hc[:, t, :]
        if h is not None:
            g = h.n.times(HEAD_BLOCKS) + q.g
            ready = None if e is not None or h.n.base > 0 else lambda t: pe.wait_ge(k.h_ready, q.h - DC + t + 1)
            pe_block(k, g, DC, lat, more=(con, h.count(3, 0)), ready=ready)
            wait(pe, k.split_lo, g + MOD_BLOCKS + 1)
            wait(pe, k.bank_free, g + (1 - (RING - 1)))
            pe_mod(k, 1, MOD_BLOCKS, range(DC), k.bank[1][:, 0:MOD_BLOCKS * P], 0).then_inc(k.block_done, MOD_BLOCKS)
            pe_block(k, g + ZB, DC, lat, more=(con, h.count(3, 1)))
            pe_block(k, g + QB, DC, lat)
        if e is not None:
            self.pe_tokens(k, e)
        if h is not None:
            pe_block(k, g + VB, DC, lat, more=(con, h.count(3, 2)))
        if e is not None:
            self.pe_states(k, e)
        if h is not None:
            pe_block(k, g + GB, DC, lat)
        if e is not None:
            self.pe_output(k, q, e)

    def pe_tokens(self, k, e):
        pe = k.nc.tensor
        wait(pe, k.kk_done, e.count(2, 2))
        n = 0
        for src in (lambda j: k.v_st[:, j * P:(j + 1) * P], lambda j: k.kk[:, 0, j * P:(j + 1) * P],
                    lambda j: k.kk[:, 1, j * P:(j + 1) * P]):
            for tiles in (range(4), range(4, 6)):
                if n < 2:
                    wait(pe, k.o_taken, e.n)
                else:
                    wait(pe, k.tok_copied, e.count(N_TOK, n - 1))
                for i, j in enumerate(tiles):
                    last = pe.transpose(k.gbank[n % 2][:, i * P:(i + 1) * P], src(j), k.ident[:, :])
                last.then_inc(k.gla_full, 1)
                n += 1
        wait(pe, k.qq_done, e.count(2, 2))
        for d in range(2):
            wait(pe, k.tok_copied, e.count(N_TOK, 5 + d))
            for j in range(T // P):
                last = pe.matmul(k.gbank[d][:, j * P:(j + 1) * P], k.kk[:, d, TC + j * P:TC + (j + 1) * P],
                                 k.qq[:, d, j * P:(j + 1) * P], start=True, stop=True)
            last.then_inc(k.gla_full, 1)
            n += 1

    def pe_states(self, k, e):
        pe = k.nc.tensor
        for n in range(N_KV):
            d, lot = n % 2, n // 2
            if n < 2:
                wait(pe, k.tok_copied, e.count(N_TOK, N_TOK))
                wait(pe, k.tok_part, e.count(4, 4))
                wait(pe, k.pt_ready, e.count(N_SC, n + 1))
            else:
                wait(pe, k.chain_step, e.count(2 * STEPS, 2 * (4 * lot - 1) + d + 1))
            for i, j in enumerate(range(4 * lot, min(4 * lot + 4, STEPS))):
                c = CHAIN[d][j]
                last = pe.matmul(k.gbank[d][:, i * P:(i + 1) * P], k.ktok[:, d, c // 2, :],
                                 k.v_half[:, c % 2, c // 2, :], start=True, stop=True)
            last.then_inc(k.gla_full, 1)

    def pe_output(self, k, q, e):
        pe = k.nc.tensor
        wait(pe, k.chain_step, e.count(2 * STEPS, 2 * STEPS))
        wait(pe, k.state_copied, e.count(STATE_COPIES, STATE_COPIES))
        o = k.gbank[0]
        for j in range(T // P):
            for d in range(2):
                pe.matmul(o[:, j * P:(j + 1) * P], k.vtok[:, j, :], k.pt[:, d, j, :], start=(d == 0), stop=False)
            for half in range(2):
                c = 2 * j + half
                for d in range(2):
                    at = c if d == 0 else T // CH - 1 - c
                    last = pe.matmul(o[:, c * CH:(c + 1) * CH], k.state[:, d, at, :], k.qq[:, d, c * CH:(c + 1) * CH],
                                     start=False, stop=(half == 1 and d == 1))
        last.then_inc(k.gla_full, 1)
        wait(pe, k.osq_ready, e.count(1, 1))
        wait(pe, k.rstd_ready, e.n + q.norm)
        pe.matmul(k.nbank[:, :], k.ones[:, :], k.osq[:, :], start=True, stop=True).then_inc(k.norm_sum, 1)

    def run(self, eng, k, q, iteration):
        iteration(k, q, Head(0), None)
        iteration(k, q, Head(1), Head(0))
        with eng.Fori(0, HEADS - 2) as it:
            iteration(k, q, Head(At(2, 1, it)), Head(At(1, 1, it)))
        iteration(k, q, None, Head(HEADS - 1))

    def pe(self, k, q):
        pe = k.nc.tensor
        self.run(pe, k, q, self.pe_iteration)

    def act_iteration(self, k, q, h, e):
        act = k.nc.scalar
        g = h.n.times(HEAD_BLOCKS) + q.g if h is not None else None
        last = h is None
        def split(b):
            if h is not None:
                act_split(k, g + b + LEAD)
        split(0)
        split(1)
        if e is not None:
            wait(act, k.bank_free, e.n.times(HEAD_BLOCKS) + (q.g + HEAD_BLOCKS))
            wait(act, k.cbank_free, e.count(3, 3))
            for d in range(2):
                act.activation(k.keep[:, d, :], k.z_st[:, d, :], ACT.Sigmoid).then_inc(k.sig_done, 1)
                act.activation(k.kk[:, d, :], k.z_st[:, d, :], ACT.Sigmoid, scale=-1.0).then_inc(k.sig_done, 1)
        split(2)
        if e is not None:
            act.activation(k.qq[:, 0, :], k.q_st[:, :], ACT.Sigmoid).then_inc(k.sig_done, 1)
            act.activation(k.silg[:, :], k.g_st[:, :], ACT.Sigmoid).then_inc(k.sig_done, 1)
        if e is not None:
            for d in range(2):
                wait(act, k.sig_done, e.count(6, 2 * d + 1))
                act.activation(k.keep[:, d, :], k.keep[:, d, :], ACT.Ln, bias=column(k.lb[:, d, :], e.n),
                               scale=column(k.one_lb[:, d, :], e.n)).then_inc(k.ln_done, 1)
        split(3)
        if e is not None:
            for d in range(2):
                wait(act, k.scan_done, e.count(2, d + 1))
                act.activation(k.rho[:, d, :], k.rho[:, d, :], ACT.Exp).then_inc(k.rho_done, 1)
                act.activation(k.keep[:, d, :], k.cum[:, d, :], ACT.Exp, scale=-1.0).then_inc(k.exp_done, 1)
                if d == 0:
                    wait(act, k.silq_done, e.count(1, 1))
                act.activation(k.qq[:, d, :], k.cum[:, d, TC:], ACT.Exp).then_inc(k.exp_done, 1)
        split(4)
        split(5)
        if e is not None:
            n = 0
            wait(act, k.exp_done, e.count(4, 4))
            for dst in ("v", 0, 1):
                for tiles in (range(4), range(4, 6)):
                    wait(act, k.gla_full, e.count(G_HEAD, n + 1))
                    src = k.gbank[n % 2][:, :len(tiles) * P].rearrange("p (j v) -> p j v", v=P)
                    j0, j1 = tiles[0], tiles[-1] + 1
                    if dst == "v":
                        a, b = max(j0, TC // P), j1
                        act.activation(k.vtok[:, a - TC // P:b - TC // P, :], src[:, a - j0:b - j0, :], ACT.Copy).then_inc(k.tok_part, 1)
                        act.activation(k.v_half[0:CH, 0, j0:j1, :], src[0:CH], ACT.Copy).then_inc(k.tok_part, 1)
                        act.activation(k.v_half[CH:P, 1, j0:j1, :], src[CH:P], ACT.Copy).then_inc(k.tok_copied, 1)
                    else:
                        act.activation(k.ktok[:, dst, j0:j1, :], src, ACT.Copy).then_inc(k.tok_copied, 1)
                    n += 1
        split(6)
        if e is not None:
            for j in range(3, STEPS):
                for d in range(2):
                    c = CHAIN[d][j]
                    wait(act, k.chain_step, e.count(2 * STEPS, 2 * j + d + 1))
                    act.activation(k.state[:, d, j - 3, :], k.xs[:, d, j % 2, :], ACT.Copy,
                                   scale=k.rho[:, d, c:c + 1]).then_inc(k.state_copied, 1)
        split(7)
        if e is not None:
            wait(act, k.o_taken, e.count(1, 1))
            act.activation(k.osq[:, :], k.o32[:, :], ACT.Square).then_inc(k.osq_ready, 1)
            act_rstd(k, e.n + q.norm, lambda act: wait(act, k.y_ready, e.n), scale=1.0 / P)
            wait(act, k.y32_ready, e.count(1, 1))
            act.activation(head_view(k.a_hi_buf, e.n), k.o32[:, :], ACT.Copy).then_inc(k.y_hi, 1)

    def act(self, k, q):
        self.run(k.nc.scalar, k, q, self.act_iteration)

    def dve_iteration(self, k, q, h, e):
        dve = k.nc.vector
        g = h.n.times(HEAD_BLOCKS) + q.g if h is not None else None
        def split(*blocks):
            if h is not None:
                for b in blocks:
                    dve_split(k, g + b + LEAD)
        def take(b, dst, context=False):
            if h is None:
                return
            wait(dve, k.block_done, g + b + 1)
            if context:
                dve.tensor_copy(dst[:, 0:TC], k.cbank[:, 0:TC]).then_inc(k.ctx_half, 1)
                dve.tensor_copy(dst[:, TC:], k.bank[(g + b).slot][:, :]).then_inc(k.bank_free, 1)
                wait(dve, k.ctx_half, h.count(3, {0: 1, ZB: 2, VB: 3}[b]))
                dve.tensor_tensor(dst[:, 0:TC], dst[:, 0:TC], k.cbank[:, TC:], ALU.add).then_inc(k.cbank_free, 1)
            else:
                dve.tensor_copy(dst, k.bank[(g + b).slot][:, :]).then_inc(k.bank_free, 1)
        split(0, 1)
        if e is not None:
            wait(dve, k.sig_done, e.count(6, 2))
        take(0, k.z_st[:, 0, :], context=True)
        split(2)
        if e is not None:
            wait(dve, k.sig_done, e.count(6, 6))
            wait(dve, k.y32_ready, e.n)
            dve.tensor_tensor(k.q_st[:, :], k.q_st[:, :], k.qq[:, 0, :], ALU.mult).then_inc(k.silq_done, 1)
            dve.tensor_tensor(k.silg[:, :], k.silg[:, :], k.g_st[:, :], ALU.mult).then_inc(k.silg_done, 1)
        if h is not None:
            wait(dve, k.block_done, g + MOD_BLOCKS + 1)
            dve_mod(k, k.bank[1][:, 0:MOD_BLOCKS * P], MOD_BLOCKS, h.n.times(MOD_BLOCKS) + 2 * DC, 0,
                    h.n + 2 * (2 * DC // RING), g + MOD_BLOCKS + 1, MOD_BLOCKS)
        split(3)
        if e is not None:
            for d in range(2):
                wait(dve, k.ln_done, e.count(2, d + 1))
                way = slice(None) if d == 0 else slice(None, None, -1)
                dve.tensor_tensor_scan(k.cum[:, d, way], k.restart[:, :], k.keep[:, d, way], 0.0, ALU.mult, ALU.add
                                       ).then_inc(k.hd_order, 1)
                wait(dve, k.hd_order, e.count(10, 5 * d + 1))
                cum = k.cum[:, d, :].rearrange("p (n c) -> p n c", c=CH)
                dve.tensor_copy(k.refs[:, d, :], cum[:, :, REF[d]]).then_inc(k.hd_order, 1)
                wait(dve, k.hd_order, e.count(10, 5 * d + 2))
                dve.tensor_tensor(k.lastref[:, d, :], cum[:, :, END[d]], k.refs[:, d, :], ALU.subtract).then_inc(k.hd_order, 1)
                wait(dve, k.hd_order, e.count(10, 5 * d + 3))
                if d == 0:
                    dve.tensor_tensor(k.rho[:, 0, 0:NCH - 1], k.lastref[:, 0, 0:NCH - 1], k.refs[:, 0, 1:NCH], ALU.add
                                      ).then_inc(k.hd_order, 1)
                    dve.tensor_copy(k.rho[:, 0, NCH - 1:NCH], k.lastref[:, 0, NCH - 1:NCH]).then_inc(k.hd_order, 1)
                else:
                    dve.tensor_tensor(k.rho[:, 1, 1:NCH], k.lastref[:, 1, 1:NCH], k.refs[:, 1, 0:NCH - 1], ALU.add
                                      ).then_inc(k.hd_order, 1)
                    dve.tensor_tensor(k.rho[:, 1, 0:1], k.lastref[:, 1, 0:1], k.refs[:, 1, NCH - 1:NCH], ALU.add
                                      ).then_inc(k.hd_order, 1)
                wait(dve, k.hd_order, e.count(10, 5 * d + 5))
                dve.tensor_tensor(cum, cum, k.refs[:, d, :].rearrange("p (n o) -> p n o", o=1).to_broadcast([P, NCH, CH]),
                                  ALU.subtract).then_inc(k.scan_done, 1)
        take(ZB, k.z_st[:, 1, :], context=True)
        if e is not None:
            for d in range(2):
                wait(dve, k.exp_done, e.count(4, 2 * d + 2))
                dve.scalar_tensor_tensor(k.kk[:, d, :], k.kk[:, d, :], column(k.one_lb[:, d, :], e.n), k.keep[:, d, :],
                                         ALU.mult, ALU.mult).then_inc(k.kk_done, 1)
                dve.tensor_tensor(k.qq[:, d, :], k.qq[:, d, :], k.q_st[:, :], ALU.mult).then_inc(k.qq_done, 1)
            wait(dve, k.qq_done, e.count(2, 2))
        split(4)
        take(QB, k.q_st[:, :])
        if e is not None:
            wait(dve, k.gla_full, e.count(G_HEAD, N_TOK + N_SC))
        split(5)
        if e is not None:
            for d in range(2):
                dve.copy_predicated(k.pt[:, d, :, :], k.pt_mask[:, d, :, :],
                                    k.gbank[d][:, :].rearrange("p (j t) -> p j t", t=P)).then_inc(k.pt_ready, 1)
        take(VB, k.v_st[:, :], context=True)
        if e is not None:
            for j in range(STEPS):
                for d in range(2):
                    s = 2 * j + d
                    if j % 4 == 0:
                        wait(dve, k.gla_full, e.count(G_HEAD, N_TOK + N_SC + 2 * (j // 4) + d + 1))
                    if j > 0:
                        wait(dve, k.chain_step, e.count(2 * STEPS, s - 1))
                    if j >= 5:
                        wait(dve, k.state_copied, e.count(STATE_COPIES, 2 * (j - 5) + d + 1))
                    kv = k.gbank[d][:, (j % 4) * P:(j % 4 + 1) * P]
                    before = CHAIN[d][j - 1]
                    if j == 0:
                        ins = dve.tensor_copy(k.xs[:, d, 0, :], kv)
                    else:
                        ins = dve.scalar_tensor_tensor(k.xs[:, d, j % 2, :], k.xs[:, d, (j - 1) % 2, :],
                                                       k.rho[:, d, before:before + 1], kv, ALU.mult, ALU.add)
                    ins.then_inc(k.chain_step, 1)
        split(6)
        if e is not None:
            wait(dve, k.silg_done, e.count(1, 1))
        take(GB, k.g_st[:, :])
        split(7)
        if e is not None:
            wait(dve, k.gla_full, e.count(G_HEAD, G_HEAD))
            wait(dve, k.y_parts, e.n)
            dve.tensor_copy(k.o32[:, :], k.gbank[0][:, :]).then_inc(k.o_taken, 1)
            wait(dve, k.rstd_ready, e.n + (q.norm + 1))
            wait(dve, k.osq_ready, e.count(1, 1))
            dve.scalar_tensor_tensor(k.o32[:, :], k.o32[:, :], k.vec("gnorm")[:, 0:1], k.rstd[:, :], ALU.mult, ALU.mult
                                     ).then_inc(k.y_ready, 1)
            wait(dve, k.y_ready, e.count(1, 1))
            dve.tensor_tensor(k.o32[:, :], k.o32[:, :], k.silg[:, :], ALU.mult).then_inc(k.y32_ready, 1)
            wait(dve, k.y_hi, e.n + 1)
            dve.tensor_tensor(head_view(k.a_lo_buf, e.n), k.o32[:, :], head_view(k.a_hi_buf, e.n).bitcast(F32), ALU.subtract
                              ).then_inc(k.y_parts, 1)


    def dve(self, k, q):
        self.run(k.nc.vector, k, q, self.dve_iteration)


class HgrnInput(Phase):
    blocks = 0

    def advance(self, q):
        q.sq += 2 * DC
        q.norm += 2
        q.h += 2 * DC

    def layout(self, k, ctx):
        at = k.low + 2 * DC * TC * 4
        k.x1 = k.sb("x1", [P, DC, T], F32, at=at)
        k.xc1 = k.sb("xc1", [P, DC, TC], F32, at=at + DC * T * 4)
        k.sq1 = k.sb("sq1", [P, 2, T], F32, at=at + DC * (T + TC) * 4)
        k.h321 = k.sb("h321", [P, 2, T], F32, at=at + DC * (T + TC) * 4 + 2 * T * 4)

    def pool(self, k, q):
        pool = k.nc.gpsimd
        done = Order(pool, k.pool_order)
        def then(ins):
            done(ins)
            done.wait()
        then(pool.memset(k.restart[:, :], 1.0))
        then(pool.memset(k.pt_mask[:, :, :, :], 1))
        then(pool.memset(k.restart[:, ::CH], 0.0))
        for d in range(2):
            then(pool.affine_select(out=k.pt_mask[:, d, :, :], in_=k.pt_mask[:, d, :, :], compare_op=ALU.is_ge,
                                    fill=0.0, base=0, pattern=[[0, T // P], [1 - 2 * d, P]],
                                    channel_multiplier=2 * d - 1))
        then(pool.memset(k.pt_mask[0:CH, 0, :, CH:P], 0))
        then(pool.memset(k.pt_mask[CH:P, 1, :, 0:CH], 0))
        then(pool.memset(k.pt[:, :, :, :], 0.0))
        then(pool.memset(k.v_half[:, :, :, :], 0.0))

    def pe(self, k, q):
        pe_norm(k, q.norm, q.sq + DC, TC)
        pe_norm(k, q.norm + 1, q.sq + 2 * DC)

    def act(self, k, q):
        act = k.nc.scalar
        k.sq, k.h32 = k.sq1, k.h321
        act.wait_ge(k.lb_sub, 4)
        act.activation(k.lbt[:, 0:2, :], k.lbt[:, 0:2, :], ACT.Exp).then_inc(k.lb_exp, 1)
        act.activation(k.lbt[:, 2:4, :], k.lbt[:, 2:4, :], ACT.Exp).then_inc(k.lb_exp, 1)
        for c in range(DC):
            act_square(k, k.xc1[:, c, :], At(q.sq + c), lambda act: wait(act, k.x_loaded, 32))
        act_rstd(k, q.norm, lambda act: None, TC)
        for c in range(DC):
            act_square(k, k.x1[:, c, :], At(q.sq + DC + c), lambda act: wait(act, k.x_loaded, 32))
        act_prenorm(k, q.h, k.shift1[:, 1, :], k.hc_hi, TC)
        act_rstd(k, q.norm + 1, lambda act: wait(act, k.h_ready, q.h + DC))
        act_prenorm(k, q.h + DC, k.shift1[:, 0, :], k.h_hi_buf)
        act.wait_ge(k.pool_order, 9)
        act.wait_ge(k.lb_ready, 4)

    def dve(self, k, q):
        dve = k.nc.vector
        k.sq, k.h32 = k.sq1, k.h321
        lbf, lbb = k.vec("lb_f"), k.vec("lb_b")
        for d, v in enumerate((lbf, lbb)):
            dve.tensor_tensor(k.lb[:, d, :], v[:, 0:8], v[:, 8:16], ALU.max).then_inc(k.lb_max, 1)
        dve.wait_ge(k.lb_max, 2)
        for d, v in enumerate((lbf, lbb)):
            dve.tensor_tensor(k.lbt[:, 2 * d, :], v[:, 0:8], k.lb[:, d, :], ALU.subtract).then_inc(k.lb_sub, 1)
            dve.tensor_tensor(k.lbt[:, 2 * d + 1, :], v[:, 8:16], k.lb[:, d, :], ALU.subtract).then_inc(k.lb_sub, 1)
        dve.wait_ge(k.lb_sub, 4)
        for c in range(DC):
            dve_add_square(k, At(q.sq + c), first=(c == 0), width=TC)
        dve.wait_ge(k.lb_exp, 2)
        for d in range(2):
            dve.tensor_tensor(k.lb[:, d, :], k.lbt[:, 2 * d, :], k.lbt[:, 2 * d + 1, :], ALU.add).then_inc(k.lb_sum, 1)
        dve.wait_ge(k.lb_sum, 2)
        dve.reciprocal(k.lb[:, :, :], k.lb[:, :, :]).then_inc(k.lb_sum, 1)
        dve.wait_ge(k.lb_sum, 3)
        for d in range(2):
            dve.tensor_tensor(k.one_lb[:, d, :], k.lbt[:, 2 * d + 1, :], k.lb[:, d, :], ALU.mult).then_inc(k.lb_ready, 1)
        dve.wait_ge(k.lb_ready, 2)
        for d in range(2):
            dve.tensor_tensor(k.lb[:, d, :], k.lbt[:, 2 * d, :], k.lb[:, d, :], ALU.mult).then_inc(k.lb_ready, 1)
        dve.wait_ge(k.mod_kept, 4 * DC // RING)
        b = k.vec("b_mod")
        for w in range(2):
            dve.tensor_tensor(k.shift1[:, w, :], k.mod[:, 0:DC, w], b[:, 0:DC], ALU.add).then_inc(k.mod1, 1)
            dve.tensor_tensor(k.gain1[:, w, :], k.mod[:, DC:2 * DC, w], b[:, DC:2 * DC], ALU.add).then_inc(k.mod1, 1)
        dve.wait_ge(k.mod1, 4)
        for w in range(2):
            dve.scalar_tensor_tensor(k.gain1[:, w, :], k.gain1[:, w, :], 1.0, k.vec("norm1_g"), ALU.add, ALU.mult
                                     ).then_inc(k.mod1, 1)
        dve.wait_ge(k.rstd_ready, q.norm + 1)
        for c in range(DC):
            dve_add_square(k, At(q.sq + DC + c), first=(c == 0))
        dve.wait_ge(k.mod1, 6)
        dve_prenorm(k, q.norm, q.h, k.xc1, k.gain1[:, 1, :], k.shift1[:, 1, :], k.hc_hi, k.hc_lo, TC)
        dve_prenorm(k, q.norm + 1, q.h + DC, k.x1, k.gain1[:, 0, :], k.shift1[:, 0, :], k.h_hi_buf, k.h_lo_buf)
        dve.wait_ge(k.pool_order, 9)


class HgrnOutput(Phase):
    blocks = DC

    def advance(self, q):
        q.g += self.blocks
        q.sq += DC

    def pe(self, k, q):
        pe = k.nc.tensor
        pe.wait_ge(k.y_parts, HEADS)
        y = lambda t: (k.a_hi_buf[:, t, :], k.a_lo_buf[:, t, :])
        with pe.Fori(0, DC // RING) as it:
            for b in range(RING):
                pe_block(k, At(q.g + b, RING, it), DC, y)

    def act(self, k, q):
        act = k.nc.scalar
        k.sq, k.h32 = k.sq0, k.h320
        act.wait_ge(k.block_done, q.g)
        act.wait_ge(k.y32_ready, HEADS)
        act.wait_ge(k.y_parts, HEADS)
        act.dma_start(k.x[:, :, :], k.xT).then_inc(k.x_loaded, 16)
        with act.Fori(0, DC // RING) as it:
            for b in range(RING):
                g = At(q.g + b, RING, it)
                act_split(k, g + LEAD)
                c = At(b, RING, it)
                act_square(k, k.x[:, bass.ds(c.value, 1), :], c + q.sq, lambda act: wait(act, k.bank_free, g + 1))

    def dve(self, k, q):
        dve = k.nc.vector
        k.sq, k.h32 = k.sq0, k.h320
        n = DC * 3 + 2 * DC
        b = k.vec("b_mod")
        dve.wait_ge(k.mod_kept, 4 * DC // RING + HEADS)
        dve.tensor_tensor(k.mod[:, 2 * DC:n, 0], k.mod[:, 2 * DC:n, 0], b[:, 2 * DC:n], ALU.add).then_inc(k.mod2, 1)
        dve.wait_ge(k.mod2, 1)
        dve.scalar_tensor_tensor(k.gain2[:, :], k.mod[:, 4 * DC:5 * DC, 0], 1.0, k.vec("norm2_g"), ALU.add, ALU.mult
                                 ).then_inc(k.mod2, 1)
        dve.tensor_copy(k.shift2[:, :], k.mod[:, 3 * DC:4 * DC, 0]).then_inc(k.mod2, 1)
        dve.memset(k.ssq[:, :], 0.0).then_inc(k.ssq_clear, 1)
        k.n_clear += 1
        dve.wait_ge(k.ssq_clear, k.n_clear)
        dve.wait_ge(k.x_loaded, 48)
        with dve.Fori(0, DC // RING) as it:
            for b in range(RING):
                g = At(q.g + b, RING, it)
                dve_split(k, g + LEAD)
                c = At(b, RING, it)
                x = k.x[:, bass.ds(c.value, 1), :]
                wait(dve, k.block_done, g + 1)
                dve.scalar_tensor_tensor(x, k.bank[g.slot][:, :].rearrange("p (o f) -> p o f", o=1),
                                         k.mod[:, bass.ds((c + 2 * DC).value, 1), 0], x, ALU.mult, ALU.add
                                         ).then_inc(k.bank_free, 1)
                dve_add_square(k, c + q.sq, first=False)


N_EXPERTS = 16
GROUPS = 4
PER_GROUP = N_EXPERTS // GROUPS
D_EXPERT = 256
TT4 = T // P


class MoeInput(Phase):
    blocks = DC

    def advance(self, q):
        q.g += self.blocks
        q.norm += 1
        q.h += DC

    def layout(self, k, ctx):
        at = k.top
        def put(name, shape, dt=F32):
            nonlocal at
            t = k.sb(name, shape, dt, at=at)
            at += -(-int(np.prod(shape[1:])) * 4 // 64) * 64
            return t
        k.share_sel = put("share_sel", [N_EXPERTS, N_EXPERTS, T])
        E = [P, TT4, GROUPS, PER_GROUP]
        k.score = put("score", E)
        k.choice = put("choice", E)
        k.rank = put("rank", E)
        k.above = put("above", E)
        k.keep4 = put("keep4", E)
        k.gsum = put("gsum", [P, TT4, GROUPS])
        k.grank = put("grank", [P, TT4, GROUPS])
        k.gabove = put("gabove", [P, TT4, GROUPS])
        k.den = put("den", [P, TT4])
        k.share_t = put("share_t", [N_EXPERTS, T])
        k.rw = put("rw", [P, DC, N_EXPERTS])
        k.rw_hi = k.sb("rw_hi", [P, DC, P], F32R, at=k.arena["acc"][0])
        k.rw_lo = k.sb("rw_lo", [P, DC, P], F32R, at=k.arena["acc"][0] + DC * P * 4)
        assert at <= k.limit, at
        (k.share_ready, k.share_used, k.share_sel_ready, k.rw_loaded, k.rw_split, k.logits_done, k.score_done
         ) = k.sems("share_ready share_used share_sel_ready rw_loaded rw_split logits_done score_done")
        k.route, k.logits_copied = k.sems("route logits_copied")

    def pe(self, k, q):
        pe = k.nc.tensor
        pe_norm(k, q.norm, q.sq)
        pe.wait_ge(k.bank_free, q.g)
        self.pe_mod_group(k, q, 0)
        pe.wait_ge(k.rw_split, 2)
        for c in range(DC):
            pe.wait_ge(k.h_ready, q.h + c + 1)
            w_hi, w_lo = k.rw_hi[:, c, :], k.rw_lo[:, c, :]
            pe.matmul(k.gbank[0][:, :], w_hi, k.h_hi_buf[:, c, :], start=(c == 0), stop=False)
            pe.matmul(k.gbank[0][:, :], w_hi, k.h_lo_buf[:, c, :], start=False, stop=False)
            last = pe.matmul(k.gbank[0][:, :], w_lo, k.h_hi_buf[:, c, :], start=False, stop=(c == DC - 1))
        last.then_inc(k.logits_done, 1)
        pe.wait_ge(k.logits_copied, 1)
        for t in range(TT4):
            last = pe.transpose(k.gbank[1][:, t * N_EXPERTS:(t + 1) * N_EXPERTS], k.share_t[:, t * P:(t + 1) * P],
                                k.ident[0:N_EXPERTS, 0:N_EXPERTS])
        last.then_inc(k.logits_done, 1)
        self.pe_mod_group(k, q, 1)
        pe.wait_ge(k.route, k.ROUTE_STEPS)
        for t in range(TT4):
            last = pe.transpose(k.gbank[1][0:N_EXPERTS, t * P:(t + 1) * P],
                                k.keep4[:, t, :, :].rearrange("p g e -> p (g e)"), k.ident[:, :])
        last.then_inc(k.logits_done, 1)

    @staticmethod
    def repeats(w):
        return w.rearrange("p c (r e) -> p c r e", e=N_EXPERTS)

    @staticmethod
    def repeated(k):
        return k.rw[:, :, :].rearrange("p c (o e) -> p c o e", o=1).to_broadcast([P, DC, P // N_EXPERTS, N_EXPERTS])

    @staticmethod
    def pe_mod_group(k, q, n):
        for b in range(RING):
            wait(k.nc.tensor, k.split_lo, q.g + RING * n + b + 1)
            pe_mod(k, 0, RING, (2 * b, 2 * b + 1), k.bank[n][:, :], 0).then_inc(k.block_done, 1)

    @staticmethod
    def dve_mod_group(k, q, n):
        wait(k.nc.vector, k.block_done, q.g + RING * (n + 1))
        dve_mod(k, k.bank[n][:, :], RING, 5 * DC + RING * n, 0, 4 * DC // RING + HEADS + n, q.g + RING * (n + 1), RING)

    def act(self, k, q):
        act = k.nc.scalar
        act.wait_ge(k.mod_kept, 4 * DC // RING + HEADS)
        act.dma_start(k.rw[:, :, :], k.dram["rw"]).then_inc(k.rw_loaded, 16)
        for b in range(2):
            act_split(k, At(q.g + b + LEAD))
        act_rstd(k, q.norm, lambda act: None)
        act.wait_ge(k.rw_loaded, 16)
        act.activation(self.repeats(k.rw_hi[:, :, :]), self.repeated(k), ACT.Copy).then_inc(k.rw_split, 1)
        act_prenorm(k, q.h, k.shift2[:, :], k.h_hi_buf)
        for b in range(2, 4):
            act_split(k, At(q.g + b + LEAD))
        act.wait_ge(k.logits_done, 1)
        act.activation(k.share_t[:, :], k.gbank[0][0:N_EXPERTS, :], ACT.Copy).then_inc(k.logits_copied, 1)
        act.wait_ge(k.logits_done, 2)
        act.activation(k.score[:, :, :, :].rearrange("p t g e -> p (t g e)"), k.gbank[1][:, 0:TT4 * N_EXPERTS], ACT.Sigmoid
                       ).then_inc(k.score_done, 1)
        for b in range(4, DC):
            act_split(k, At(q.g + b + LEAD))

    def dve(self, k, q):
        dve = k.nc.vector
        for b in range(2):
            dve_split(k, At(q.g + b + LEAD))
        dve.wait_ge(k.rw_split, 1)
        dve.tensor_tensor(self.repeats(k.rw_lo[:, :, :]), self.repeated(k), self.repeats(k.rw_hi[:, :, :].bitcast(F32)), ALU.subtract
                          ).then_inc(k.rw_split, 1)
        dve_prenorm(k, q.norm, q.h, k.x, k.gain2, k.shift2, k.h_hi_buf, k.h_lo_buf)
        for b in range(2, 4):
            dve_split(k, At(q.g + b + LEAD))
        self.dve_mod_group(k, q, 0)
        step = Order(dve, k.route)
        def then(ins):
            step(ins)
            step.wait()
        for i in range(PER_GROUP):
            then(dve.memset(k.rank[:, :, :, i:i + 1], float(PER_GROUP - 1 - i)))
            then(dve.memset(k.grank[:, :, i:i + 1], float(GROUPS - 1 - i)))
        dve_split(k, At(q.g + 4 + LEAD))
        dve.wait_ge(k.score_done, 1)
        bias = k.vec("router_b").rearrange("p (o g e) -> p o g e", o=1, g=GROUPS).to_broadcast([P, TT4, GROUPS, PER_GROUP])
        then(dve.tensor_tensor(k.choice[:, :, :, :], k.score[:, :, :, :], bias, ALU.add))
        for d in range(1, PER_GROUP):
            n = PER_GROUP - d
            ab = k.above[:, :, :, 0:n]
            then(dve.tensor_tensor(ab, k.choice[:, :, :, 0:n], k.choice[:, :, :, d:], ALU.is_ge))
            then(dve.tensor_tensor(k.rank[:, :, :, d:], k.rank[:, :, :, d:], ab, ALU.add))
            then(dve.tensor_tensor(k.rank[:, :, :, 0:n], k.rank[:, :, :, 0:n], ab, ALU.subtract))
        then(dve.tensor_scalar(k.keep4[:, :, :, :], k.rank[:, :, :, :], 1.5, None, ALU.is_lt))
        then(dve.tensor_tensor(k.above[:, :, :, :], k.keep4[:, :, :, :], k.choice[:, :, :, :], ALU.mult))
        then(dve.tensor_reduce(k.gsum[:, :, :], k.above[:, :, :, :], AX.X, ALU.add))
        for d in range(1, GROUPS):
            n = GROUPS - d
            ab = k.gabove[:, :, 0:n]
            then(dve.tensor_tensor(ab, k.gsum[:, :, 0:n], k.gsum[:, :, d:], ALU.is_ge))
            then(dve.tensor_tensor(k.grank[:, :, d:], k.grank[:, :, d:], ab, ALU.add))
            then(dve.tensor_tensor(k.grank[:, :, 0:n], k.grank[:, :, 0:n], ab, ALU.subtract))
        then(dve.tensor_scalar(k.grank[:, :, :], k.grank[:, :, :], 0.5, None, ALU.is_lt))
        then(dve.tensor_tensor(k.keep4[:, :, :, :], k.keep4[:, :, :, :],
                               k.grank[:, :, :].rearrange("p t (g o) -> p t g o", o=1).to_broadcast([P, TT4, GROUPS, PER_GROUP]), ALU.mult))
        then(dve.tensor_tensor(k.keep4[:, :, :, :], k.keep4[:, :, :, :], k.score[:, :, :, :], ALU.mult))
        then(dve.tensor_reduce(k.den[:, :], k.keep4[:, :, :, :], AX.XY, ALU.add))
        then(dve.reciprocal(k.den[:, :], k.den[:, :]))
        then(dve.tensor_tensor(k.keep4[:, :, :, :], k.keep4[:, :, :, :],
                               k.den[:, :].rearrange("p (t a b) -> p t a b", a=1, b=1).to_broadcast([P, TT4, GROUPS, PER_GROUP]), ALU.mult))
        assert step.n.base == k.ROUTE_STEPS, step.n.base
        dve_split(k, At(q.g + 5 + LEAD))
        dve.wait_ge(k.logits_done, 3)
        dve.tensor_copy(k.share_t[:, :], k.gbank[1][0:N_EXPERTS, :]).then_inc(k.share_used, 1)
        dve.wait_ge(k.share_used, 1)
        for n in range(4):
            dve.tensor_tensor(k.share_sel[:, 4 * n:4 * n + 4, :],
                              k.share_t[:, :].rearrange("p (o f) -> p o f", o=1).to_broadcast([N_EXPERTS, 4, T]),
                              k.ident[0:N_EXPERTS, 4 * n:4 * n + 4].rearrange("p (e o) -> p e o", o=1).to_broadcast([N_EXPERTS, 4, T]),
                              ALU.mult).then_inc(k.share_sel_ready, 1)
            if n < 2:
                dve_split(k, At(q.g + 6 + n + LEAD))
        self.dve_mod_group(k, q, 1)


class Moe(Phase):
    PASSES = N_EXPERTS // 4
    blocks = PASSES * (16 + DC)

    def advance(self, q):
        q.g += self.blocks
        q.a += 2 * N_EXPERTS
        q.sq += DC
        q.xc += DC

    def pe(self, k, q):
        for n in range(self.PASSES):
            pe_pass(k, q.g + n * 24, 8, q.a + 8 * n, e0=4 * n)

    def act(self, k, q):
        for n in range(self.PASSES):
            act_pass(k, q.g + n * 24, 8, q.a + 8 * n)
            end = n == self.PASSES - 1
            act_down(k, q.g + n * 24 + 16, q.sq if end else None, q.xc if end else None)

    def dve(self, k, q):
        for n in range(self.PASSES):
            end = n == self.PASSES - 1
            if end:
                k.nc.vector.wait_ge(k.mod_kept, 4 * DC // RING + HEADS + 2)
                k.nc.vector.tensor_tensor(k.mod[:, 5 * DC:6 * DC, 0], k.mod[:, 5 * DC:6 * DC, 0],
                                          k.vec("b_mod")[:, 5 * DC:6 * DC], ALU.add).then_inc(k.mod2, 1)
                k.nc.vector.wait_ge(k.mod2, 4)
            dve_pass(k, q.g + n * 24, 8, q.a + 8 * n, e0=4 * n)
            dve_down(k, q.g + n * 24 + 16, add=n > 0, sq0=q.sq if end else None,
                     into_x=(q.xc, k.mod[:, 5 * DC:6 * DC, 0]) if end else None)


class Ffn(Phase):
    blocks = sum(2 * nk + DC for nk in FF_SEGMENTS)

    def advance(self, q):
        q.g += self.blocks
        q.a += D_FF // P
        q.f += D_FF // P
        q.sq += DC

    def passes(self, q):
        g, a, f = q.g, q.a, q.f
        for s, nk in enumerate(FF_SEGMENTS):
            yield g, nk, a, f, s == 0, s == len(FF_SEGMENTS) - 1
            g, a, f = g + 2 * nk + DC, a + nk, f + nk

    def pe(self, k, q):
        for g, nk, a, f, first, last in self.passes(q):
            pe_pass(k, g, nk, a, begun=first)

    def counts(self, k, q):
        k.n_first = q.first - RING
        k.n_unscaled = 2 * (q.f // (D_FF // P) + 1)

    def act(self, k, q):
        self.counts(k, q)
        for g, nk, a, f, first, last in self.passes(q):
            act_ffn_pass(k, g, nk, a, f, first)
            act_down(k, g + 2 * nk, q.sq if last else None)

    def dve(self, k, q):
        self.counts(k, q)
        for g, nk, a, f, first, last in self.passes(q):
            dve_ffn_pass(k, g, nk, a, f, first)
            dve_down(k, g + 2 * nk, add=not first, sq0=q.sq if last else None)


A_HEADS = 4
LAM_INIT = 0.8 - 0.6 * math.exp(-0.3 * 0)
B_HEADS = 8
BH = 64
BC = 4
RC = P
RN = T // RC
KAPPA = math.exp(-0.5)
LN_SCALE = 2.0 ** 17
LEVELS = [2, 4, 8, 16, 32, 64]
PREP_MM = 5


class EvenProj(Phase):
    blocks = 26

    def advance(self, q):
        q.g += self.blocks

    def layout(self, k, ctx):
        base = k.arena["acc"][0]
        def put(name, at, shape, dt=F32):
            size = int(np.prod(shape[1:])) * (1 if dt == I8 else 4)
            assert base + at + size <= k.limit, (name, base + at + size, k.limit)
            t = k.sb(name, shape, dt, at=base + at)
            return t, at + -(-size // 32) * 32
        KB = 1024
        k.rkv, _ = put("rkv", 0, [P, 3 * BC, T])
        k.qkv, _ = put("qkv", 24 * KB, [P, 12, T])
        k.ar, _ = put("ar", 24 * KB, [P, BC, 2, T])
        k.bt_y, _ = put("bt_y", 40 * KB, [P, BC, T])
        k.gin, _ = put("gin", 48 * KB, [P, T])
        k.lvl_mask, at = put("lvl_mask", 50 * KB, [P, len(LEVELS) + 1, 2, P], I8)
        k.tri, at = put("tri", at, [P, 3, P], I8)
        k.mcol, at = put("mcol", at, [P, BC, RN])
        k.rhos, at = put("rhos", at, [P, RN, BC])
        mats = at
        k.mat_at, at = put("mat_at", at, [P, B_HEADS, P])
        k.inv, at = put("inv", at, [P, B_HEADS, P])
        k.inv_t, at = put("inv_t", at, [P, B_HEADS, P])
        k.zst, at = put("zst", mats, [P, 2, T + 1])
        at = mats
        k.cumw, at = put("cumw", at, [P, T])
        k.ab, at = put("ab", at, [P, T])
        k.e_pos, at = put("e_pos", at, [P, RN * (RC + 1)])
        k.e_neg, at = put("e_neg", at, [P, T])
        k.kkr, at = put("kkr", at, [P, T])
        k.tmp1, at = put("tmp1", at, [P, T])
        k.tmp2, at = put("tmp2", at, [P, T])
        hb, ab = k.arena["h_hi_buf"][0], k.arena["a_hi_buf"][0]
        def putat(name, at, shape):
            return k.sb(name, shape, F32, at=at), at + int(np.prod(shape[1:])) * 4
        at = hb
        k.vtok_a, at = putat("vtok_a", at, [P, T // P, T])
        k.sc, at = putat("sc", at, [P, 2, 2, T])
        k.pn, at = putat("pn", at, [P, 2, T])
        k.ptr, at = putat("ptr", at, [P, 2, T])
        k.dist, at = putat("dist", at, [P, T])
        k.bias_h, at = putat("bias_h", at, [P, T])
        k.oa, at = putat("oa", at, [P, T])
        k.att_small, at = putat("att_small", at, [P, 64])
        assert at <= hb + 32 * KB
        k.vt, at = putat("vt", hb, [P, RN, T])
        k.btok, at = putat("btok", at, [P, RN, T])
        k.ktokr, at = putat("ktokr", at, [P, RN, T])
        k.mat_x, at = putat("mat_x", at, [P, B_HEADS, P])
        k.t_ak, at = putat("t_ak", at, [P, B_HEADS, P])
        assert at <= hb + 32 * KB
        k.t_rb, at = putat("t_rb", ab + 8 * KB, [P, B_HEADS, P])
        k.t_rk, at = putat("t_rk", at, [P, B_HEADS, P])
        at = k.arena["a_lo_buf"][0] + 8 * KB
        k.sqa, _ = putat("sqa", at, [P, 2, T])
        k.u_sb, at = putat("u_sb", at, [P, B_HEADS * BH])
        k.rhs_sb, at = putat("rhs_sb", at, [P, B_HEADS * BH])
        k.st, at = putat("st", at, [P, BC, BH])
        k.st2, at = putat("st2", at, [P, BC, BH])
        k.gup, at = putat("gup", at, [P, T])
        k.waup, _ = putat("waup", ab + 8 * KB, [P, T])
        k.wa, _ = putat("wa", ab + 10 * KB, [P, T])
        k.lam_in, _ = putat("lam_in", k.arena["a_lo_buf"][0] + 8 * KB, [P, 4 * BH])
        k.up_loaded, k.lam_loaded, k.shift_d, k.shifted = k.sems("up_loaded lam_loaded shift_d shifted")

    def pe(self, k, q):
        pe = k.nc.tensor
        h = lambda t: (k.h_hi_buf[:, t, :], k.h_lo_buf[:, t, :])
        with pe.Fori(0, 5) as it:
            for b in range(RING):
                pe_block(k, At(q.g + RING + b, RING, it), DC, h)
        for b in range(24, 26):
            pe_block(k, At(q.g + b), DC, h)

    def act(self, k, q):
        act = k.nc.scalar
        act.wait_ge(k.block_done, q.g)
        act.dma_start(k.waup[:, :], k.dram["waup"]).then_inc(k.up_loaded, 16)
        act.dma_start(k.gup[:, :], k.dram["gup"]).then_inc(k.up_loaded, 16)
        act.dma_start(k.lam_in[:, :], k.dram["lam"]).then_inc(k.lam_loaded, 16)
        with act.Fori(0, 5) as it:
            for b in range(RING):
                act_split(k, At(q.g + RING + b, RING, it) + LEAD)
        for b in range(24, 26):
            act_split(k, At(q.g + b) + LEAD)

    def dve(self, k, q):
        dve = k.nc.vector
        rstd = k.rstd[:, :].rearrange("p (o f) -> p o f", o=1)
        with dve.Fori(0, 2) as it:
            for b in range(RING):
                g = At(q.g + RING + b, RING, it)
                dve_split(k, g + LEAD)
                wait(dve, k.block_done, g + 1)
                dve.tensor_tensor(k.qkv[:, bass.ds(At(RING + b, RING, it).value, 1), :],
                                  k.bank[g.slot][:, :].rearrange("p (o f) -> p o f", o=1), rstd, ALU.mult).then_inc(k.bank_free, 1)
        dve.memset(k.zst[:, :, 0:1], 0.0).then_inc(k.shifted, 1)
        dve.wait_ge(k.shifted, 1)
        mu = k.vec("mu")

        def shifted_block(g, i, dst, col):
            z = k.zst[:, i.base % 2, :].rearrange("p (o f) -> p o f", o=1)
            dve_split(k, g + LEAD)
            wait(dve, k.block_done, g + 1)
            if i.base >= 2:
                wait(dve, k.shifted, i)
            dve.tensor_tensor(z[:, :, 1:], k.bank[g.slot][:, :].rearrange("p (o f) -> p o f", o=1), rstd, ALU.mult
                              ).then_inc(k.bank_free, 1)
            wait(dve, k.bank_free, g + 1)
            dve.tensor_tensor(dst, z[:, :, 0:T], z[:, :, 1:], ALU.subtract).then_inc(k.shift_d, 1)
            wait(dve, k.shift_d, i + 1)
            dve.scalar_tensor_tensor(dst, dst, col, z[:, :, 1:], ALU.mult, ALU.add).then_inc(k.shifted, 1)

        for b in range(RING):
            shifted_block(At(q.g + 12 + b), At(b), k.rkv[:, b:b + 1, :], mu[:, b:b + 1])
        with dve.Fori(0, 2) as it:
            for b in range(RING):
                j = At(RING + b, RING, it)
                shifted_block(At(q.g + 16 + b, RING, it), j, k.rkv[:, bass.ds(j.value, 1), :], mu[:, bass.ds(j.value, 1)])
        for n, buf in enumerate((k.wa, k.gin)):
            shifted_block(At(q.g + 24 + n), At(12 + n), buf[:, :].rearrange("p (o f) -> p o f", o=1), mu[:, 12 + n:13 + n])


class Attention(Phase):
    blocks = 0
    UNITS = [(h, b) for h in range(A_HEADS) for b in range(T // P)]

    def advance(self, q):
        q.norm += A_HEADS

    def layout(self, k, ctx):
        (k.dist_ready, k.bias_ready, k.lam_ready, k.sc_full, k.sc_biased, k.mx_ready, k.p_exp
         ) = k.sems("dist_ready bias_ready lam_ready sc_full sc_biased mx_ready p_exp")
        (k.rinv, k.p_neg, k.p_ready, k.ptr_full, k.ptr_copied, k.pv_done, k.oa_copied
         ) = k.sems("rinv p_neg p_ready ptr_full ptr_copied pv_done oa_copied")
        (k.oa_sq, k.oa_scaled, k.oa_hi, k.at_parts, k.vt_full, k.vt_copied, k.lam_exp
         ) = k.sems("oa_sq oa_scaled oa_hi at_parts vt_full vt_copied lam_exp")

    def pool(self, k, q):
        pool = k.nc.gpsimd
        pool.wait_ge(k.block_done, q.g)
        pool.iota(k.dist[:, :], pattern=[[1, T]], base=-(T - P), channel_multiplier=-1,
                  allow_small_or_imprecise_dtypes=True).then_inc(k.dist_ready, 1)

    def pe(self, k, q):
        pe = k.nc.tensor
        for n in range(T // P):
            if n >= 2:
                pe.wait_ge(k.vt_copied, n - 1)
            else:
                pe.wait_ge(k.bank_free, q.g)
            for c in range(4):
                last = pe.transpose(k.gbank[n % 2][:, c * P:(c + 1) * P], k.qkv[:, 8 + c, n * P:(n + 1) * P], k.ident[:, :])
            last.then_inc(k.vt_full, 1)
        units = self.UNITS

        def scores(u):
            h, b = units[u]
            if u >= 2:
                pe.wait_ge(k.sc_biased, 2 * (u - 1))
            for m in range(2):
                half = slice(m * BH, (m + 1) * BH)
                last = pe.matmul(k.bank[2 * (u % 2) + m][:, 0:(b + 1) * P], k.qkv[half, h, b * P:(b + 1) * P],
                                 k.qkv[half, 4 + h, 0:(b + 1) * P], start=True, stop=True)
                last.then_inc(k.sc_full, 1)

        def values(u):
            h, b = units[u]
            pe.wait_ge(k.p_ready, u + 1)
            if u >= 2:
                pe.wait_ge(k.ptr_copied, u - 1)
            else:
                pe.wait_ge(k.vt_copied, T // P)
            for j in range(b + 1):
                last = pe.transpose(k.gbank[u % 2][:, j * P:(j + 1) * P], k.pn[:, u % 2, j * P:(j + 1) * P], k.ident[:, :])
            last.then_inc(k.ptr_full, 1)

        def weigh(u):
            h, b = units[u]
            pe.wait_ge(k.ptr_copied, u + 1)
            if b == 0 and h > 0:
                pe.wait_ge(k.oa_copied, h)
            for j in range(b + 1):
                last = pe.matmul(k.cbank[:, b * P:(b + 1) * P], k.vtok_a[:, j, h * P:(h + 1) * P], k.ptr[:, u % 2, j * P:(j + 1) * P],
                                 start=(j == 0), stop=(j == b))
            last.then_inc(k.pv_done, 1)
            if b == T // P - 1:
                pe.wait_ge(k.oa_sq, h + 1)
                pe.wait_ge(k.rstd_ready, q.norm + h)
                pe.matmul(k.nbank[:, :], k.ones[:, :], k.sqa[:, h % 2, :], start=True, stop=True).then_inc(k.norm_sum, 1)

        N = len(units)
        for u in range(N + 2):
            if u < N:
                scores(u)
            if 1 <= u <= N:
                values(u - 1)
            if u >= 2:
                weigh(u - 2)

    def act(self, k, q):
        act = k.nc.scalar
        units = self.UNITS
        act.wait_ge(k.lam_ready, 2)
        act.activation(k.att_small[:, 0:2], k.att_small[:, 0:2], ACT.Exp).then_inc(k.lam_exp, 1)
        for n in range(T // P):
            act.wait_ge(k.vt_full, n + 1)
            act.activation(k.vtok_a[:, n, :], k.gbank[n % 2][:, :], ACT.Copy).then_inc(k.vt_copied, 1)

        def exps(u):
            h, b = units[u]
            for m in range(2):
                act.wait_ge(k.mx_ready, 2 * u + m + 1)
                act.activation(k.sc[:, u % 2, m, 0:(b + 1) * P], k.sc[:, u % 2, m, 0:(b + 1) * P], ACT.Exp,
                               bias=k.att_small[:, 8 + 4 * (u % 2) + m:9 + 4 * (u % 2) + m],
                               accum_out=k.att_small[:, 16 + 4 * (u % 2) + m:17 + 4 * (u % 2) + m]).then_inc(k.p_exp, 1)

        def copies(u):
            h, b = units[u]
            act.wait_ge(k.ptr_full, u + 1)
            if u >= 2:
                act.wait_ge(k.pv_done, u - 1)
            act.activation(k.ptr[:, u % 2, 0:(b + 1) * P], k.gbank[u % 2][:, 0:(b + 1) * P], ACT.Copy).then_inc(k.ptr_copied, 1)

        def head(h):
            act.wait_ge(k.oa_copied, h + 1)
            if h >= 2:
                act.wait_ge(k.norm_sum, q.norm + h - 1)
            act.activation(k.sqa[:, h % 2, :], k.oa[:, :], ACT.Square).then_inc(k.oa_sq, 1)
            act_rstd(k, q.norm + h, lambda act: wait(act, k.oa_scaled, h), scale=1.0 / P)
            act.wait_ge(k.oa_scaled, h + 1)
            act.activation(k.a_hi_buf[:, h, :], k.oa[:, :], ACT.Copy).then_inc(k.oa_hi, 1)

        N = len(units)
        for u in range(N + 2):
            if u < N:
                exps(u)
            if 1 <= u <= N:
                copies(u - 1)
            if u >= 5 and u % 4 == 1:
                head((u - 2) // 4)

    def dve(self, k, q):
        dve = k.nc.vector
        units = self.UNITS
        dve.wait_ge(k.lam_loaded, 16)
        lam = k.lam_in[:, :].rearrange("p (a b d) -> p a b d", a=2, b=2)
        prod = k.oa[:, 0:2 * BH].rearrange("p (a d) -> p a d", a=2)
        dve.wait_ge(k.block_done, q.g)
        dve.tensor_tensor(prod, lam[:, :, 0, :], lam[:, :, 1, :], ALU.mult).then_inc(k.lam_ready, 1)
        dve.wait_ge(k.lam_ready, 1)
        dve.tensor_reduce(k.att_small[:, 0:2], prod, AX.X, ALU.add).then_inc(k.lam_ready, 1)
        dve.wait_ge(k.lam_exp, 1)
        dve.tensor_tensor(k.att_small[:, 2:3], k.att_small[:, 0:1], k.att_small[:, 1:2], ALU.subtract).then_inc(k.lam_ready, 1)
        dve.wait_ge(k.lam_ready, 3)
        dve.tensor_scalar(k.att_small[:, 2:3], k.att_small[:, 2:3], LAM_INIT, None, ALU.add).then_inc(k.lam_ready, 1)
        dve.tensor_scalar(k.att_small[:, 4:5], k.vec("subln"), 1.0 - LAM_INIT, None, ALU.mult).then_inc(k.lam_ready, 1)
        dve.wait_ge(k.lam_ready, 5)
        dve.wait_ge(k.dist_ready, 1)
        dve.scalar_tensor_tensor(k.dist[:, :], k.dist[:, :], -1.0, k.dist[:, :], ALU.mult, ALU.min).then_inc(k.dist_ready, 1)
        dve.wait_ge(k.dist_ready, 2)
        dve.memset(k.dist[0:CH, T - CH:T], -1e30).then_inc(k.dist_ready, 1)
        dve.wait_ge(k.dist_ready, 3)

        def bias(u):
            h, b = units[u]
            w = (b + 1) * P
            if b == 0:
                if h > 0:
                    dve.wait_ge(k.sc_biased, 2 * u)
                dve.tensor_scalar(k.bias_h[:, :], k.dist[:, :], 2.0 ** (-8.0 / A_HEADS * (h + 1)), None, ALU.mult).then_inc(k.bias_ready, 1)
                dve.wait_ge(k.bias_ready, h + 1)
            for m in range(2):
                dve.wait_ge(k.sc_full, 2 * u + m + 1)
                if u >= 2:
                    dve.wait_ge(k.p_ready, u - 1)
                dve.scalar_tensor_tensor(k.sc[:, u % 2, m, 0:w], k.bank[2 * (u % 2) + m][:, 0:w], BH ** -0.5,
                                         k.bias_h[:, T - w:T], ALU.mult, ALU.add).then_inc(k.sc_biased, 1)
            for m in range(2):
                dve.wait_ge(k.sc_biased, 2 * u + m + 1)
                dve.tensor_reduce(k.att_small[:, 8 + 4 * (u % 2) + m:9 + 4 * (u % 2) + m], k.sc[:, u % 2, m, 0:w], AX.X, ALU.max,
                                  negate=True).then_inc(k.mx_ready, 1)

        def mix(u):
            h, b = units[u]
            w = (b + 1) * P
            s = 16 + 4 * (u % 2)
            dve.wait_ge(k.p_exp, 2 * u + 2)
            dve.reciprocal(k.att_small[:, s:s + 2], k.att_small[:, s:s + 2]).then_inc(k.rinv, 1)
            dve.wait_ge(k.rinv, 2 * u + 1)
            dve.tensor_tensor(k.att_small[:, s + 1:s + 2], k.att_small[:, s + 1:s + 2], k.att_small[:, 2:3], ALU.mult).then_inc(k.rinv, 1)
            dve.wait_ge(k.rinv, 2 * u + 2)
            dve.tensor_scalar(k.sc[:, u % 2, 1, 0:w], k.sc[:, u % 2, 1, 0:w], k.att_small[:, s + 1:s + 2], None, ALU.mult).then_inc(k.p_neg, 1)
            dve.wait_ge(k.p_neg, u + 1)
            if u >= 2:
                dve.wait_ge(k.ptr_full, u - 1)
            dve.scalar_tensor_tensor(k.pn[:, u % 2, 0:w], k.sc[:, u % 2, 0, 0:w], k.att_small[:, s:s + 1], k.sc[:, u % 2, 1, 0:w],
                                     ALU.mult, ALU.subtract).then_inc(k.p_ready, 1)

        def head(h):
            dve.wait_ge(k.pv_done, 4 * (h + 1))
            if h > 0:
                dve.wait_ge(k.at_parts, h)
            dve.tensor_copy(k.oa[:, :], k.cbank[:, :]).then_inc(k.oa_copied, 1)
            dve.wait_ge(k.rstd_ready, q.norm + h + 1)
            dve.scalar_tensor_tensor(k.oa[:, :], k.oa[:, :], k.att_small[:, 4:5], k.rstd[:, :], ALU.mult, ALU.mult).then_inc(k.oa_scaled, 1)
            dve.wait_ge(k.oa_hi, h + 1)
            dve.tensor_tensor(k.a_lo_buf[:, h, :], k.oa[:, :], k.a_hi_buf[:, h, :].bitcast(F32), ALU.subtract).then_inc(k.at_parts, 1)

        N = len(units)
        for u in range(N + 2):
            if u < N:
                bias(u)
            if 1 <= u <= N:
                mix(u - 1)
            if u >= 5 and u % 4 == 1:
                head((u - 2) // 4)


class Steps:

    def __init__(self, sem, *names):
        self.sem, self.names = sem, " ".join(names).split()

    def done(self, rep, name):
        return rep * len(self.names) + self.names.index(name) + 1


def stage(eng, steps, rep):
    at = [0]

    def do(name, ins):
        assert steps.names[at[0]] == name, (name, steps.names[at[0]])
        at[0] += 1
        ins.then_inc(steps.sem, 1)

    def after(other, name, r=None):
        r = rep if r is None else r
        if r >= 0:
            eng.wait_ge(other.sem, other.done(r, name))
    return do, after


class Rwkv(Phase):
    blocks = 0

    def advance(self, q):
        pass

    def layout(self, k, ctx):
        S = lambda name, *n: Steps(k.sem("s_" + name), *n)
        k.pp = S("pp", "w a ss bs")
        k.pa = S("pa", "sigw siga kksq ln rn epos ecol eneg")
        k.pd = S("pd", "kkr", *[f"scan{n}" for n in range(RN)], "mcol sub rho ssm am kp kkn rt at beta bt rk kt bon")
        (k.tk_full, k.tk_copied, k.rw_start, k.rho_exp, k.rw_masks, k.rw_zero
         ) = k.sems("tk_full tk_copied rw_start rho_exp rw_masks rw_zero")
        lv = range(1, len(LEVELS) + 1)
        k.cp = S("cp", "a0 a1 at0 at1 ak0 ak1 rk0 rk1 rb0 rb1", *[f"x{l}0 x{l}1 y{l}0 z{l}0 y{l}1 z{l}1" if l < len(LEVELS) else
                                                           f"x{l}0 x{l}1 z{l}0 z{l}1" for l in lv], "rhs0 rhs1 u y0 y1 p")
        k.ca = S("ca", "i0 i1 it0 it1", *[f"x{l}0 x{l}1" for l in lv], "rhs0 rhs1 y0 y1")
        k.cd = S("cd", "a0 a1 at0 it0 at1 it1 ak0 ak1 rk0 rk1 rb0 rb1", *[f"y{l}0 z{l}0 y{l}1 z{l}1" if l < len(LEVELS) else
                                                                     f"z{l}0 z{l}1" for l in lv], "u sp s")
        each = lambda names: " ".join(f"{name}{c}" for name in names.split() for c in range(BC))
        k.fp = S("fp", each("mean var g"))
        k.fa = S("fa", each("sq ln rs hi"))
        k.fd = S("fd", each("yc"), *[f"yw{c} yb{c} yg{c}" + (f" lo{c - 1}" if c else "") for c in range(BC)], f"lo{BC - 1}")

    def pool(self, k, q):
        pool = k.nc.gpsimd
        done = Order(pool, k.rw_masks)
        def then(ins):
            done(ins)
            done.wait()
        pool.wait_ge(k.block_done, q.g)
        then(pool.memset(k.tri[:, :, :], 1))
        for i, (sign, base) in enumerate(((1, -1), (-1, -1), (-1, 0))):
            then(pool.affine_select(out=k.tri[:, i, :], in_=k.tri[:, i, :], compare_op=ALU.is_ge, fill=0.0, base=base,
                                    pattern=[[-sign, P]], channel_multiplier=sign))
        then(pool.memset(k.lvl_mask[:, :, :, :], 1))
        for l, b in enumerate([1] + LEVELS):
            m = k.lvl_mask[:, l, 0, :].rearrange("p (i two s) -> p i two s", two=2, s=b)
            mt = k.lvl_mask[:, l, 1, :].rearrange("p (i two s) -> p i two s", two=2, s=b)
            n = P // (2 * b)
            then(pool.affine_select(out=m, in_=m, compare_op=ALU.is_ge, fill=0.0, base=-b,
                                    pattern=[[-2 * b, n], [-b * 0 - 10000, 2], [0, b]], channel_multiplier=1))
            then(pool.affine_select(out=m, in_=m, compare_op=ALU.is_ge, fill=0.0, base=2 * b - 1,
                                    pattern=[[2 * b, n], [0, 2], [0, b]], channel_multiplier=-1))
            then(pool.affine_select(out=mt, in_=mt, compare_op=ALU.is_ge, fill=0.0, base=-10000,
                                    pattern=[[-2 * b, n], [10000, 2], [0, b]], channel_multiplier=1))
            then(pool.affine_select(out=mt, in_=mt, compare_op=ALU.is_ge, fill=0.0, base=b - 1,
                                    pattern=[[2 * b, n], [0, 2], [0, b]], channel_multiplier=-1))
        self.n_masks = done.n.base
        pool.wait_ge(k.pd.sem, BC * len(k.pd.names))
        pool.wait_ge(k.pa.sem, BC * len(k.pa.names))
        pool.wait_ge(k.pp.sem, BC * len(k.pp.names))
        zero = Order(pool, k.rw_zero)
        for buf in (k.mat_at, k.t_ak, k.t_rb, k.t_rk):
            zero(pool.memset(buf[:, :, :], 0.0))
            zero.wait()

    def pe(self, k, q):
        pe = k.nc.tensor
        pe.wait_ge(k.up_loaded, 32)
        pe.wait_ge(k.rw_start, 2)
        for c in range(BC):
            do, after = stage(pe, k.pp, c)
            col = slice(c * P, (c + 1) * P)
            after(k.pa, "sigw", c - 1)
            do("w", pe.matmul(k.bank[0][:, :], k.waup[0:BH, col], k.wa[0:BH, :], start=True, stop=True))
            after(k.pa, "siga", c - 1)
            do("a", pe.matmul(k.bank[1][:, :], k.waup[BH:P, col], k.wa[BH:P, :], start=True, stop=True))
            after(k.pa, "kksq")
            after(k.pd, "ssm", c - 1)
            do("ss", pe.matmul(k.bank[2][:, :], k.pair_ones[:, :], k.tmp1[:, :], start=True, stop=True))
            after(k.pd, "rk")
            after(k.pd, "bon", c - 1)
            do("bs", pe.matmul(k.bank[3][:, :], k.pair_ones[:, :], k.tmp1[:, :], start=True, stop=True))
        n = 0
        after(k.pd, "kt")
        for src in (lambda c: k.rkv[:, 2 * BC + c], lambda c: k.bt_y[:, c], lambda c: k.rkv[:, BC + c]):
            for t in range(RN):
                if n >= 2:
                    pe.wait_ge(k.tk_copied, n - 1)
                for c in range(BC):
                    last = pe.transpose(k.gbank[n % 2][:, c * P:(c + 1) * P], src(c)[:, t * RC:(t + 1) * RC], k.ident[:, :])
                last.then_inc(k.tk_full, 1)
                n += 1
        pe.wait_ge(k.tk_copied, n)
        after(k.pd, "bon")
        pe.wait_ge(k.rho_exp, 1)
        banks = k.bank + k.gbank + [k.cbank, k.nbank]
        for t in range(RN):
            self.pe_chunk(k, t, banks)
        do, after = stage(pe, k.fp, 0)
        after(k.ca, "y1", RN - 1)
        for c in range(BC):
            do(f"mean{c}", pe.matmul(k.bank[c][:, :], k.pair_ones[:, :], k.bt_y[:, c, :], start=True, stop=True))
        for c in range(BC):
            after(k.fa, f"sq{c}")
            do(f"var{c}", pe.matmul(self.var_bank(k, c)[:, :], k.pair_ones[:, :], self.norm_buf(k, c)[:, :], start=True, stop=True))
        for c in range(BC):
            after(k.fd, f"yc{c}")
            do(f"g{c}", pe.matmul(k.bank[c][:, :], k.gup[:, c * P:(c + 1) * P], k.gin[:, :], start=True, stop=True))

    @staticmethod
    def var_bank(k, c):
        return (k.gbank[0], k.gbank[1], k.cbank, k.nbank)[c]

    @staticmethod
    def norm_buf(k, c):
        return (k.tmp1, k.tmp2, k.kkr, k.cumw)[c]

    def pe_chunk(self, k, t, banks):
        pe = k.nc.tensor
        do, after = stage(pe, k.cp, t)
        tok = slice(t * RC, (t + 1) * RC)
        ar = lambda i: (lambda c, half: k.ar[half, c, i, tok])
        b, kt = (lambda c, half: k.bt_y[half, c, tok]), (lambda c, half: k.rkv[half, BC + c, tok])
        kinds = [("a", ar(0), b), ("at", b, ar(0)), ("ak", kt, ar(0)), ("rk", kt, ar(1)), ("rb", b, ar(1))]
        for i, (name, lhs, rhs) in enumerate(kinds):
            for p in range(2):
                half = slice(p * BH, (p + 1) * BH)
                n = (2 * i + p) % 8
                if i == 0 and p == 0 and t > 0:
                    after(k.ca, "y1", t - 1)
                    after(k.cd, "u", t - 1)
                    if t - 1 < RN - 1:
                        after(k.cd, "s", t - 1)
                if i == 4:
                    after(k.cd, f"a{p}")
                for c in range(BC):
                    last = pe.matmul(banks[n][:, c * P:(c + 1) * P], lhs(c, half), rhs(c, half), start=True, stop=True)
                do(f"{name}{p}", last)
        grp = lambda buf, p, c: buf[:, p * BC + c, :]
        X, Y, Z = k.bank[0:2], k.bank[2:4], k.gbank
        for l in range(1, len(LEVELS) + 1):
            full = l < len(LEVELS)
            for p in range(2):
                if l == 1:
                    after(k.cd, f"rb{p}")
                    after(k.cd, f"a{p}")
                    after(k.cd, f"it{p}")
                else:
                    after(k.cd, f"y{l - 1}{p}")
                for c in range(BC):
                    last = pe.matmul(X[p][:, c * P:(c + 1) * P], grp(k.mat_at, p, c), grp(k.inv, p, c), start=True, stop=True)
                do(f"x{l}{p}", last)
            for p in range(2):
                after(k.ca, f"x{l}{p}")
                if l == 1:
                    after(k.cd, f"ak{p}")
                    after(k.cd, f"at{p}")
                else:
                    after(k.cd, f"z{l - 1}{p}")
                if full:
                    for c in range(BC):
                        last = pe.matmul(Y[p][:, c * P:(c + 1) * P], grp(k.inv_t, p, c), grp(k.mat_x, p, c), start=True, stop=True)
                    do(f"y{l}{p}", last)
                for c in range(BC):
                    last = pe.matmul(Z[p][:, c * P:(c + 1) * P], grp(k.mat_x, p, c), grp(k.inv_t, p, c), start=True, stop=True)
                do(f"z{l}{p}", last)
        L = len(LEVELS)
        for p in range(2):
            half = slice(p * BH, (p + 1) * BH)
            after(k.cd, f"rk{p}")
            after(k.cd, f"ak{p}")
            out = (k.cbank, k.nbank)[p]
            for c in range(BC):
                h = 2 * c + p
                o = out[:, c * BH:(c + 1) * BH]
                if t > 0:
                    pe.matmul(o, k.ar[half, c, 0, tok], k.st[half, c, :], start=True, stop=False)
                last = pe.matmul(o, grp(k.t_ak, p, c), k.vt[:, t, h * BH:(h + 1) * BH], start=(t == 0), stop=True)
            do(f"rhs{p}", last)
        after(k.cd, f"z{L}1")
        after(k.cd, f"z{L}0")
        for p in range(2):
            after(k.ca, f"rhs{p}")
            for c in range(BC):
                i = p * BC + c
                last = pe.matmul(k.gbank[0][:, i * BH:(i + 1) * BH], grp(k.inv_t, p, c), k.rhs_sb[:, i * BH:(i + 1) * BH],
                                 start=True, stop=True)
        do("u", last)
        after(k.cd, "u")
        for p in range(2):
            half = slice(p * BH, (p + 1) * BH)
            after(k.cd, f"rb{p}")
            after(k.cd, f"y{L - 1}{p}")
            for c in range(BC):
                h, i = 2 * c + p, p * BC + c
                o = Y[p][half, c * P:(c + 1) * P]
                if t > 0:
                    pe.matmul(o, k.st[half, c, :], k.ar[half, c, 1, tok], start=True, stop=False)
                pe.matmul(o, k.u_sb[:, i * BH:(i + 1) * BH], grp(k.t_rb, p, c), start=(t == 0), stop=False)
                last = pe.matmul(o, k.vt[:, t, h * BH:(h + 1) * BH], grp(k.t_rk, p, c), start=False, stop=True)
            do(f"y{p}", last)
        for p in range(2):
            half = slice(p * BH, (p + 1) * BH)
            for c in range(BC):
                h, i = 2 * c + p, p * BC + c
                o = k.gbank[1][half, c * BH:(c + 1) * BH]
                pe.matmul(o, k.btok[:, t, h * BH:(h + 1) * BH], k.u_sb[:, i * BH:(i + 1) * BH], start=True, stop=False)
                last = pe.matmul(o, k.ktokr[:, t, h * BH:(h + 1) * BH], k.vt[:, t, h * BH:(h + 1) * BH], start=False, stop=True)
        do("p", last)

    def act(self, k, q):
        act = k.nc.scalar
        act.wait_ge(k.shifted, 15)
        act.activation(k.wa[0:BH, :], k.wa[0:BH, :], ACT.Tanh).then_inc(k.rw_start, 1)
        act.activation(k.gin[:, :], k.gin[:, :], ACT.Sigmoid).then_inc(k.rw_start, 1)
        chunks = lambda b: b.rearrange("p (n c) -> p n c", n=RN)
        ep = chunks(k.e_pos[:, :])
        for c in range(BC):
            do, after = stage(act, k.pa, c)
            after(k.pp, "w")
            after(k.pd, "kkn", c - 1)
            do("sigw", act.activation(k.tmp2[:, :], k.bank[0][:, :], ACT.Sigmoid, bias=k.vec("w0")[:, c:c + 1]))
            after(k.pp, "a")
            after(k.pd, "bt", c - 1)
            do("siga", act.activation(k.ab[:, :], k.bank[1][:, :], ACT.Sigmoid, bias=k.vec("a0")[:, c:c + 1]))
            after(k.pd, "kkr")
            after(k.pp, "bs", c - 1)
            do("kksq", act.activation(k.tmp1[:, :], k.kkr[:, :], ACT.Square))
            after(k.pd, "ssm")
            do("ln", act.activation(k.tmp2[:, :], k.tmp2[:, :], ACT.Ln, scale=LN_SCALE))
            after(k.pa, "ln")
            do("rn", act.activation(k.tmp2[:, :], k.tmp2[:, :], ACT.Exp, scale=-0.5))
            after(k.pd, "rho")
            after(k.pd, "at", c - 1)
            do("epos", act.activation(ep[:, :, 1:], chunks(k.cumw[:, :]), ACT.Exp, scale=-KAPPA))
            do("ecol", act.activation(ep[:, :, 0], k.mcol[:, c, :], ACT.Exp, scale=KAPPA))
            after(k.pd, "kt", c - 1)
            do("eneg", act.activation(k.e_neg[:, :], k.cumw[:, :], ACT.Exp, scale=KAPPA))
        act.activation(k.rhos[:, 0:RN - 1, :], k.rhos[:, 0:RN - 1, :], ACT.Exp, scale=-KAPPA).then_inc(k.rho_exp, 1)
        n = 0
        for dst in (k.vt, k.btok, k.ktokr):
            for t in range(RN):
                act.wait_ge(k.tk_full, n + 1)
                act.activation(dst[:, t, :], k.gbank[n % 2][:, :], ACT.Copy).then_inc(k.tk_copied, 1)
                n += 1
        halves = lambda b, p: b[:, p * BC:(p + 1) * BC, :]
        idb = k.ident[:, :].rearrange("p (o f) -> p o f", o=1).to_broadcast([P, BC, P])
        as4 = lambda bank: bank[:, :].rearrange("p (h f) -> p h f", f=P)
        for t in range(RN):
            do, after = stage(act, k.ca, t)
            if t == 0:
                after(k.pd, "bon", BC - 1)
                after(k.pp, "bs", BC - 1)
            for p in range(2):
                after(k.cp, "x60", t - 1)
                after(k.cp, "x61", t - 1)
                do(f"i{p}", act.activation(halves(k.inv, p), idb, ACT.Copy))
            for p in range(2):
                after(k.cp, "u", t - 1)
                do(f"it{p}", act.activation(halves(k.inv_t, p), idb, ACT.Copy))
            for l in range(1, len(LEVELS) + 1):
                for p in range(2):
                    after(k.cp, f"x{l}{p}")
                    do(f"x{l}{p}", act.activation(halves(k.mat_x, p), as4(k.bank[p]), ACT.Copy))
            for p in range(2):
                after(k.cp, f"rhs{p}")
                do(f"rhs{p}", act.activation(k.rhs_sb[:, p * 256:(p + 1) * 256], (k.cbank, k.nbank)[p][:, 0:256], ACT.Copy))
            for p in range(2):
                half = slice(p * BH, (p + 1) * BH)
                after(k.cp, f"y{p}")
                do(f"y{p}", act.activation(k.bt_y[half, :, t * RC:(t + 1) * RC],
                                           k.bank[2 + p][half, :].rearrange("p (c f) -> p c f", f=RC), ACT.Copy))
        do, after = stage(act, k.fa, 0)
        for c in range(BC):
            after(k.fd, f"yc{c}")
            do(f"sq{c}", act.activation(self.norm_buf(k, c)[:, :], k.bt_y[:, c, :], ACT.Square))
        for c in range(BC):
            after(k.fp, f"var{c}")
            do(f"ln{c}", act.activation(self.norm_buf(k, c)[:, :], self.var_bank(k, c)[:, :], ACT.Ln, bias=k.eps2_col[:, :],
                                        scale=1.0 / BH))
        for c in range(BC):
            after(k.fa, f"ln{c}")
            do(f"rs{c}", act.activation(self.norm_buf(k, c)[:, :], self.norm_buf(k, c)[:, :], ACT.Exp, scale=-0.5))
        for c in range(BC):
            after(k.fd, f"yg{c}")
            do(f"hi{c}", act.activation(k.a_hi_buf[:, BC + c, :], k.bt_y[:, c, :], ACT.Copy))

    def dve(self, k, q):
        dve = k.nc.vector
        chunks = lambda b: b.rearrange("p (n c) -> p n c", n=RN)
        ep = chunks(k.e_pos[:, :])
        vec = lambda name, c: k.vec(name)[:, c:c + 1]
        for c in range(BC):
            do, after = stage(dve, k.pd, c)
            r, kk, v = k.rkv[:, c, :], k.rkv[:, BC + c, :], k.rkv[:, 2 * BC + c, :]
            if c == 0:
                dve.wait_ge(k.shifted, 15)
            after(k.pd, "beta", c - 1)
            do("kkr", dve.tensor_scalar(k.kkr[:, :], kk, vec("k_k", c), None, ALU.mult))
            after(k.pa, "sigw")
            after(k.pa, "eneg", c - 1)
            cum, sigw = chunks(k.cumw[:, :]), chunks(k.tmp2[:, :])
            for n in range(RN):
                do(f"scan{n}", dve.tensor_tensor_scan(cum[:, n, :], k.ones[:, :], sigw[:, n, :], 0.0, ALU.mult, ALU.add))
            after(k.pd, f"scan{RN - 1}")
            do("mcol", dve.tensor_copy(k.mcol[:, c, :], cum[:, :, RC // 2 - 1]))
            after(k.pd, "mcol")
            do("sub", dve.tensor_tensor(cum, cum, k.mcol[:, c, :].rearrange("p (n o) -> p n o", o=1).to_broadcast([P, RN, RC]), ALU.subtract))
            after(k.pd, "sub")
            do("rho", dve.tensor_tensor(k.rhos[:, 0:RN - 1, c], cum[:, 0:RN - 1, RC - 1], k.mcol[:, c, 1:RN], ALU.add))
            after(k.pp, "ss")
            do("ssm", dve.tensor_scalar(k.tmp2[:, :], k.bank[2][:, :], 1e-24, None, ALU.max))
            after(k.pa, "siga")
            do("am", dve.tensor_scalar(k.tmp1[:, :], k.ab[:, :], 1.0, vec("k_a", c), ALU.subtract, ALU.mult))
            after(k.pd, "am")
            do("kp", dve.scalar_tensor_tensor(kk, k.tmp1[:, :], 1.0, kk, ALU.add, ALU.mult))
            after(k.pa, "rn")
            do("kkn", dve.scalar_tensor_tensor(k.kkr[:, :], k.kkr[:, :], LN_SCALE ** 0.5, k.tmp2[:, :], ALU.mult, ALU.mult))
            after(k.pa, "eneg")
            do("rt", dve.tensor_tensor(chunks(k.ar[:, c, 1, :]), chunks(r), ep[:, :, 1:], ALU.mult))
            after(k.pd, "kkn")
            do("at", dve.scalar_tensor_tensor(chunks(k.ar[:, c, 0, :]), chunks(k.kkr[:, :]), -1.0, ep[:, :, 0:RC], ALU.mult, ALU.mult))
            do("beta", dve.tensor_tensor(k.ab[:, :], k.ab[:, :], k.kkr[:, :], ALU.mult))
            after(k.pd, "beta")
            do("bt", dve.tensor_tensor(k.bt_y[:, c, :], k.ab[:, :], k.e_neg[:, :], ALU.mult))
            after(k.pd, "kp")
            do("rk", dve.scalar_tensor_tensor(k.tmp1[:, :], r, vec("r_k", c), kk, ALU.mult, ALU.mult))
            after(k.pd, "rk")
            do("kt", dve.tensor_tensor(kk, kk, k.e_neg[:, :], ALU.mult))
            after(k.pp, "bs")
            do("bon", dve.tensor_tensor(r, k.bank[3][:, :], v, ALU.mult))
        dve.wait_ge(k.rw_masks, self.n_masks)
        dve.wait_ge(k.rw_zero, 4)
        as4 = lambda bank: bank[:, :].rearrange("p (h f) -> p h f", f=P)
        over = lambda m: m.rearrange("p (o f) -> p o f", o=1).to_broadcast([P, BC, P])
        halves = lambda b, p: b[:, p * BC:(p + 1) * BC, :]
        banks = k.bank + k.gbank + [k.cbank, k.nbank]
        for t in range(RN):
            do, after = stage(dve, k.cd, t)
            for p in range(2):
                after(k.cp, f"a{p}")
                after(k.ca, f"i{p}")
                do(f"a{p}", dve.copy_predicated(halves(k.inv, p), over(k.lvl_mask[:, 0, 0, :]), as4(banks[p])))
            for p in range(2):
                after(k.cp, f"at{p}")
                after(k.ca, f"it{p}")
                do(f"at{p}", dve.copy_predicated(halves(k.mat_at, p), over(k.tri[:, 1, :]), as4(banks[2 + p])))
                do(f"it{p}", dve.copy_predicated(halves(k.inv_t, p), over(k.lvl_mask[:, 0, 1, :]), as4(banks[2 + p])))
            for name, buf, b, m in (("ak", k.t_ak, 4, 1), ("rk", k.t_rk, 6, 2), ("rb", k.t_rb, 0, 2)):
                for p in range(2):
                    after(k.cp, f"{name}{p}")
                    do(f"{name}{p}", dve.copy_predicated(halves(buf, p), over(k.tri[:, m, :]), as4(banks[b + p])))
            for l in range(1, len(LEVELS) + 1):
                for p in range(2):
                    if l < len(LEVELS):
                        after(k.cp, f"y{l}{p}")
                        do(f"y{l}{p}", dve.copy_predicated(halves(k.inv, p), over(k.lvl_mask[:, l, 0, :]), as4(k.bank[2 + p])))
                    after(k.cp, f"z{l}{p}")
                    do(f"z{l}{p}", dve.copy_predicated(halves(k.inv_t, p), over(k.lvl_mask[:, l, 1, :]), as4(k.gbank[p])))
            after(k.cp, "u")
            do("u", dve.tensor_copy(k.u_sb[:, :], k.gbank[0][:, :]))
            after(k.cp, "p")
            P4 = k.gbank[1][:, 0:BC * BH].rearrange("p (c f) -> p c f", f=BH)
            if t == 0:
                do("sp", dve.tensor_copy(k.st2[:, :, :], P4))
            else:
                do("sp", dve.tensor_tensor(k.st2[:, :, :], P4, k.st[:, :, :], ALU.add))
            after(k.cd, "sp")
            n = min(t, RN - 2)
            do("s", dve.tensor_tensor(k.st[:, :, :], k.st2[:, :, :],
                                      k.rhos[:, n, :].rearrange("p (c o) -> p c o", o=1).to_broadcast([P, BC, BH]), ALU.mult))
        do, after = stage(dve, k.fd, 0)
        for c in range(BC):
            after(k.fp, f"mean{c}")
            do(f"yc{c}", dve.scalar_tensor_tensor(k.bt_y[:, c, :], k.bank[c][:, :], -1.0 / BH, k.bt_y[:, c, :], ALU.mult, ALU.add))
        def low(c):
            after(k.fa, f"hi{c}")
            do(f"lo{c}", dve.tensor_tensor(k.a_lo_buf[:, BC + c, :], k.bt_y[:, c, :], k.a_hi_buf[:, BC + c, :].bitcast(F32),
                                           ALU.subtract))
        for c in range(BC):
            y = k.bt_y[:, c, :]
            after(k.fa, f"rs{c}")
            do(f"yw{c}", dve.scalar_tensor_tensor(y, y, vec("ln_w", c), self.norm_buf(k, c)[:, :], ALU.mult, ALU.mult))
            after(k.fd, f"yw{c}")
            do(f"yb{c}", dve.scalar_tensor_tensor(y, y, vec("ln_b", c), k.rkv[:, c, :], ALU.add, ALU.add))
            after(k.fp, f"g{c}")
            after(k.fd, f"yb{c}")
            do(f"yg{c}", dve.tensor_tensor(y, y, k.bank[c][:, :], ALU.mult))
            if c:
                low(c - 1)
        low(BC - 1)


class MixerOutput(Phase):
    blocks = DC

    def advance(self, q):
        q.g += self.blocks
        q.sq += DC

    def ready(self, eng, k, q):
        eng.wait_ge(k.at_parts, A_HEADS)
        eng.wait_ge(k.fd.sem, len(k.fd.names))

    def pe(self, k, q):
        pe = k.nc.tensor
        pe.wait_ge(k.at_parts, A_HEADS)
        pe.wait_ge(k.fd.sem, k.fd.done(0, f"yg{q.g % RING}"))
        def ready(t):
            if t >= DC - BC:
                pe.wait_ge(k.fd.sem, k.fd.done(0, f"lo{t - (DC - BC)}"))
        y = lambda t: (k.a_hi_buf[:, t, :], k.a_lo_buf[:, t, :])
        with pe.Fori(0, DC // RING) as it:
            for b in range(RING):
                pe_block(k, At(q.g + b, RING, it), DC, y, ready=ready if b == 0 else None)

    def act(self, k, q):
        self.ready(k.nc.scalar, k, q)
        act_down(k, q.g, q.sq)

    def dve(self, k, q):
        self.ready(k.nc.vector, k, q)
        dve_down(k, q.g, add=False, sq0=q.sq)


C_HEADS = 4
C_QK = D // C_HEADS
C_V = 2 * C_QK
QT, VT = C_QK // P, C_V // P
ODD_BLOCKS = 2 * QT + 2 * VT
KEY_BLOCKS = T // P


class Odd(Phase):
    FIRST_OUT = 3 * ODD_BLOCKS
    LAST_HEAD = FIRST_OUT + DC
    SECOND_OUT = LAST_HEAD + ODD_BLOCKS
    blocks = SECOND_OUT + DC

    def advance(self, q):
        q.g += self.blocks
        q.norm += C_HEADS
        q.sq += DC

    def layout(self, k, ctx):
        at = k.arena["sq"][0]
        def put(name, shape):
            nonlocal at
            t = k.sb(name, shape, F32, at=at)
            at += int(np.prod(shape[1:])) * 4
            assert at <= k.limit, (name, at, k.limit)
            return t
        k.r_scores = put("r_scores", [P, sum(T - P * s for s in range(KEY_BLOCKS))])
        k.r_dist = put("r_dist", [P, T])
        k.r_decay = put("r_decay", [P, T])
        k.r_sq = put("r_sq", [P, 2, T])
        k.r_v = put("r_v", [P, VT, T])
        k.r_qk = put("r_qk", [P, 2 * QT, T])
        k.r_gate = put("r_gate", [P, VT, T])
        k.r_vtok = put("r_vtok", [P, KEY_BLOCKS, C_V])
        k.r_y = put("r_y", [P, VT, T])
        (k.r_dist_ready, k.r_decay_ready, k.r_vt_full, k.r_vt_copied, k.r_sc_full, k.r_weighed, k.r_y_full
         ) = k.sems("r_dist_ready r_decay_ready r_vt_full r_vt_copied r_sc_full r_weighed r_y_full")
        (k.r_squared, k.r_added, k.r_gated, k.r_scaled, k.r_high, k.r_parts, k.r_silu
         ) = k.sems("r_squared r_added r_gated r_scaled r_high r_parts r_silu")

    def g0(self, q, h):
        return q.g + (h * ODD_BLOCKS if h < 3 else self.LAST_HEAD)

    STEPS = [(0, None), (1, 0), (2, 1), "out", (3, 2), (None, 3), "out"]

    @staticmethod
    def score_cols(s):
        at = sum(T - P * i for i in range(s))
        return slice(at, at + T - P * s)

    def pool(self, k, q):
        pool = k.nc.gpsimd
        pool.wait_ge(k.a_ready, q.a)
        pool.iota(k.r_dist[:, :], pattern=[[1, T]], base=0, channel_multiplier=-1,
                  allow_small_or_imprecise_dtypes=True).then_inc(k.r_dist_ready, 1)

    def pe(self, k, q):
        pe = k.nc.tensor
        n_out = 0
        for step in self.STEPS:
            if step == "out":
                pe.wait_ge(k.r_parts, 2 * VT * (n_out + 1))
                y = lambda t: (k.a_hi_buf[:, t, :], k.a_lo_buf[:, t, :])
                with pe.Fori(0, DC // RING) as it:
                    for b in range(RING):
                        pe_block(k, At(q.g + (self.FIRST_OUT, self.SECOND_OUT)[n_out] + b, RING, it), DC, y)
                n_out += 1
            else:
                self.pe_step(k, q, *step)

    def pe_step(self, k, q, h, e):
        pe = k.nc.tensor
        hh = lambda t: (k.h_hi_buf[:, t, :], k.h_lo_buf[:, t, :])
        def blocks(lo, hi):
            if h is not None:
                for b in range(lo, hi):
                    pe_block(k, At(self.g0(q, h) + b), DC, hh)
        if e is not None:
            pe.wait_ge(k.bank_free, self.g0(q, e) + 2 * QT + VT)
            for n in range(KEY_BLOCKS):
                if n >= 2:
                    pe.wait_ge(k.r_vt_copied, KEY_BLOCKS * e + n - 1)
                elif e > 0:
                    pe.wait_ge(k.r_gated, VT * e)
                else:
                    pe.wait_ge(k.rstd_ready, q.norm)
                for c in range(VT):
                    last = pe.transpose(k.gbank[n % 2][:, c * P:(c + 1) * P], k.r_v[:, c, n * P:(n + 1) * P], k.ident[:, :])
                last.then_inc(k.r_vt_full, 1)
            for s in range(KEY_BLOCKS):
                out = self.banks(k)[s][:, 0:T - P * s]
                if s == 1:
                    pe.wait_ge(k.rstd_ready, q.norm + e)
                if s >= 2:
                    pe.wait_ge(k.r_vt_copied, KEY_BLOCKS * e + s + 1)
                for c in range(QT):
                    last = pe.matmul(out, k.r_qk[:, QT + c, s * P:(s + 1) * P], k.r_qk[:, c, s * P:T],
                                     start=(c == 0), stop=(c == QT - 1))
                last.then_inc(k.r_sc_full, 1)
        if h != 0:
            blocks(0, VT)
        if e is not None:
            pe.wait_ge(k.r_weighed, KEY_BLOCKS * (e + 1))
            pe.wait_ge(k.r_vt_copied, KEY_BLOCKS * (e + 1))
            for j in range(VT):
                bank = self.banks(k)[j]
                for s in range(KEY_BLOCKS):
                    last = pe.matmul(bank[:, s * P:T], k.r_vtok[:, s, j * P:(j + 1) * P], k.r_scores[:, self.score_cols(s)],
                                     start=(s == 0), stop=(s == KEY_BLOCKS - 1))
                last.then_inc(k.r_y_full, 1)
        blocks(VT, VT + 2 * QT - 1)
        if e is not None:
            pe.wait_ge(k.r_added, VT * (e + 1))
            pe.wait_ge(k.r_gated, VT * (e + 1))
            pe.matmul(k.nbank[:, :], k.ones[:, :], k.ssq[:, :], start=True, stop=True).then_inc(k.norm_sum, 1)
        blocks(VT + 2 * QT - 1, ODD_BLOCKS)

    @staticmethod
    def banks(k):
        return [k.cbank, k.nbank, k.gbank[0], k.gbank[1]]

    def act(self, k, q):
        act = k.nc.scalar
        n_out = 0
        for step in self.STEPS:
            if step == "out":
                last = n_out == 1
                act_down(k, q.g + (self.FIRST_OUT, self.SECOND_OUT)[n_out], q.sq if last else None)
                n_out += 1
            else:
                self.act_step(k, q, *step)

    def act_step(self, k, q, h, e):
        act = k.nc.scalar
        def splits(lo, hi):
            if h is not None:
                for b in range(lo, hi):
                    act_split(k, At(self.g0(q, h) + b + LEAD))
        if e is not None:
            if e == 0:
                act.wait_ge(k.r_dist_ready, 3)
            else:
                act.wait_ge(k.r_weighed, KEY_BLOCKS * e)
            act.activation(k.r_decay[:, :], k.r_dist[:, :], ACT.Exp, scale=-math.log(1.0 - 2.0 ** (-5.0 - e))
                           ).then_inc(k.r_decay_ready, 1)
            for n in range(KEY_BLOCKS):
                act.wait_ge(k.r_vt_full, KEY_BLOCKS * e + n + 1)
                if n == 0 and e > 0:
                    act.wait_ge(k.r_y_full, VT * e)
                act.activation(k.r_vtok[:, n, :], k.gbank[n % 2][:, :], ACT.Copy).then_inc(k.r_vt_copied, 1)
        if h != 0:
            splits(0, VT)
        if e is not None:
            for j in range(VT):
                act.wait_ge(k.r_y_full, VT * e + j + 1)
                if VT * e + j >= 2:
                    act.wait_ge(k.r_added, VT * e + j - 1)
                act.activation(k.r_sq[:, j % 2, :], self.banks(k)[j][:, :], ACT.Square).then_inc(k.r_squared, 1)
        splits(VT, VT + 2 * QT)
        if e is not None:
            act_rstd(k, q.norm + e, lambda act: wait(act, k.r_scaled, VT * e), scale=1.0 / C_V, out=k.lnv)
            if e == 2:
                act.wait_ge(k.block_done, q.g + self.LAST_HEAD)
            for j in range(VT):
                act.wait_ge(k.r_scaled, VT * e + j + 1)
                act.activation(k.a_hi_buf[:, VT * (e % 2) + j, :], k.r_y[:, j, :], ACT.Copy).then_inc(k.r_high, 1)
        if h is not None:
            for j in range(VT):
                g = self.g0(q, h) + VT + 2 * QT + j
                act_split(k, At(g + LEAD))
                act.wait_ge(k.bank_free, g + 1)
                act.activation(k.r_gate[:, j, :], k.r_gate[:, j, :], ACT.Silu).then_inc(k.r_silu, 1)

    def dve(self, k, q):
        dve = k.nc.vector
        dve.wait_ge(k.r_dist_ready, 1)
        dve.scalar_tensor_tensor(k.r_dist[:, :], k.r_dist[:, :], -1.0, k.r_dist[:, :], ALU.mult, ALU.min).then_inc(k.r_dist_ready, 1)
        dve.wait_ge(k.r_dist_ready, 2)
        dve.memset(k.r_dist[CH:P, 0:CH], -1e30).then_inc(k.r_dist_ready, 1)
        n_out = 0
        for step in self.STEPS:
            if step == "out":
                last = n_out == 1
                dve_down(k, q.g + (self.FIRST_OUT, self.SECOND_OUT)[n_out], add=last, sq0=q.sq if last else None)
                n_out += 1
            else:
                self.dve_step(k, q, *step)

    def dve_step(self, k, q, h, e):
        dve = k.nc.vector
        def staged(b):
            if h is None:
                return
            g = self.g0(q, h) + b
            dve.wait_ge(k.block_done, g + 1)
            dst = k.r_v[:, b, :] if b < VT else k.r_qk[:, b - VT, :] if b < VT + 2 * QT else k.r_gate[:, b - VT - 2 * QT, :]
            dve.tensor_tensor(dst, k.bank[g % RING][:, :], k.rstd[:, :], ALU.mult).then_inc(k.bank_free, 1)
        def split(b):
            if h is not None:
                dve_split(k, At(self.g0(q, h) + b + LEAD))
        if e is not None:
            dve.wait_ge(k.r_decay_ready, e + 1)
            for s in range(KEY_BLOCKS):
                dve.wait_ge(k.r_sc_full, KEY_BLOCKS * e + s + 1)
                if s == 0 and e > 0:
                    dve.wait_ge(k.r_y_full, VT * e)
                n = T - P * s
                dve.scalar_tensor_tensor(k.r_scores[:, self.score_cols(s)], self.banks(k)[s][:, 0:n], C_QK ** -0.5,
                                         k.r_decay[:, 0:n], ALU.mult, ALU.mult).then_inc(k.r_weighed, 1)
            if h is not None:
                dve.wait_ge(k.r_vt_full, KEY_BLOCKS * (e + 1))
        if h != 0:
            for b in range(VT):
                split(b)
                staged(b)
        if e is not None:
            for j in range(VT):
                n = VT * e + j
                dve.wait_ge(k.r_squared, n + 1)
                if j == 0:
                    dve.wait_ge(k.rstd_ready, q.norm + e)
                    dve.tensor_copy(k.ssq[:, :], k.r_sq[:, 0, :]).then_inc(k.r_added, 1)
                else:
                    dve.wait_ge(k.r_added, n)
                    dve.tensor_tensor(k.ssq[:, :], k.ssq[:, :], k.r_sq[:, j % 2, :], ALU.add).then_inc(k.r_added, 1)
                if j == 0 and e > 0:
                    dve.wait_ge(k.r_parts, VT * e)
                dve.wait_ge(k.r_silu, n + 1)
                dve.tensor_tensor(k.r_y[:, j, :], self.banks(k)[j][:, :], k.r_gate[:, j, :], ALU.mult).then_inc(k.r_gated, 1)
        for b in range(VT, VT + 2 * QT):
            split(b)
            if b < VT + 2 * QT - 1:
                staged(b)
        if e is not None:
            dve.wait_ge(k.rstd_ready, q.norm + 1 + e)
            for j in range(VT + 1):
                if j < VT:
                    dve.wait_ge(k.r_gated, VT * e + j + 1)
                    dve.tensor_tensor(k.r_y[:, j, :], k.r_y[:, j, :], k.lnv[:, :], ALU.mult).then_inc(k.r_scaled, 1)
                if j >= 1:
                    i = j - 1
                    slot = VT * (e % 2) + i
                    dve.wait_ge(k.r_high, VT * e + i + 1)
                    dve.tensor_tensor(k.a_lo_buf[:, slot, :], k.r_y[:, i, :], k.a_hi_buf[:, slot, :].bitcast(F32), ALU.subtract
                                      ).then_inc(k.r_parts, 1)
        staged(VT + 2 * QT - 1)
        if e is not None and h is not None:
            dve.wait_ge(k.r_gated, VT * (e + 1))
        for b in range(VT + 2 * QT, ODD_BLOCKS):
            split(b)
            staged(b)


class Kernel:
    ROUTE_STEPS = 36


def build(nc, W, vecs, small, xT, out, phases):
    k = Kernel()
    k.nc, k.W = nc, W
    k.n_blocks = W.shape[0]
    with ExitStack() as ctx:
        base = -(-nc.sbuf_base // 64) * 64
        arena = {}

        def sb(name, shape, dt=F32, at=None):
            size = int(np.prod(shape[1:])) * (1 if dt == I8 else 4)
            t = nc.alloc_sbuf_tensor_at(name, shape, dt, offset=base + at)
            arena[name] = (at, at + size)
            return t
        k.sb = sb
        KB = 1024
        at = 0
        def bump(name, shape, dt=F32):
            nonlocal at
            size = int(np.prod(shape[1:])) * (1 if dt == I8 else 4)
            t = sb(name, shape, dt, at=at)
            at += -(-size // 64) * 64
            return t
        k.raw = bump("raw", [P, RING, D])
        k.whi = bump("whi", [P, RING, D], F32R)
        k.wlo = bump("wlo", [P, RING, D], F32R)
        k.h_hi_buf = bump("h_hi_buf", [P, DC, T], F32R)
        k.h_lo_buf = bump("h_lo_buf", [P, DC, T], F32R)
        k.a_hi_buf = bump("a_hi_buf", [P, DC, T], F32R)
        k.a_lo_buf = bump("a_lo_buf", [P, DC, T], F32R)
        k.ssq = bump("ssq", [P, T])
        k.lnv = bump("lnv", [P, T])
        k.rstd = bump("rstd", [P, T])
        k.ones = bump("ones", [P, P])
        k.ident = bump("ident", [P, P])
        k.eps_col = bump("eps_col", [P, 1])
        k.vecs = bump("vecs_sb", [P, VEC_COLS])
        k.pair_ones = bump("pair_ones", [P, P])
        k.eps2_col = bump("eps2_col", [P, 1])
        k.c_in = bump("c_in", [P, DC, 2])
        k.c32 = bump("c32", [P, DC, 2])
        k.c_hi = bump("c_hi", [P, DC, 2], F32R)
        k.c_lo = bump("c_lo", [P, DC, 2], F32R)
        k.mod = bump("mod", [P, 6 * DC, 2])
        k.gain1 = bump("gain1", [P, 2, DC])
        k.shift1 = bump("shift1", [P, 2, DC])
        k.gain2 = bump("gain2", [P, DC])
        k.shift2 = bump("shift2", [P, DC])
        k.low = at
        k.x = bump("x", [P, DC, T])
        k.acc = bump("acc", [P, DC, T])
        k.sq = bump("sq", [P, 2, T])
        k.sil = bump("sil", [P, 2, T])
        k.a32 = bump("a32", [P, 2, T])
        k.h32 = sb("h32", [P, 2, T], at=arena["a32"][0])
        k.top = at
        k.sq0, k.h320 = k.sq, k.h32
        k.limit = nc.sbuf_usable_end - base
        k.arena = arena

        def ps(name, shape):
            return ctx.enter_context(nc.psum_tensor(name, shape, F32))
        k.bank = [ps(f"bank{i}", [P, T]) for i in range(RING)]
        k.nbank = ps("nbank", [P, T])

        def sem(name):
            return ctx.enter_context(nc.semaphore(name))
        k.sem = sem
        k.sems = lambda names: [sem(n) for n in names.split()]
        k.raw_landed = [sem(f"raw_landed{i}") for i in range(RING)]
        (k.split_hi, k.split_lo, k.block_done, k.bank_free, k.sq_ready, k.ssq_added, k.norm_sum
         ) = k.sems("split_hi split_lo block_done bank_free sq_ready ssq_added norm_sum")
        (k.ln_ready, k.rstd_ready, k.h_hi, k.h_made, k.h_ready, k.x_ready, k.y_scaled
         ) = k.sems("ln_ready rstd_ready h_hi h_made h_ready x_ready y_scaled")
        (k.a_ready, k.a_hi, k.silu_ready, k.ssq_clear, k.x_loaded, k.small_loaded, k.c_ready
         ) = k.sems("a_ready a_hi silu_ready ssq_clear x_loaded small_loaded c_ready")
        k.const_ready, k.gains_halved, k.stored, k.gate_scaled, k.a_made, k.first_scaled = k.sems(
            "const_ready gains_halved stored gate_scaled a_made first_scaled")
        k.vec = lambda name: k.vecs[:, VEC_AT[name]:VEC_AT[name] + VEC_WIDTH[name]]
        k.n_clear = 0
        k.dram = small
        k.xT = xT
        k.gbank = [ps(f"gbank{i}", [P, T]) for i in range(2)]
        k.cbank = ps("cbank", [P, T])
        for ph in phases:
            ph.layout(k, ctx)
        block = ctx.enter_context(nc.Block())

        @block.sync
        def _(sp):
            sp_stream(k, k.n_blocks)
            q = Counts()
            for ph in phases:
                ph.advance(q)
            for c in range(DC):
                sp.wait_ge(k.x_ready, q.xc - DC + c + 1)
                sp.dma_start(out[:, c, :], k.x[:, c, :]).then_inc(k.stored, 16)
            sp.wait_ge(k.stored, 16 * DC)

        @block.scalar
        def _(act):
            act.dma_start(k.c_in[:, :, :], small["c"]).then_inc(k.small_loaded, 16)
            act.dma_start(k.vecs[:, :], vecs).then_inc(k.small_loaded, 16)
            act.dma_start(k.xc1[:, :, :], small["xc"]).then_inc(k.x_loaded, 16)
            act.dma_start(k.x1[:, :, :], xT).then_inc(k.x_loaded, 16)
            act.wait_ge(k.const_ready, 8)
            q = Counts()
            for ph in phases:
                ph.act(k, q)
                ph.advance(q)

        @block.gpsimd
        def _(pool):
            pool.memset(k.ones[:, :], 1.0).then_inc(k.const_ready, 1)
            pool.memset(k.eps_col[:, :], EPS).then_inc(k.const_ready, 1)
            pool.memset(k.ident[:, :], 0.0).then_inc(k.const_ready, 1)
            pool.wait_ge(k.const_ready, 3)
            pool.affine_select(out=k.ident[:, :], in_=k.ident[:, :], compare_op=ALU.not_equal, fill=1.0,
                               base=0, pattern=[[-1, P]], channel_multiplier=1).then_inc(k.const_ready, 1)
            pool.memset(k.pair_ones[:, :], 0.0).then_inc(k.const_ready, 1)
            pool.wait_ge(k.const_ready, 5)
            for half in (slice(0, P // 2), slice(P // 2, P)):
                pool.memset(k.pair_ones[half, half], 1.0).then_inc(k.const_ready, 1)
            pool.wait_ge(k.const_ready, 7)
            pool.memset(k.eps2_col[:, :], 64e-5).then_inc(k.const_ready, 1)
            q = Counts()
            for ph in phases:
                ph.pool(k, q)
                ph.advance(q)

        @block.vector
        def _(dve):
            dve.wait_ge(k.const_ready, 8)
            dve.wait_ge(k.small_loaded, 32)
            for n, name in enumerate(HALVED):
                dve.tensor_scalar(k.vec(name), k.vec(name), 0.5, None, ALU.mult).then_inc(k.gains_halved, 1)
                dve.wait_ge(k.gains_halved, n + 1)
            q = Counts()
            for ph in phases:
                ph.dve(k, q)
                ph.advance(q)

        @block.tensor
        def _(pe):
            pe.wait_ge(k.const_ready, 8)
            q = Counts()
            for ph in phases:
                ph.pe(k, q)
                ph.advance(q)

def stages():
    hidden = lambda k: [k.sil[:, 0, :], k.a32[:, 0, :], k.sil[:, 1, :], k.a32[:, 1, :]]
    queries = lambda k: [k.qkv[:, c, :] for c in range(RING)]
    values = lambda k: [k.r_v[:, c, :] for c in range(RING)]
    return [Mod(), HgrnInput(), Hgrn(), HgrnOutput(), MoeInput(), Moe(),
            Between("final_g", "norm_0_0", hidden, renorm=True), Ffn(),
            Between("norm_0_1", "norm_0_2", queries), EvenProj(), Attention(), Rwkv(), MixerOutput(),
            Between("norm_0_3", "norm_0_4", hidden), Ffn(),
            Between("norm_0_5", "norm_1_0", hidden), Ffn(),
            Between("norm_1_1", "norm_1_2", values), Odd(),
            Between("norm_1_3", "norm_1_4", hidden), Ffn(),
            Last("norm_1_5")]


def pack(w):
    K, N = w.shape
    b = np.zeros((N // P, P, DC, P), w.dtype)
    b[:, :, :K // P] = w.reshape(K // P, P, N // P, P).transpose(2, 1, 0, 3)
    return b.reshape(N // P, P, D)


def pack_wide(w):
    n = w.shape[1] // P
    wide = w.reshape(DC, P, n * P).transpose(1, 0, 2).reshape(P, n, D)
    return np.ascontiguousarray(wide.transpose(1, 0, 2))


def ffn_blocks(wgu, wd):
    gate, up = pack(wgu[:, :D_FF]), pack(wgu[:, D_FF:])
    out, f = [], 0
    for nk in FF_SEGMENTS:
        gu = np.stack([gate[f:f + nk], up[f:f + nk]], 1).reshape(2 * nk, P, D)
        out += [gu, pack(wd[f * P:(f + nk) * P])]
        f += nk
    return out


def cols(v):
    return v.reshape(-1, P).T


def moe_blocks(wg, wu, wd):
    out = []
    for n in range(N_EXPERTS // 4):
        for e in range(4 * n, 4 * n + 4):
            g, u = pack(wg[e]), pack(wu[e])
            out.append(np.stack([g, u], 1).reshape(4, P, D))
        out.append(pack(wd[4 * n:4 * n + 4].reshape(4 * D_EXPERT, D)))
    return out


def odd_blocks(w_in, w_out):
    p = pack(w_in)
    nq, nv = C_HEADS * QT, C_HEADS * VT
    head = lambda h: np.concatenate([p[2 * nq + h * VT:2 * nq + (h + 1) * VT], p[h * QT:(h + 1) * QT],
                                     p[nq + h * QT:nq + (h + 1) * QT], p[2 * nq + nv + h * VT:2 * nq + nv + (h + 1) * VT]])
    return [head(0), head(1), head(2), pack(w_out[:D]), head(3), pack(w_out[D:])]


def token_cols(x):
    return x.T.reshape(DC, P, -1).transpose(1, 0, 2)


def weight_blocks(i):
    w_mod, hg, hg_out = i["w_mod"][0], pack(i["hg_w_in"][0]), pack(i["hg_w_out"][0])
    mod = lambda at, blocks: pack_wide(w_mod[:, at * P:(at + blocks) * P])
    out = [mod(RING * n, RING) for n in range(2 * DC // RING)]
    for h in range(HEADS):
        q, v, zf, zb, g = (hg[n * HEADS + h:n * HEADS + h + 1] for n in range(5))
        out += [zf, mod(2 * DC + MOD_BLOCKS * h, MOD_BLOCKS), zb, q, v, g]
    out += [hg_out, mod(5 * DC, RING), mod(5 * DC + RING, RING)]
    out += moe_blocks(i["moe_w_gate"][0], i["moe_w_up"][0], i["moe_w_down"][0])
    wgu, wd = i["ffn_wgu_2"], i["ffn_wd_2"]
    out += ffn_blocks(wgu[0, 0], wd[0, 0])
    out += [pack(i["even_w_in_2"][0]), pack(i["even_w_out_2"][0])]
    out += ffn_blocks(wgu[0, 1], wd[0, 1]) + ffn_blocks(wgu[1, 0], wd[1, 0])
    out += odd_blocks(i["odd_w_in_2"][0], i["odd_w_out_2"][0])
    out += ffn_blocks(wgu[1, 1], wd[1, 1])
    return np.concatenate(out)


def kernel(**inputs):
    import concourse.bacc as _bacc
    from concourse.bass_utils import run_bass_kernel_spmd as _run

    i = {name: np.asarray(a) for name, a in inputs.items()}
    wide = lambda v: np.broadcast_to(v.reshape(1, -1), (P, v.size))
    two = lambda v: np.concatenate([cols(v[0]), cols(v[1])], 1)
    vec = {"b_mod": cols(i["b_mod"][0]), "norm1_g": cols(i["norm1_g"][0]), "norm2_g": cols(i["norm2_g"][0]),
           "gnorm": cols(i["hg_gnorm"][0]), "lb_f": two(i["hg_lb_fwd"]), "lb_b": two(i["hg_lb_bwd"]),
           "final_g": cols(i["final_g"]), "router_b": wide(i["router_b"]),
           "mu": cols(i["rwkv_mu_2"][0]), "subln": cols(i["diff_subln_2"][0])}
    for b in range(2):
        for n in range(6):
            vec[f"norm_{b}_{n}"] = cols(i["norms_2"][b, n])
    for n, name in enumerate(RWKV_VECS):
        vec[name] = cols(i["rwkv_vec_2"][0, n])
    arrays = {"w": weight_blocks(i), "vecs": np.concatenate([vec[name] for name in VEC_WIDTH], 1),
              "x": token_cols(i["x"][0]), "xc": token_cols(i["ctx"][0]),
              "c": np.stack([cols(i["c"][0]), cols(i["c_ctx"])], -1),
              "rw": i["router_w"].reshape(DC, P, N_EXPERTS).transpose(1, 0, 2),
              "waup": np.concatenate([i["rwkv_w_up_2"][0], i["rwkv_a_up_2"][0]]), "gup": i["rwkv_g_up_2"][0],
              "lam": wide(i["diff_lam_2"][0])}
    nc = _bacc.Bacc("TRN2", target_bir_lowering=False, num_devices=1)
    arrays = {f"in_{name}": np.ascontiguousarray(a) for name, a in arrays.items()}
    dram = {name[3:]: nc.dram_tensor(name, a.shape, mybir.dt.from_np(a.dtype), kind="ExternalInput").ap()
            for name, a in arrays.items()}
    out = nc.dram_tensor("out", (P, DC, T), F32, kind="ExternalOutput").ap()
    build(nc, dram["w"], dram["vecs"], dram, dram["x"], out, stages())
    y = _run(nc, [arrays], core_ids=[0]).results[0]["out"]
    return y.transpose(1, 0, 2).reshape(D, T).T.reshape(1, T, D)
```
